# Optimizing a Trainium2 kernel written in Bass

```python
import jax
import jax.numpy as jnp
from jax import lax
import numpy as np

D_MODEL = 1024
BATCH = 1
SEQ = 512
DEPTH = 1
DEC_BATCH = 8
DEC_SEQ = 16
PAST_LEN = 256

CHUNK = 64
EPS = 1e-6
ROPE_BASE = 10000.0
RET_HEADS = 8
RET_DK = 64
RET_DV = 64
MLA_HEADS = 8
MLA_NOPE = 64
MLA_ROPE = 32
MLA_V = 64
MLA_Q_RANK = 256
MLA_KV_RANK = 256
Q_BLOCK = 128
RET_QK_W = RET_HEADS * RET_DK
RET_V_W = RET_HEADS * RET_DV
MLA_OUT_W = MLA_HEADS * MLA_V
MIX_W = RET_V_W + MLA_OUT_W
IN_COLS = 2 * RET_QK_W + 2 * RET_V_W + MLA_Q_RANK + MLA_KV_RANK + MLA_ROPE
PEER_HEADS = 8
PEER_N_KEYS = 128
PEER_N_EXPERTS = PEER_N_KEYS * PEER_N_KEYS
PEER_DK = 256
PEER_TOPK = 16
PEER_BLOCK = 256

kernel_name = 'hybrid_retention_mla_peer_stream'

def rms_norm(x, w):
    xf = x.astype(jnp.float32)
    y = xf * lax.rsqrt(jnp.mean(xf * xf, axis=-1, keepdims=True) + EPS)
    return (y * w.astype(jnp.float32)).astype(x.dtype)

def rope(x, pos):
    half = x.shape[-1] // 2
    inv = ROPE_BASE ** (-jnp.arange(half, dtype=jnp.float32) / half)
    ang = pos.astype(jnp.float32)[:, None] * inv[None, :]
    shape = (pos.shape[0],) + (1,) * (x.ndim - 3) + (half,)
    cos = jnp.cos(ang).reshape(shape)
    sin = jnp.sin(ang).reshape(shape)
    x1 = x[..., :half].astype(jnp.float32)
    x2 = x[..., half:].astype(jnp.float32)
    return jnp.concatenate([x1 * cos - x2 * sin, x2 * cos + x1 * sin], axis=-1).astype(x.dtype)

def ret_log_decay():
    return jnp.log(1.0 - jnp.exp2(-5.0 - jnp.arange(RET_HEADS, dtype=jnp.float32)))

def retention_chunk(state, q, k, v):
    C = q.shape[2]
    lg = ret_log_decay()[:, None]
    idx = jnp.arange(C, dtype=jnp.float32)[None, :]
    intra = jnp.exp(lg[:, :, None] * jnp.abs(idx[:, :, None] - idx[:, None, :]))
    s = jnp.einsum('bhad,bhcd->bhac', q, k) * intra
    o = jnp.einsum('bhac,bhce->bhae', s, v)
    o = o + jnp.einsum('bhad,bhde->bhae', q * jnp.exp(lg * (idx + 1.0))[..., None], state)
    k_dec = k * jnp.exp(lg * (C - 1.0 - idx))[..., None]
    new_state = jnp.exp(lg * float(C))[..., None] * state + jnp.einsum('bhcd,bhce->bhde', k_dec, v)
    return o, new_state

def retention_prompt(q, k, v):
    B, H, S, _ = q.shape
    nc = S // CHUNK

    def to_chunks(t):
        return t.astype(jnp.float32).reshape(B, H, nc, CHUNK, t.shape[-1]).transpose(2, 0, 1, 3, 4)

    def step(state, qkv):
        o, new_state = retention_chunk(state, *qkv)
        return new_state, o

    state0 = jnp.zeros((B, H, RET_DK, RET_DV), jnp.float32)
    state, o = lax.scan(step, state0, (to_chunks(q), to_chunks(k), to_chunks(v)))
    o = o.transpose(1, 2, 0, 3, 4).reshape(B, H, S, RET_DV)
    return o, state

def mla_attend(q_lat, q_pe, c_kv, k_pe, mask):
    scale = (MLA_NOPE + MLA_ROPE) ** -0.5
    s = (jnp.einsum('bqhc,bkc->bhqk', q_lat, c_kv)
         + jnp.einsum('bqhr,bkr->bhqk', q_pe, k_pe)).astype(jnp.float32) * scale
    if mask is not None:
        s = jnp.where(mask, s, -jnp.inf)
    p = jax.nn.softmax(s, axis=-1).astype(c_kv.dtype)
    return jnp.einsum('bhqk,bkc->bqhc', p, c_kv)

def mla_prompt(q_lat, q_pe, c_kv, k_pe):
    B, S, H, R = q_lat.shape
    nb = S // Q_BLOCK
    k_chunk = jnp.arange(S) // CHUNK

    def one_block(args):
        ql, qp, qc = args
        mask = k_chunk[None, :] <= qc[:, None]
        return mla_attend(ql, qp, c_kv, k_pe, mask)

    ql_b = q_lat.reshape(B, nb, Q_BLOCK, H, R).transpose(1, 0, 2, 3, 4)
    qp_b = q_pe.reshape(B, nb, Q_BLOCK, H, MLA_ROPE).transpose(1, 0, 2, 3, 4)
    qc_b = k_chunk.reshape(nb, Q_BLOCK)
    o = lax.map(one_block, (ql_b, qp_b, qc_b))
    return o.transpose(1, 0, 2, 3, 4).reshape(B, S, H, R)

def mixer_project(xn, pos, w_in, q_norm_w, w_uq, kv_norm_w, w_uk):
    B, S, _ = xn.shape
    proj = xn @ w_in
    o1 = RET_QK_W
    o2 = o1 + RET_QK_W
    o3 = o2 + RET_V_W
    o4 = o3 + RET_V_W
    o5 = o4 + MLA_Q_RANK
    o6 = o5 + MLA_KV_RANK
    q_r, k_r, v_r, gate, c_q, c_kv, k_pe = jnp.split(proj, [o1, o2, o3, o4, o5, o6], axis=-1)
    q_r = rope(q_r.reshape(B, S, RET_HEADS, RET_DK), pos).transpose(0, 2, 1, 3)
    k_r = (rope(k_r.reshape(B, S, RET_HEADS, RET_DK), pos) * (RET_DK ** -0.5)).transpose(0, 2, 1, 3)
    v_r = v_r.reshape(B, S, RET_HEADS, RET_DV).transpose(0, 2, 1, 3)
    c_q = rms_norm(c_q, q_norm_w)
    q_m = jnp.einsum('bsc,chd->bshd', c_q, w_uq)
    q_nope = q_m[..., :MLA_NOPE]
    q_pe = rope(q_m[..., MLA_NOPE:], pos)
    q_lat = jnp.einsum('bshn,chn->bshc', q_nope, w_uk)
    c_kv = rms_norm(c_kv, kv_norm_w)
    k_pe = rope(k_pe, pos)
    return q_r, k_r, v_r, gate, q_lat, q_pe, c_kv, k_pe

def mixer_output(ret_o, gate, mla_lat, gn_w, w_uv, w_o):
    B, H, S, _ = ret_o.shape
    mu = jnp.mean(ret_o, axis=-1, keepdims=True)
    var = jnp.mean(jnp.square(ret_o - mu), axis=-1, keepdims=True)
    y = ((ret_o - mu) * lax.rsqrt(var + EPS)).transpose(0, 2, 1, 3).reshape(B, S, RET_V_W)
    y = (y * gn_w.astype(jnp.float32)).astype(gate.dtype) * jax.nn.silu(gate)
    mla_o = jnp.einsum('bshc,chn->bshn', mla_lat, w_uv).reshape(B, S, MLA_OUT_W)
    return jnp.concatenate([y, mla_o], axis=-1) @ w_o

def peer_ffn(xn, w_q, sub_keys, u_tab, v_tab):
    B, S, D = xn.shape
    xt = xn.reshape(B * S, D)
    n = B * S
    blk = min(PEER_BLOCK, n)
    n_pad = -(-n // blk) * blk
    xt = jnp.pad(xt, ((0, n_pad - n), (0, 0)))

    def one_block(xb):
        q = (xb @ w_q).reshape(blk, PEER_HEADS, 2, PEER_DK // 2)
        s = jnp.einsum('thpd,hpnd->thpn', q, sub_keys)
        top_s, top_i = lax.top_k(s, PEER_TOPK)
        cand = top_s[:, :, 0, :, None] + top_s[:, :, 1, None, :]
        cand_idx = top_i[:, :, 0, :, None] * PEER_N_KEYS + top_i[:, :, 1, None, :]
        cand = cand.reshape(blk, PEER_HEADS, PEER_TOPK * PEER_TOPK)
        cand_idx = cand_idx.reshape(blk, PEER_HEADS, PEER_TOPK * PEER_TOPK)
        best_s, best_j = lax.top_k(cand, PEER_TOPK)
        expert = jnp.take_along_axis(cand_idx, best_j, axis=-1)
        g = jax.nn.softmax(best_s.astype(jnp.float32), axis=-1).astype(xb.dtype)
        u = jnp.take(u_tab, expert, axis=0)
        a = jax.nn.gelu(jnp.einsum('td,thkd->thk', xb, u), approximate=False) * g
        v = jnp.take(v_tab, expert, axis=0)
        return jnp.einsum('thk,thkd->td', a, v)

    out = lax.map(one_block, xt.reshape(n_pad // blk, blk, D)).reshape(n_pad, D)[:n]
    return out.reshape(B, S, D)

def prompt_layer(x, lw):
    (ln1_w, w_in, ret_gn_w, q_norm_w, w_uq, kv_norm_w, w_uk, w_uv, w_o,
     ln2_w, peer_w_q, peer_sub_keys, peer_u, peer_v) = lw
    B, S, _ = x.shape
    pos = jnp.arange(S)
    q_r, k_r, v_r, gate, q_lat, q_pe, c_kv, k_pe = mixer_project(
        rms_norm(x, ln1_w), pos, w_in, q_norm_w, w_uq, kv_norm_w, w_uk)
    ret_o, ret_state = retention_prompt(q_r, k_r, v_r)
    mla_lat = mla_prompt(q_lat, q_pe, c_kv, k_pe)
    h = x + mixer_output(ret_o, gate, mla_lat, ret_gn_w, w_uv, w_o)
    h = h + peer_ffn(rms_norm(h, ln2_w), peer_w_q, peer_sub_keys, peer_u, peer_v)
    return h, c_kv, k_pe, ret_state

def sample_layer(x, ckv_past, kpe_past, ret_state, lw):
    (ln1_w, w_in, ret_gn_w, q_norm_w, w_uq, kv_norm_w, w_uk, w_uv, w_o,
     ln2_w, peer_w_q, peer_sub_keys, peer_u, peer_v) = lw
    B, T, _ = x.shape
    pos = ckv_past.shape[1] + jnp.arange(T)
    q_r, k_r, v_r, gate, q_lat, q_pe, c_kv, k_pe = mixer_project(
        rms_norm(x, ln1_w), pos, w_in, q_norm_w, w_uq, kv_norm_w, w_uk)
    ret_o, new_state = retention_chunk(ret_state.astype(jnp.float32), q_r.astype(jnp.float32),
                                       k_r.astype(jnp.float32), v_r.astype(jnp.float32))
    ckv_all = jnp.concatenate([ckv_past.astype(c_kv.dtype), c_kv], axis=1)
    kpe_all = jnp.concatenate([kpe_past.astype(k_pe.dtype), k_pe], axis=1)
    mla_lat = mla_attend(q_lat, q_pe, ckv_all, kpe_all, None)
    h = x + mixer_output(ret_o, gate, mla_lat, ret_gn_w, w_uv, w_o)
    h = h + peer_ffn(rms_norm(h, ln2_w), peer_w_q, peer_sub_keys, peer_u, peer_v)
    return h, c_kv, k_pe, new_state

def setup_inputs(seed: int = 0) -> dict:
    key = jax.random.key(seed)
    ks = jax.random.split(key, 20)
    f32 = jnp.float32

    def nrm(k, shape, scale):
        return jax.random.normal(k, shape, f32) * scale

    def gain(k, shape):
        return 1.0 + 0.02 * jax.random.normal(k, shape, f32)

    return {
        'x_prompt': nrm(ks[0], (BATCH, SEQ, D_MODEL), 1.0),
        'x_sample': nrm(ks[1], (DEC_BATCH, DEC_SEQ, D_MODEL), 1.0),
        'cache_mla_ckv': nrm(ks[2], (DEPTH, DEC_BATCH, PAST_LEN, MLA_KV_RANK), 1.0),
        'cache_mla_krope': nrm(ks[3], (DEPTH, DEC_BATCH, PAST_LEN, MLA_ROPE), 1.0),
        'state_retention': nrm(ks[4], (DEPTH, DEC_BATCH, RET_HEADS, RET_DK, RET_DV), 0.5),
        'ln1_w': gain(ks[5], (DEPTH, D_MODEL)),
        'w_in': nrm(ks[6], (DEPTH, D_MODEL, IN_COLS), D_MODEL ** -0.5),
        'ret_gn_w': gain(ks[7], (DEPTH, RET_V_W)),
        'mla_q_norm_w': gain(ks[8], (DEPTH, MLA_Q_RANK)),
        'mla_w_uq': nrm(ks[9], (DEPTH, MLA_Q_RANK, MLA_HEADS, MLA_NOPE + MLA_ROPE), MLA_Q_RANK ** -0.5),
        'mla_kv_norm_w': gain(ks[10], (DEPTH, MLA_KV_RANK)),
        'mla_w_uk': nrm(ks[11], (DEPTH, MLA_KV_RANK, MLA_HEADS, MLA_NOPE), MLA_KV_RANK ** -0.5),
        'mla_w_uv': nrm(ks[12], (DEPTH, MLA_KV_RANK, MLA_HEADS, MLA_V), MLA_KV_RANK ** -0.5),
        'w_o': nrm(ks[13], (DEPTH, MIX_W, D_MODEL), MIX_W ** -0.5),
        'ln2_w': gain(ks[14], (DEPTH, D_MODEL)),
        'peer_w_q': nrm(ks[15], (DEPTH, D_MODEL, PEER_HEADS * PEER_DK), D_MODEL ** -0.5),
        'peer_sub_keys': nrm(ks[16], (DEPTH, PEER_HEADS, 2, PEER_N_KEYS, PEER_DK // 2), (PEER_DK // 2) ** -0.5),
        'peer_u': nrm(ks[17], (DEPTH, PEER_N_EXPERTS, D_MODEL), D_MODEL ** -0.5),
        'peer_v': nrm(ks[18], (DEPTH, PEER_N_EXPERTS, D_MODEL), PEER_HEADS ** -0.5),
        'lnf_w': gain(ks[19], (D_MODEL,)),
    }

def reference(x_prompt, x_sample, cache_mla_ckv, cache_mla_krope, state_retention,
              ln1_w, w_in, ret_gn_w, mla_q_norm_w, mla_w_uq, mla_kv_norm_w, mla_w_uk,
              mla_w_uv, w_o, ln2_w, peer_w_q, peer_sub_keys, peer_u, peer_v, lnf_w):
    hp = x_prompt
    hs = x_sample
    ckv_p, kpe_p, st_p, ckv_s, kpe_s, st_s = [], [], [], [], [], []
    for l in range(DEPTH):
        lw = (ln1_w[l], w_in[l], ret_gn_w[l], mla_q_norm_w[l], mla_w_uq[l], mla_kv_norm_w[l],
              mla_w_uk[l], mla_w_uv[l], w_o[l], ln2_w[l], peer_w_q[l], peer_sub_keys[l],
              peer_u[l], peer_v[l])
        hp, c1, k1, s1 = prompt_layer(hp, lw)
        hs, c2, k2, s2 = sample_layer(hs, cache_mla_ckv[l], cache_mla_krope[l], state_retention[l], lw)
        ckv_p.append(c1)
        kpe_p.append(k1)
        st_p.append(s1)
        ckv_s.append(c2)
        kpe_s.append(k2)
        st_s.append(s2)
    y_prompt = rms_norm(hp, lnf_w)
    y_sample = rms_norm(hs, lnf_w)
    return (y_prompt, y_sample, jnp.stack(ckv_p), jnp.stack(kpe_p), jnp.stack(st_p),
            jnp.stack(ckv_s), jnp.stack(kpe_s), jnp.stack(st_s))


_drawn_inputs = setup_inputs


def setup_inputs(seed=0):
    import zlib

    import numpy as np

    out = dict(_drawn_inputs(seed))
    spreads = {}
    factors = {'ret_gn_w': 13.089,
     'mla_q_norm_w': 7.588,
     'mla_kv_norm_w': 2.736,
     'lnf_w': 22.76,
     'ln2_w': 13.378}
    for name, (base, spread) in spreads.items():
        noise = np.random.default_rng([zlib.crc32(name.encode()), seed]).standard_normal(out[name].shape)
        drawn = base * np.exp(spread * noise) if base else spread * noise
        out[name] = jnp.asarray(drawn.astype(out[name].dtype))
    for name, factor in factors.items():
        out[name] = (out[name] * factor).astype(out[name].dtype)
    return out
```

```python
from contextlib import ExitStack

import numpy as np

import concourse.bass as bass
from concourse import mybir

F32 = mybir.dt.float32
U32 = mybir.dt.uint32
ALU = mybir.AluOpType
ACT = mybir.ActivationFunctionType
AX_X = mybir.AxisListType.X

P = 128
D_MODEL = 1024
SEQ = 512
DEC_BATCH = 8
DEC_SEQ = 16
PAST = 256
CHUNK = 64
EPS = 1e-6
HEADS = 8
HD = 64
ROPE = 32
RANK = 256
QD = HD + ROPE
IN_COLS = 4 * HEADS * HD + 2 * RANK + ROPE
PROMPT_TILES = SEQ // P
TILES = PROMPT_TILES + 1
SAMPLE = PROMPT_TILES
KD = D_MODEL // P
KEYS = 128
TOPK = 16
EXPERTS = KEYS * KEYS
HP = 2 * HEADS
PICKS = HEADS * TOPK
SLOTS = 8
ROUNDS = PICKS // SLOTS
GROUP = 2
GROUPS = SLOTS // GROUP
SCALE = float(QD) ** -0.5
OFF_Q, OFF_K, OFF_V, OFF_G = 0, 512, 1024, 1536
OFF_CQ, OFF_CKV, OFF_KPE = 2048, 2304, 2560
MASKED = -1e30
LOWEST = -3.0e38
PARTS = 13
SLICES = [2, 1, 1, 1, 1, 1, 1, 1, 1, 1, 2, 2, 1]
assert len(SLICES) == PARTS and sum(SLICES) == ROUNDS


def log_decay():
    return np.log1p(-np.exp2(-5.0 - np.arange(HEADS)))


def tables():
    pos = np.concatenate([np.arange(SEQ), PAST + np.tile(np.arange(DEC_SEQ), DEC_BATCH)]).astype(np.float32)

    def angles(half):
        inv = (np.float32(10000.0) ** (-np.arange(half, dtype=np.float32) / half)).astype(np.float32)
        a = (pos[:, None] * inv[None, :]).astype(np.float32).astype(np.float64)
        lay = lambda m: np.ascontiguousarray(m.astype(np.float32).reshape(TILES, P, half).transpose(1, 0, 2))
        return lay(np.cos(a)), lay(np.sin(a))

    lg = log_decay()
    k_scale = HD ** -0.5
    i = np.arange(P)
    gap = np.abs(i[:, None] - i[None, :])
    seen = (i[:, None] // CHUNK) <= (i[None, :] // CHUNK)
    same = (i[:, None] // DEC_SEQ) == (i[None, :] // DEC_SEQ)
    decay = np.exp(lg[None, :, None] * gap[:, None, :]) * k_scale
    d_prompt = decay * seen[:, None, :]
    d_sample = decay * same[:, None, :]
    s = i % DEC_SEQ
    own = (i[:, None] // DEC_SEQ == np.arange(DEC_BATCH)[None, :]).astype(np.float64)
    q_prompt = np.exp(lg[None, :] * (i[:, None] + 1.0))
    q_sample = np.exp(lg[None, :] * (s[:, None] + 1.0))[:, :, None] * own[:, None, :]
    k_prompt = np.exp(lg[None, :] * (P - 1.0 - i[:, None])) * k_scale
    k_sample = np.exp(lg[None, :] * (DEC_SEQ - 1.0 - s[:, None])) * k_scale
    cos64, sin64 = angles(HD // 2)
    cos32, sin32 = angles(ROPE // 2)
    out = dict(cos64=cos64, sin64=sin64, cos32=cos32, sin32=sin32, d_prompt=d_prompt, d_sample=d_sample,
               q_prompt=q_prompt, q_sample=q_sample, k_prompt=k_prompt, k_sample=k_sample, own=own,
               s_decay=np.tile(np.exp(lg * P)[None, :], (HD, 1)), ident=np.eye(P),
               count16=np.tile(np.arange(TOPK)[None, :], (P, 1)))
    return {k: np.ascontiguousarray(v.astype(np.float32)) for k, v in out.items()}


def build(nc, a, out):
    g_sample = [float(np.exp(v * DEC_SEQ)) for v in log_decay()]
    ctx = ExitStack()
    with ctx:
        def sb(name, shape, dt=F32):
            return ctx.enter_context(nc.sbuf_tensor(name, shape, dt))

        def sem(name):
            return ctx.enter_context(nc.semaphore(name))

        proj_d = nc.dram_tensor("proj_d", (TILES, P, IN_COLS), F32, kind="Internal").ap()

        rows = sb("rows", [P, SLOTS, 2 * D_MODEL])
        WB = 3
        wblk = sb("wblk", [P, WB, D_MODEL])
        PJ, MIX, R = 0, 3104, 4128
        work = sb("work", [P, R + 9216])
        w_uq = sb("w_uq", [P, 2, HEADS * QD])
        w_ukt = sb("w_ukt", [HD, HEADS, RANK])
        w_uv = sb("w_uv", [P, 2, HEADS * HD])
        subk = sb("subk", [P, HP, KEYS])
        dmask = sb("dmask", [P, HEADS, P])
        cos64 = sb("cos64", [P, TILES, HD // 2])
        sin64 = sb("sin64", [P, TILES, HD // 2])
        cos32 = sb("cos32", [P, TILES, ROPE // 2])
        sin32 = sb("sin32", [P, TILES, ROPE // 2])
        q_prompt = sb("q_prompt", [P, HEADS])
        q_sample = sb("q_sample", [P, HEADS, DEC_BATCH])
        k_prompt = sb("k_prompt", [P, HEADS])
        k_sample = sb("k_sample", [P, HEADS])
        own = sb("own", [P, DEC_BATCH])
        s_decay = sb("s_decay", [HD, HEADS])
        count16 = sb("count16", [P, TOPK])
        ident = sb("ident", [P, P])
        ln1 = sb("ln1", [P, KD])
        ln2 = sb("ln2", [P, D_MODEL])
        lnf = sb("lnf", [P, D_MODEL])
        gnw = sb("gnw", [P, HEADS * HD])
        qnw = sb("qnw", [P, RANK])
        kvw = sb("kvw", [P, RANK])
        keys_all = sb("keys_all", [P, 2560])
        ckv = keys_all[:, 0:1024].rearrange("p (t c) -> p t c", t=PROMPT_TILES)
        ckvt = keys_all[:, 1024:2048].rearrange("p (k n) -> p k n", k=2)
        krt = keys_all[0:ROPE, 2048:2560]
        st_in = [keys_all[0:HD, 512 * i:512 * i + 512].rearrange("p (b e) -> p b e", b=DEC_BATCH) for i in range(2)]
        st_out = [keys_all[0:HD, 1024 + 512 * i:1536 + 512 * i].rearrange("p (b e) -> p b e", b=DEC_BATCH)
                  for i in range(2)]
        state = sb("state", [HD, HEADS, HD])
        hbuf = sb("hbuf", [P, 2, D_MODEL])
        xn2 = sb("xn2", [P, 2, D_MODEL])
        eidx = sb("eidx", [P, 2, PICKS], U32)
        gate = sb("gate", [P, 2, PICKS])
        cur = sb("cur", [P, 2, SLOTS], U32)
        DR = 4
        diag = sb("diag", [P, DR, P])
        dots = sb("dots", [P, SLOTS])
        gel = sb("gel", [P, SLOTS])
        wgt = sb("wgt", [P, SLOTS])
        ssq1 = sb("ssq1", [P, TILES])
        rstd1 = sb("rstd1", [P, TILES])
        stat = sb("stat", [P, 64])

        def wv(lo, n, parts=P, dt=None):
            return work[0:parts, lo:lo + n]

        def three(ap, k):
            return ap.rearrange("p (k n) -> p k n", k=k)

        flat_rows = rows[:, :, :].rearrange("p s n -> p (s n)")
        xs = three(flat_rows[:, 0:TILES * D_MODEL], TILES)
        xt = three(flat_rows[:, TILES * D_MODEL:2 * TILES * D_MODEL], KD)
        stage = three(flat_rows[:, 10240:10240 + 4 * 512], 4)
        win = [three(wv(i * 4096, 4096), KD) for i in range(2)]
        pj = wv(PJ, IN_COLS)
        mix = wv(MIX, D_MODEL)
        qk = wv(R, 1024)
        rtmp = wv(R + 1024, 1024)
        q_t = three(wv(R + 2048, 1024, HD), HEADS)
        k_t = three(wv(R + 3072, 1024, HD), HEADS)
        s_td = [three(wv(R + 4096 + 512 * i, 512), 4) for i in range(2)]
        kdec = wv(R + 5120, 512)
        ret_o = wv(R + 5632, 512)
        osq = wv(R + 6144, 512)
        vmask = [three(wv(R + 6656 + 512 * i, 512), DEC_BATCH) for i in range(2)]
        ost = [three(wv(R + 7680, 512), DEC_BATCH)] * 2
        sgm = wv(R + 8192, 512)
        cqn = wv(R, 256)
        ckvn_s = wv(R + 256, 256)
        cq_t = three(wv(R + 512, 256), 2)
        ckvt_s = three(wv(R + 768, 256), 2)
        krt_s = wv(R + 1024, 128, ROPE)
        qpe = wv(R + 1152, 256)
        ptmp = wv(R + 1408, 256)
        kpe = wv(R + 1664, ROPE)
        ktmp = wv(R + 1696, ROPE)
        qpe_t = three(wv(R + 1728, 1024, ROPE), HEADS)
        qn_t = three(wv(R + 2752, 1024, HD), HEADS)
        prob = [wv(R + 2752 + 512 * i, 512) for i in range(2)]
        qlat = wv(R + 3776, 2048).rearrange("p (k h n) -> p k h n", k=2, h=HEADS)
        qlat_s = wv(R + 3776, 2048).rearrange("p (k b m) -> p k b m", k=2, b=DEC_BATCH)
        prob_t = [wv(R + 5824 + 512 * i, 512) for i in range(2)]
        olat = wv(R + 6848, 2048).rearrange("p (k h n) -> p k h n", k=2, h=HEADS)
        mix_t = three(wv(R + 1728, 1024), KD)
        ca_t = [three(wv(PJ + 1536 * i, 512), 2) for i in range(2)]
        ca = [three(wv(PJ + 1536 * i + 512, 512), 2) for i in range(2)]
        ca_r = [wv(PJ + 1536 * i + 1024, 256, ROPE) for i in range(2)]
        ca_n = [wv(PJ + 1536 * i + 1280, 256, DEC_SEQ) for i in range(2)]
        x2_t = three(wv(R, 1024), KD)
        pq_t = three(wv(R + 1024, 2048), HP)
        sc = three(wv(R + 3072, 2048), HP)
        cand = wv(R + 5120, 2048).rearrange("p (h i j) -> p h i j", h=HEADS, i=TOPK)
        candf = three(wv(R + 5120, 2048), HEADS)
        hot = wv(R + 7168, 2048).rearrange("p (h k i) -> p h k i", h=HEADS, k=TOPK)
        tv = three(wv(MIX, 256), HP)
        ti = three(wv(MIX + 256, 256).bitcast(U32), HP)
        tif = three(wv(MIX + 512, 256), HP)
        bv = three(wv(MIX + 768, 128), HEADS)
        bj = three(wv(MIX + 896, 128).bitcast(U32), HEADS)
        sm = [wv(PJ + 128 * i, 128) for i in range(8)]

        F = [ctx.enter_context(nc.psum_tensor(f"F{i}", [P, 512], F32)) for i in range(4)]
        acc = ctx.enter_context(nc.psum_tensor("acc", [P, D_MODEL], F32))
        xps = ctx.enter_context(nc.psum_tensor("xps", [P, D_MODEL], F32))

        def f4(i, parts=P):
            return F[i][0:parts, :].rearrange("p (k n) -> p k n", k=4)

        def f8(i, parts=P):
            return F[i][0:parts, :].rearrange("p (k n) -> p k n", k=8)

        x_in, consts_in, small_in = sem("x_in"), sem("consts_in"), sem("small_in")
        win_in = [sem(f"win_in{i}") for i in range(2)]
        stored = [sem(f"stored{i}") for i in range(4)]
        pj_in, xres_in, wblk_in = sem("pj_in"), sem("xres_in"), [sem(f"wblk_in{i}") for i in range(WB)]
        dmask_in = sem("dmask_in")
        st_landed = [sem(f"st_landed{i}") for i in range(2)]
        st_stored = [sem(f"st_stored{i}") for i in range(2)]
        cache_in = [sem(f"cache_in{i}") for i in range(2)]
        outs_done = sem("outs_done")
        new_ckv_out = sem("new_ckv_out")
        y_out = sem("y_out")
        sq_done, ms1, root1, rstd1_ok = sem("sq_done"), sem("ms1"), sem("root1"), sem("rstd1_ok")
        xt_ok, mm_in, ev_in = sem("xt_ok"), sem("mm_in"), sem("ev_in")
        dve_step, act_step = sem("dve_step"), sem("act_step")
        qk_ok, tr_qk, ev_qk = sem("qk_ok"), sem("tr_qk"), sem("ev_qk")
        mm_s, ev_s, mm_oi, mm_os, mm_up = sem("mm_s"), sem("ev_s"), sem("mm_oi"), sem("mm_os"), sem("mm_up")
        mm_ss, ev_ss, mm_su, ev_su, vm_ok = sem("mm_ss"), sem("ev_ss"), sem("mm_su"), sem("ev_su"), sem("vm_ok")
        kd_ok, state_ok = sem("kd_ok"), sem("state_ok")
        ms_gn, root_gn, eg_ok = sem("ms_gn"), sem("root_gn"), sem("eg_ok")
        y_ok = sem("y_ok")
        ms_c, root_c, c_ok, kpe_ok = sem("ms_c"), sem("root_c"), sem("c_ok"), sem("kpe_ok")
        tr_c, ev_c, mm_pe, qpe_ok = sem("tr_c"), sem("ev_c"), sem("mm_pe"), sem("qpe_ok")
        mm_qn, ev_qn, tr_pe, ev_pe, mm_ql, ev_ql = (sem("mm_qn"), sem("ev_qn"), sem("tr_pe"), sem("ev_pe"),
                                                    sem("mm_ql"), sem("ev_ql"))
        mm_sc, nm_ok, exp_ok, p_ok = sem("mm_sc"), sem("nm_ok"), sem("exp_ok"), sem("p_ok")
        tr_p, ev_pt, mm_pv, ev_pv = sem("tr_p"), sem("ev_pt"), sem("mm_pv"), sem("ev_pv")
        mm_mo, ev_mo, tr_mix, ev_mix, mm_wo, h_ok = (sem("mm_mo"), sem("ev_mo"), sem("tr_mix"), sem("ev_mix"),
                                                     sem("mm_wo"), sem("h_ok"))
        wblk_used = sem("wblk_used")
        ms_2, root_2, x2_ok, tr_x2, ev_x2 = sem("ms_2"), sem("root_2"), sem("x2_ok"), sem("tr_x2"), sem("ev_x2")
        ev_pq, mm_ps, ev_ps = sem("ev_pq"), sem("mm_ps"), sem("ev_ps")
        bd_ok, be_ok, picks_ok = sem("bd_ok"), sem("be_ok"), sem("picks_ok")
        idx_here, rows_free = sem("idx_here"), sem("rows_free")
        rows_in = [sem(f"rows_in{i}") for i in range(SLOTS)]
        xps_ok, dot_ok, gel_ok, wgt_ok, diag_ok = (sem("xps_ok"), sem("dot_ok"), sem("gel_ok"), sem("wgt_ok"),
                                                   sem("diag_ok"))
        sq_f, ms_f, root_f, y_done = sem("sq_f"), sem("ms_f"), sem("root_f"), sem("y_done")

        NIN = TILES * 6
        width = [512] * 5 + [ROPE]
        N_SMALL = 7

        def nkeys(t):
            return P * (t + 1) if t < SAMPLE else PAST + DEC_SEQ

        def pieces(t):
            return [(P * j, min(P, nkeys(t) - P * j)) for j in range((nkeys(t) + P - 1) // P)]

        block = ctx.enter_context(nc.Block())

        @block.sync
        def _(sp):
            def load_win(cb):
                lo = 512 * cb
                sp.dma_start(win[cb % 2][:, :, 0:width[cb]],
                             a["w_in"][:, lo:lo + width[cb]].rearrange("(k p) n -> p k n", p=P)
                             ).then_inc(win_in[cb % 2], 16)

            sp.dma_start(xt, a["x_t"]).then_inc(x_in, 16)
            sp.dma_start(ln1[:, :], a["ln1"]).then_inc(x_in, 16)
            load_win(0)
            sp.dma_start(xs, a["x_all"].rearrange("(t p) d -> p t d", p=P)).then_inc(x_in, 16)
            load_win(1)
            for dst, name in ((cos64, "cos64"), (sin64, "sin64"), (cos32, "cos32"), (sin32, "sin32"),
                              (q_sample, "q_sample"), (dmask, "d_prompt")):
                sp.dma_start(dst[:, :, :], a[name]).then_inc(consts_in, 16)
            for dst, name in ((q_prompt, "q_prompt"), (k_prompt, "k_prompt"), (k_sample, "k_sample"), (own, "own"),
                              (s_decay, "s_decay"), (count16, "count16"), (ident, "ident"), (ln2, "ln2"),
                              (lnf, "lnf"), (gnw, "gn"), (qnw, "qn"), (kvw, "kvn")):
                sp.dma_start(dst[:, :], a[name]).then_inc(consts_in, 16)
            sp.dma_start(w_uq[:, :, :], a["w_uq"].rearrange("(k p) n -> p k n", p=P)).then_inc(small_in, 16)
            sp.dma_start(w_ukt[:, :, :], a["w_ukt"]).then_inc(small_in, 16)
            sp.dma_start(w_uv[:, :, :], a["w_uv"].rearrange("(k p) n -> p k n", p=P)).then_inc(small_in, 16)
            sp.dma_start(subk[:, :, :], a["subk"]).then_inc(small_in, 16)
            for n in range(NIN):
                cb, t = divmod(n, TILES)
                sp.wait_ge(ev_in, n + 1)
                sp.dma_start(proj_d[t, :, 512 * cb:512 * cb + width[cb]], stage[:, n % 4, 0:width[cb]]
                             ).then_inc(stored[n % 4], 16)
                if t == TILES - 1 and cb + 2 < 6:
                    sp.wait_ge(mm_in, TILES * (cb + 1))
                    load_win(cb + 2)
            for i in range(4):
                sp.wait_ge(stored[i], 16 * len(range(i, NIN, 4)))

            def store_y(t):
                sp.wait_ge(y_done, t + 1)
                dst = out["y_prompt"][P * t:P * t + P, :] if t < SAMPLE else out["y_sample"]
                sp.dma_start(dst, hbuf[:, t % 2, :]).then_inc(y_out, 16)

            for t in range(TILES):
                if t >= 1:
                    sp.wait_ge(picks_ok, t)
                else:
                    sp.wait_ge(mm_in, NIN)
                sp.dma_start(pj, proj_d[t]).then_inc(pj_in, 16)
                if t >= 2:
                    sp.wait_ge(y_out, 16 * (t - 1))
                sp.dma_start(hbuf[:, t % 2, :], a["x_all"][P * t:P * t + P, :]).then_inc(xres_in, 16)
                if t == SAMPLE:
                    sp.wait_ge(ev_s, 2 * SAMPLE)
                    sp.dma_start(dmask[:, :, :], a["d_sample"]).then_inc(dmask_in, 16)
                    sp.wait_ge(state_ok, SAMPLE)
                    sp.dma_start(out["state_p"], state[:, :, :]).then_inc(outs_done, 16)
                    for h in range(HEADS):
                        if h >= 2:
                            sp.wait_ge(ev_su, h - 1)
                        sp.dma_start(st_in[h % 2], a["state"][:, h].rearrange("b d e -> d b e")
                                     ).then_inc(st_landed[h % 2], 16)
                        if h >= 1:
                            sp.wait_ge(ev_su, h)
                            sp.dma_start(out["state_s"][:, h - 1].rearrange("b d e -> d b e"), st_out[(h - 1) % 2]
                                         ).then_inc(st_stored[(h - 1) % 2], 16)
                    sp.wait_ge(ev_su, HEADS)
                    sp.dma_start(out["state_s"][:, HEADS - 1].rearrange("b d e -> d b e"), st_out[(HEADS - 1) % 2]
                                 ).then_inc(st_stored[(HEADS - 1) % 2], 16)
                sp.wait_ge(c_ok, t + 1)
                if t < SAMPLE:
                    sp.dma_start(out["ckv_p"][P * t:P * t + P, :], ckv[:, t, :]).then_inc(outs_done, 16)
                else:
                    sp.dma_start(out["ckv_s"], ckvn_s).then_inc(new_ckv_out, 16)
                sp.wait_ge(kpe_ok, t + 1)
                dst = out["kr_p"][P * t:P * t + P, :] if t < SAMPLE else out["kr_s"]
                sp.dma_start(dst, kpe).then_inc(outs_done, 16)
                if t == SAMPLE:
                    sp.wait_ge(new_ckv_out, 16)
                    for b in range(DEC_BATCH):
                        if b >= 2:
                            sp.wait_ge(mm_pv, SAMPLE * HEADS + b - 1)
                        s = cache_in[b % 2]
                        sp.dma_start(ca_t[b % 2], a["cache_t"][b]).then_inc(s, 16)
                        sp.dma_start(ca_r[b % 2], a["cache_rt"][b]).then_inc(s, 16)
                        sp.dma_start(ca[b % 2], a["cache"][b].rearrange("(k p) c -> p k c", p=P)).then_inc(s, 16)
                        sp.dma_start(ca_n[b % 2], out["ckv_s"][DEC_SEQ * b:DEC_SEQ * b + DEC_SEQ, :]
                                     ).then_inc(s, 16)
                for i in range(KD + HP):
                    n = t * (KD + HP) + i
                    if n >= WB:
                        sp.wait_ge(wblk_used, n - WB + 1)
                    src = a["w_o"][P * i:P * i + P, :] if i < KD else a["w_q"][i - KD]
                    sp.dma_start(wblk[:, n % WB, :], src).then_inc(wblk_in[n % WB], 16)
                if t >= 1:
                    store_y(t - 1)
            store_y(SAMPLE)
            sp.wait_ge(y_out, 16 * TILES)
            sp.wait_ge(outs_done, 16 * (1 + SAMPLE + TILES))
            for i in range(2):
                sp.wait_ge(st_stored[i], 16 * HEADS // 2)

        @block.gpsimd
        def _(pool):
            for t in range(TILES):
                pool.wait_ge(picks_ok, t + 1)
                with pool.Fori(0, ROUNDS // 2) as r2:
                    for half in range(2):
                        j = r2 * 2 + (t * ROUNDS + half)
                        pool.wait_ge(rows_free, j * SLOTS + 1)
                        pool.nop(nofuse=True)
                        nc.gpsimd.tensor_copy(cur[:, half, :], eidx[:, t % 2, bass.ds(r2 * (2 * SLOTS) + half * SLOTS, SLOTS)]
                                              ).then_inc(idx_here, 1)
                        pool.wait_ge(idx_here, j + 1)
                        for s in range(SLOTS):
                            pool.wait_ge(rows_free, j * SLOTS + s + 1)
                            pool.nop(nofuse=True)
                            nc.gpsimd.indirect_dma_start(
                                rows[:, s, :], None, a["uv"], bass.IndirectOffsetOnAxis(cur[:, half, s:s + 1], 0)
                            ).then_inc(rows_in[s], 16)

        @block.tensor
        def _(pe):
            mm, tr = nc.tensor.matmul, nc.tensor.transpose
            pe.wait_ge(x_in, 48)
            pe.wait_ge(xt_ok, KD)
            for n in range(NIN):
                cb, t = divmod(n, TILES)
                if t == 0:
                    pe.wait_ge(win_in[cb % 2], 16 * (cb // 2 + 1))
                if n >= 4:
                    pe.wait_ge(ev_in, n - 3)
                for k in range(KD):
                    last = mm(F[n % 4][:, 0:width[cb]], xt[:, k, P * t:P * t + P], win[cb % 2][:, k, 0:width[cb]],
                              start=(k == 0), stop=(k == KD - 1))
                last.then_inc(mm_in, 1)
            pe.wait_ge(ev_in, NIN)
            pe.wait_ge(consts_in, 16 * 18)
            pe.wait_ge(small_in, 16 * 4)

            def retention(t):
                pe.wait_ge(qk_ok, t + 1)
                for g in range(4):
                    dst = f4(g, HD)
                    for i in range(4):
                        last = tr(dst[:, i, :], qk[:, HD * (4 * g + i):HD * (4 * g + i + 1)], ident[:, :])
                    last.then_inc(tr_qk, 1)
                pe.wait_ge(ev_qk, 4 * (t + 1))
                for g in range(2):
                    for i in range(4):
                        h = 4 * g + i
                        last = mm(f4(g)[:, i, :], k_t[:, h, :], q_t[:, h, :], start=True, stop=True)
                    last.then_inc(mm_s, 1)
                v = pj[:, OFF_V:OFF_V + 512]
                for g in range(2):
                    pe.wait_ge(ev_s, 2 * t + g + 1)
                    for i in range(4):
                        h = 4 * g + i
                        last = mm(f8(2)[:, h, :], s_td[g][:, i, :], v[:, HD * h:HD * h + HD], start=True, stop=True)
                last.then_inc(mm_oi, 1)
                pe.wait_ge(kd_ok, t + 1)
                if t < SAMPLE:
                    if t >= 1:
                        pe.wait_ge(state_ok, t)
                        for h in range(HEADS):
                            last = mm(f8(3)[:, h, :], q_t[:, h, :], state[:, h, :], start=True, stop=True)
                        last.then_inc(mm_os, 1)
                    for h in range(HEADS):
                        last = mm(f8(0, HD)[:, h, :], kdec[:, HD * h:HD * h + HD], v[:, HD * h:HD * h + HD],
                                  start=True, stop=True)
                    last.then_inc(mm_up, 1)
                else:
                    for h in range(HEADS):
                        if h >= 2:
                            pe.wait_ge(ev_ss, h - 1)
                        pe.wait_ge(st_landed[h % 2], 16 * (h // 2 + 1))
                        mm(F[h % 2][:, :], q_t[:, h, :], st_in[h % 2].rearrange("p b e -> p (b e)"),
                           start=True, stop=True).then_inc(mm_ss, 1)
                        if h >= 1:
                            pe.wait_ge(ev_su, h)
                        pe.wait_ge(vm_ok, h + 1)
                        mm(F[3][0:HD, :], kdec[:, HD * h:HD * h + HD], vmask[h % 2].rearrange("p b e -> p (b e)"),
                           start=True, stop=True).then_inc(mm_su, 1)

            def latent(t):
                kv_new = ckv[:, t, :] if t < SAMPLE else ckvn_s
                pe.wait_ge(c_ok, t + 1)
                pe.wait_ge(kpe_ok, t + 1)
                for k in range(2):
                    tr(f4(2)[:, k, :], cqn[:, P * k:P * k + P], ident[:, :])
                    tr(f4(2)[:, 2 + k, :], kv_new[:, P * k:P * k + P], ident[:, :])
                tr(F[3][0:ROPE, 0:P], kpe, ident[:, :]).then_inc(tr_c, 1)
                pe.wait_ge(ev_c, t + 1)
                w4 = w_uq[:, :, :].rearrange("p k (h d) -> p k h d", h=HEADS)
                for k in range(2):
                    last = mm(F[0][:, 0:256], cq_t[:, k, :], w4[:, k, :, HD:QD], start=(k == 0), stop=(k == 1))
                last.then_inc(mm_pe, 1)
                for g in range(2):
                    for i in range(4):
                        for k in range(2):
                            last = mm(f4(1 + g, HD)[:, i, :], w4[:, k, 4 * g + i, 0:HD], cq_t[:, k, :],
                                      start=(k == 0), stop=(k == 1))
                    last.then_inc(mm_qn, 1)
                pe.wait_ge(qpe_ok, t + 1)
                for g, bank in ((0, 3), (1, 0)):
                    for i in range(4):
                        h = 4 * g + i
                        last = tr(f4(bank, ROPE)[:, i, :], qpe[:, ROPE * h:ROPE * h + ROPE], ident[:, :])
                    last.then_inc(tr_pe, 1)
                pe.wait_ge(ev_qn, 2 * (t + 1))
                for n, bank in enumerate((1, 2, 3, 0)):
                    if n == 2:
                        pe.wait_ge(ev_pe, 2 * (t + 1))
                    k, g = divmod(n, 2)
                    for i in range(4):
                        h = 4 * g + i
                        last = mm(f4(bank)[:, i, :], w_ukt[:, h, P * k:P * k + P], qn_t[:, h, :],
                                  start=True, stop=True)
                    last.then_inc(mm_ql, 1)
                pe.wait_ge(ev_ql, 4 * (t + 1))

            def scores(t, u):
                n = t * HEADS + u
                if u >= 2:
                    pe.wait_ge(exp_ok, n - 1)
                nk = nkeys(t)
                dst = F[u % 2]
                if t < SAMPLE:
                    for k in range(2):
                        mm(dst[:, 0:nk], qlat[:, k, u, :], ckvt[:, k, 0:nk], start=(k == 0), stop=False)
                    last = mm(dst[:, 0:nk], qpe_t[:, u, :], krt[:, 0:nk], start=False, stop=True)
                else:
                    pe.wait_ge(cache_in[u % 2], 64 * (u // 2 + 1))
                    cut = slice(DEC_SEQ * u, DEC_SEQ * u + DEC_SEQ)
                    for k in range(2):
                        mm(dst[:, 0:PAST], qlat_s[:, k, u, :], ca_t[u % 2][:, k, :], start=(k == 0), stop=False)
                    mm(dst[:, 0:PAST], qpe_t[:, u, :], ca_r[u % 2], start=False, stop=True)
                    for k in range(2):
                        mm(dst[:, PAST:nk], qlat_s[:, k, u, :], ckvt_s[:, k, cut], start=(k == 0), stop=False)
                    last = mm(dst[:, PAST:nk], qpe_t[:, u, :], krt_s[:, cut], start=False, stop=True)
                last.then_inc(mm_sc, 1)

            def values(t, u):
                n = t * HEADS + u
                pe.wait_ge(p_ok, n + 1)
                if u >= 1:
                    pe.wait_ge(ev_pt, n)
                for j, (lo, w) in enumerate(pieces(t)):
                    last = tr(F[2][0:w, P * j:P * j + P], prob[u % 2][:, lo:lo + w], ident[:, :])
                last.then_inc(tr_p, 1)
                pe.wait_ge(ev_pt, n + 1)
                if u >= 1:
                    pe.wait_ge(ev_pv, n)
                for k in range(2):
                    for j, (lo, w) in enumerate(pieces(t)):
                        if t < SAMPLE:
                            lhs = ckv[:, j, P * k:P * k + P]
                        else:
                            lhs = ca[u % 2][:, j, P * k:P * k + P] if j < 2 else ca_n[u % 2][:, P * k:P * k + P]
                        last = mm(F[3][:, P * k:P * k + P], lhs, prob_t[u % 2][0:w, P * j:P * j + P],
                                  start=(j == 0), stop=(j == len(pieces(t)) - 1))
                last.then_inc(mm_pv, 1)

            def take_block(n):
                pe.wait_ge(wblk_in[n % WB], 16 * (n // WB + 1))

            def project(t):
                pe.wait_ge(ev_pv, HEADS * (t + 1))
                for h in range(HEADS):
                    for k in range(2):
                        last = mm(f8(0)[:, h, :], olat[:, k, h, :], w_uv[:, k, HD * h:HD * h + HD],
                                  start=(k == 0), stop=(k == 1))
                last.then_inc(mm_mo, 1)
                pe.wait_ge(y_ok, t + 1)
                pe.wait_ge(ev_mo, t + 1)
                for g in range(2):
                    for i in range(4):
                        k = 4 * g + i
                        last = tr(f4(1 + g)[:, i, :], mix[:, P * k:P * k + P], ident[:, :])
                    last.then_inc(tr_mix, 1)
                pe.wait_ge(ev_mix, 2 * (t + 1))
                for k in range(KD):
                    n = t * (KD + HP) + k
                    take_block(n)
                    for half, bank in ((0, 3), (1, 0)):
                        last = mm(F[bank][:, :], mix_t[:, k, :], wblk[:, n % WB, 512 * half:512 * half + 512],
                                  start=(k == 0), stop=(k == KD - 1), skip_group_check=True)
                    last.then_inc(wblk_used, 1)
                pe.wait_ge(x2_ok, t + 1)
                for g in range(2):
                    for i in range(4):
                        k = 4 * g + i
                        last = tr(f4(1 + g)[:, i, :], xn2[:, t % 2, P * k:P * k + P], ident[:, :])
                    last.then_inc(tr_x2, 1)
                pe.wait_ge(ev_x2, 2 * (t + 1))

            def queries(t, g):
                bank = 3 if g % 2 == 0 else 0
                if g >= 2:
                    pe.wait_ge(ev_pq, 4 * t + g - 1)
                for i in range(4):
                    n = t * (KD + HP) + KD + 4 * g + i
                    take_block(n)
                    for k in range(KD):
                        last = mm(f4(bank)[:, i, :], wblk[:, n % WB, P * k:P * k + P], x2_t[:, k, :],
                                  start=(k == 0), stop=(k == KD - 1))
                    last.then_inc(wblk_used, 1)
                bank = 1 + g % 2
                pe.wait_ge(ev_pq, 4 * t + g + 1)
                if g >= 2:
                    pe.wait_ge(ev_ps, 4 * t + g - 1)
                for i in range(4):
                    hp = 4 * g + i
                    last = mm(f4(bank)[:, i, :], pq_t[:, hp, :], subk[:, hp, :], start=True, stop=True)
                last.then_inc(mm_ps, 1)

            def experts(t, lo, hi):
                if lo == 0:
                    if t >= 1:
                        pe.wait_ge(y_done, t)
                    for c in range(2):
                        mm(acc[:, 512 * c:512 * c + 512], ident[:, :], hbuf[:, t % 2, 512 * c:512 * c + 512],
                           start=True, stop=False, skip_group_check=True)
                with pe.Fori(lo, hi) as r:
                    j = r + t * ROUNDS
                    for s in range(SLOTS):
                        pe.wait_ge(diag_ok, j * SLOTS + s + 1)
                        for c in range(2):
                            last = mm(acc[:, 512 * c:512 * c + 512], diag[:, s % DR, :],
                                      rows[:, s, D_MODEL + 512 * c:D_MODEL + 512 * c + 512],
                                      start=False, stop=False, skip_group_check=True)
                        last.then_inc(rows_free, 1)

            pe.sem_inc(rows_free, SLOTS)
            for t in range(TILES + 1):
                done = 0
                for part in range(PARTS):
                    if t < TILES:
                        if part == 0:
                            retention(t)
                        elif part == 1:
                            latent(t)
                            scores(t, 0)
                        elif part < 10:
                            u = part - 2
                            if u + 1 < HEADS:
                                scores(t, u + 1)
                            values(t, u)
                        elif part == 10:
                            project(t)
                        elif part == 11:
                            for g in range(2):
                                queries(t, g)
                        else:
                            for g in range(2, 4):
                                queries(t, g)
                    if t >= 1:
                        experts(t - 1, done, done + SLICES[part])
                        done += SLICES[part]

        @block.scalar
        def _(act):
            copy = nc.scalar.copy
            steps = [0]

            def link(ins):
                steps[0] += 1
                ins.then_inc(act_step, 1)
                act.wait_ge(act_step, steps[0])

            act.wait_ge(x_in, 48)
            for t in range(TILES):
                nc.scalar.activation(stage[:, 0:2, :].rearrange("p a b -> p (a b)"), xs[:, t, :], ACT.Square,
                                     accum_out=ssq1[:, t:t + 1]).then_inc(sq_done, 1)
                act.wait_ge(sq_done, t + 1)
            act.wait_ge(ms1, 1)
            nc.scalar.activation(rstd1[:, :], ssq1[:, :], ACT.Sqrt).then_inc(root1, 1)
            act.wait_ge(rstd1_ok, 1)
            for n in range(NIN):
                cb, t = divmod(n, TILES)
                act.wait_ge(mm_in, n + 1)
                if n >= 4:
                    act.wait_ge(stored[n % 4], 16 * (n // 4))
                nc.scalar.activation(stage[:, n % 4, 0:width[cb]], F[n % 4][:, 0:width[cb]], ACT.Copy,
                                     scale=rstd1[:, t:t + 1]).then_inc(ev_in, 1)

            def retention(t):
                for g in range(4):
                    act.wait_ge(tr_qk, 4 * t + g + 1)
                    dst = (q_t, q_t, k_t, k_t)[g][:, 4 * (g % 2):4 * (g % 2) + 4, :]
                    copy(dst, f4(g, HD)).then_inc(ev_qk, 1)
                act.wait_ge(pj_in, 16 * (t + 1))
                nc.scalar.activation(sgm, pj[:, OFF_G:OFF_G + 512], ACT.Exp, scale=-1.0).then_inc(eg_ok, 1)
                act.wait_ge(ms_gn, t + 1)
                nc.scalar.activation(stat[:, 8:16], stat[:, 0:8], ACT.Sqrt).then_inc(root_gn, 1)
                act.wait_ge(ms_c, t + 1)
                nc.scalar.activation(stat[:, 18:20], stat[:, 16:18], ACT.Sqrt).then_inc(root_c, 1)

            def spread_copy(t, dst, g, src):
                if t < SAMPLE:
                    return copy(dst[:, 4 * g:4 * g + 4, :], src)
                by_seq = dst.rearrange("p b (h s) -> p b h s", h=HEADS)[:, :, 4 * g:4 * g + 4, :]
                return copy(by_seq, src.rearrange("p h (b s) -> p b h s", b=DEC_BATCH))

            def latent(t):
                act.wait_ge(tr_c, t + 1)
                copy(cq_t, f4(2)[:, 0:2, :])
                if t < SAMPLE:
                    copy(ckvt[:, :, P * t:P * t + P], f4(2)[:, 2:4, :])
                    copy(krt[:, P * t:P * t + P], F[3][0:ROPE, 0:P]).then_inc(ev_c, 1)
                else:
                    copy(ckvt_s, f4(2)[:, 2:4, :])
                    copy(krt_s, F[3][0:ROPE, 0:P]).then_inc(ev_c, 1)
                for g in range(2):
                    act.wait_ge(mm_qn, 2 * t + g + 1)
                    copy(qn_t[:, 4 * g:4 * g + 4, :], f4(1 + g, HD)).then_inc(ev_qn, 1)
                for g, bank in ((0, 3), (1, 0)):
                    act.wait_ge(tr_pe, 2 * t + g + 1)
                    spread_copy(t, qpe_t, g, f4(bank, ROPE)).then_inc(ev_pe, 1)
                for n, bank in enumerate((1, 2, 3, 0)):
                    act.wait_ge(mm_ql, 4 * t + n + 1)
                    k, g = divmod(n, 2)
                    spread_copy(t, qlat[:, k, :, :], g, f4(bank)).then_inc(ev_ql, 1)

            def exps(t, u):
                n = t * HEADS + u
                nk = nkeys(t)
                act.wait_ge(nm_ok, n + 1)
                if u >= 2:
                    act.wait_ge(tr_p, n - 1)
                nc.scalar.activation(prob[u % 2][:, 0:nk], F[u % 2][:, 0:nk], ACT.Exp, scale=SCALE,
                                     bias=stat[:, 24 + u % 2:25 + u % 2],
                                     accum_out=stat[:, 26 + u % 2:27 + u % 2]).then_inc(exp_ok, 1)

            def values(t, u):
                n = t * HEADS + u
                act.wait_ge(tr_p, n + 1)
                if u >= 2:
                    act.wait_ge(mm_pv, n - 1)
                full = [q for q in pieces(t) if q[1] == P]
                last = copy(prob_t[u % 2][:, 0:P * len(full)], F[2][:, 0:P * len(full)])
                if t == SAMPLE:
                    last = copy(prob_t[u % 2][0:DEC_SEQ, PAST:PAST + P], F[2][0:DEC_SEQ, PAST:PAST + P])
                last.then_inc(ev_pt, 1)
                act.wait_ge(mm_pv, n + 1)
                src = F[3][:, 0:256].rearrange("p (k n) -> p k n", k=2)
                if t < SAMPLE:
                    copy(olat[:, :, u, :], src).then_inc(ev_pv, 1)
                else:
                    for k in range(2):
                        last = copy(olat[:, k, :, DEC_SEQ * u:DEC_SEQ * u + DEC_SEQ],
                                    src[:, k, :].rearrange("p (h s) -> p h s", h=HEADS))
                    last.then_inc(ev_pv, 1)

            def project(t):
                act.wait_ge(mm_mo, t + 1)
                copy(mix[:, 512:1024], F[0][:, :]).then_inc(ev_mo, 1)
                for g in range(2):
                    act.wait_ge(tr_mix, 2 * t + g + 1)
                    copy(mix_t[:, 4 * g:4 * g + 4, :], f4(1 + g)).then_inc(ev_mix, 1)
                act.wait_ge(ms_2, t + 1)
                nc.scalar.activation(stat[:, 31:32], stat[:, 30:31], ACT.Sqrt).then_inc(root_2, 1)
                for g in range(2):
                    act.wait_ge(tr_x2, 2 * t + g + 1)
                    copy(x2_t[:, 4 * g:4 * g + 4, :], f4(1 + g)).then_inc(ev_x2, 1)

            def queries(t, g):
                bank = 3 if g % 2 == 0 else 0
                act.wait_ge(wblk_used, t * (KD + HP) + KD + 4 * g + 4)
                copy(pq_t[:, 4 * g:4 * g + 4, :], f4(bank)).then_inc(ev_pq, 1)
                act.wait_ge(mm_ps, 4 * t + g + 1)
                copy(sc[:, 4 * g:4 * g + 4, :], f4(1 + g % 2)).then_inc(ev_ps, 1)

            def softmax_picks(t):
                act.wait_ge(bd_ok, t + 1)
                nc.scalar.activation(sm[1], sm[0], ACT.Exp).then_inc(be_ok, 1)

            def experts(t, lo, hi):
                with act.Fori(lo, hi) as r:
                    j = r + t * ROUNDS
                    for g in range(GROUPS):
                        act.wait_ge(dot_ok, j * GROUPS + g + 1)
                        cols = slice(GROUP * g, GROUP * g + GROUP)
                        nc.scalar.activation(gel[:, cols], dots[:, cols], ACT.Gelu).then_inc(gel_ok, 1)
                        act.wait_ge(gel_ok, j * GROUPS + g + 1)
                        act.wait_ge(picks_ok, t + 1)
                        for i in range(GROUP):
                            s = GROUP * g + i
                            nc.scalar.activation(wgt[:, s:s + 1], gel[:, s:s + 1], ACT.Copy,
                                                 scale=gate[:, t % 2, bass.ds(r * SLOTS + s, 1)]
                                                 ).then_inc(wgt_ok, 1)
                        for i in range(GROUP):
                            s = GROUP * g + i
                            act.wait_ge(wgt_ok, j * SLOTS + s + 1)
                            act.wait_ge(rows_free, j * SLOTS + s + 1 + SLOTS - DR)
                            nc.scalar.activation(diag[:, s % DR, :], ident[:, :], ACT.Copy,
                                                 scale=wgt[:, s:s + 1]).then_inc(diag_ok, 1)
                if hi == ROUNDS:
                    act.wait_ge(rows_free, SLOTS + PICKS * (t + 1))
                    act.wait_ge(dot_ok, GROUPS * ROUNDS * (t + 1))
                    nc.scalar.activation(xps[:, :], acc[:, :], ACT.Square, accum_out=stat[:, 36:37]
                                         ).then_inc(sq_f, 1)
                    act.wait_ge(ms_f, t + 1)
                    nc.scalar.activation(stat[:, 38:39], stat[:, 37:38], ACT.Sqrt).then_inc(root_f, 1)

            for t in range(TILES + 1):
                done = 0
                for part in range(PARTS):
                    if t < TILES:
                        if part == 0:
                            retention(t)
                        elif part == 1:
                            latent(t)
                            exps(t, 0)
                        elif part < 10:
                            u = part - 2
                            if u + 1 < HEADS:
                                exps(t, u + 1)
                            values(t, u)
                        elif part == 10:
                            project(t)
                        elif part == 11:
                            for g in range(2):
                                queries(t, g)
                        else:
                            for g in range(2, 4):
                                queries(t, g)
                            softmax_picks(t)
                    if t >= 1:
                        experts(t - 1, done, done + SLICES[part])
                        done += SLICES[part]

        @block.vector
        def _(dve):
            v = nc.vector
            steps = [0]

            def link(ins):
                steps[0] += 1
                ins.then_inc(dve_step, 1)
                dve.wait_ge(dve_step, steps[0])

            def row(ap, n):
                return ap.unsqueeze(2).to_broadcast([ap.shape[0], ap.shape[1], n])

            def mid(ap, n):
                return ap.unsqueeze(1).to_broadcast([ap.shape[0], n, ap.shape[1]])

            def rotate(dst, src, tmp, cos, sin, heads, half):
                s = src.rearrange("p (h c d) -> p h c d", h=heads, c=2)
                d = dst.rearrange("p (h c d) -> p h c d", h=heads, c=2)
                m = tmp.rearrange("p (h c d) -> p h c d", h=heads, c=2)
                c, sn = mid(cos, heads), mid(sin, heads)
                v.tensor_tensor(d[:, :, 0, :], s[:, :, 0, :], c, ALU.mult)
                v.tensor_tensor(m[:, :, 0, :], s[:, :, 1, :], sn, ALU.mult)
                v.tensor_tensor(d[:, :, 1, :], s[:, :, 1, :], c, ALU.mult)
                link(v.tensor_tensor(m[:, :, 1, :], s[:, :, 0, :], sn, ALU.mult))
                v.tensor_tensor(d[:, :, 0, :], d[:, :, 0, :], m[:, :, 0, :], ALU.subtract)
                return v.tensor_tensor(d[:, :, 1, :], d[:, :, 1, :], m[:, :, 1, :], ALU.add)

            dve.wait_ge(x_in, 48)
            for k in range(KD):
                v.tensor_scalar(xt[:, k, :], xt[:, k, :], ln1[:, k:k + 1], None, ALU.mult).then_inc(xt_ok, 1)
            dve.wait_ge(sq_done, TILES)
            v.tensor_scalar(ssq1[:, :], ssq1[:, :], 1.0 / D_MODEL, EPS, ALU.mult, ALU.add).then_inc(ms1, 1)
            dve.wait_ge(root1, 1)
            v.reciprocal(rstd1[:, :], rstd1[:, :]).then_inc(rstd1_ok, 1)
            dve.wait_ge(consts_in, 16 * 18)

            def retention(t):
                sample = t == SAMPLE
                dve.wait_ge(pj_in, 16 * (t + 1))
                rotate(qk, pj[:, 0:1024], rtmp, cos64[:, t, :], sin64[:, t, :], 2 * HEADS, HD // 2
                       ).then_inc(qk_ok, 1)
                dve.wait_ge(qk_ok, t + 1)
                kd = k_sample if sample else k_prompt
                v.tensor_tensor(three(kdec, HEADS), three(qk[:, 512:1024], HEADS), row(kd[:, :], HD), ALU.mult
                                ).then_inc(kd_ok, 1)
                if sample:
                    dve.wait_ge(dmask_in, 16)
                for g in range(2):
                    dve.wait_ge(mm_s, 2 * t + g + 1)
                    v.tensor_tensor(s_td[g], f4(g), dmask[:, 4 * g:4 * g + 4, :], ALU.mult).then_inc(ev_s, 1)
                o3 = three(ret_o, HEADS)
                if sample:
                    vv = three(pj[:, OFF_V:OFF_V + 512], HEADS)
                    for h in range(HEADS):
                        if h >= 2:
                            dve.wait_ge(mm_su, h - 1)
                        v.tensor_tensor(vmask[h % 2], mid(vv[:, h, :], DEC_BATCH), row(own[:, :], HD), ALU.mult
                                        ).then_inc(vm_ok, 1)
                        dve.wait_ge(mm_ss, h + 1)
                        v.tensor_tensor(ost[0], f8(h % 2), row(q_sample[:, h, :], HD), ALU.mult).then_inc(ev_ss, 1)
                        dve.wait_ge(ev_ss, h + 1)
                        link(v.tensor_reduce(o3[:, h, :], ost[0].rearrange("p b e -> p e b"), AX_X, ALU.add))
                        dve.wait_ge(mm_su, h + 1)
                        if h >= 2:
                            dve.wait_ge(st_stored[h % 2], 16 * (h // 2))
                        v.scalar_tensor_tensor(st_out[h % 2].rearrange("p b e -> p (b e)"),
                                               st_in[h % 2].rearrange("p b e -> p (b e)"), g_sample[h],
                                               F[3][0:HD, :], ALU.mult, ALU.add).then_inc(ev_su, 1)
                    dve.wait_ge(mm_oi, t + 1)
                    link(v.tensor_tensor(ret_o, ret_o, F[2][:, :], ALU.add))
                else:
                    dve.wait_ge(mm_oi, t + 1)
                    if t == 0:
                        link(v.tensor_copy(ret_o, F[2][:, :]))
                    else:
                        dve.wait_ge(mm_os, t)
                        link(v.tensor_tensor(o3, f8(3), row(q_prompt[:, :], HD), ALU.mult))
                        link(v.tensor_tensor(ret_o, ret_o, F[2][:, :], ALU.add))
                    dve.wait_ge(mm_up, t + 1)
                    if t == 0:
                        v.tensor_copy(state[:, :, :], f8(0, HD)).then_inc(state_ok, 1)
                    else:
                        link(v.tensor_tensor(state[:, :, :], state[:, :, :], row(s_decay[:, :], HD), ALU.mult))
                        v.tensor_tensor(state[:, :, :], state[:, :, :], f8(0, HD), ALU.add).then_inc(state_ok, 1)
                    dve.wait_ge(state_ok, t + 1)
                mean, var = stat[:, 40:48], stat[:, 0:8]
                link(v.tensor_reduce(mean, o3, AX_X, ALU.add))
                link(v.tensor_scalar(mean, mean, 1.0 / HD, None, ALU.mult))
                link(v.tensor_tensor(o3, o3, row(mean, HD), ALU.subtract))
                link(v.tensor_tensor(osq, ret_o, ret_o, ALU.mult))
                link(v.tensor_reduce(var, three(osq, HEADS), AX_X, ALU.add))
                v.tensor_scalar(var, var, 1.0 / HD, EPS, ALU.mult, ALU.add).then_inc(ms_gn, 1)
                dve.wait_ge(eg_ok, t + 1)
                link(v.tensor_scalar(sgm, sgm, 1.0, None, ALU.add))
                link(v.reciprocal(sgm, sgm))
                link(v.tensor_tensor(sgm, sgm, pj[:, OFF_G:OFF_G + 512], ALU.mult))
                dve.wait_ge(root_gn, t + 1)
                link(v.reciprocal(stat[:, 8:16], stat[:, 8:16]))
                link(v.tensor_tensor(o3, o3, row(stat[:, 8:16], HD), ALU.mult))
                link(v.tensor_tensor(ret_o, ret_o, gnw[:, :], ALU.mult))
                v.tensor_tensor(mix[:, 0:512], ret_o, sgm, ALU.mult).then_inc(y_ok, 1)
                dve.wait_ge(y_ok, t + 1)
                v.tensor_tensor_reduce(cqn, pj[:, OFF_CQ:OFF_CQ + RANK], pj[:, OFF_CQ:OFF_CQ + RANK], 1.0, 0.0,
                                       ALU.mult, ALU.add, stat[:, 16:17])
                kv = ckvn_s if sample else ckv[:, t, :]
                link(v.tensor_tensor_reduce(kv, pj[:, OFF_CKV:OFF_CKV + RANK], pj[:, OFF_CKV:OFF_CKV + RANK],
                                            1.0, 0.0, ALU.mult, ALU.add, stat[:, 17:18]))
                v.tensor_scalar(stat[:, 16:18], stat[:, 16:18], 1.0 / RANK, EPS, ALU.mult, ALU.add
                                ).then_inc(ms_c, 1)
                dve.wait_ge(root_c, t + 1)
                link(v.reciprocal(stat[:, 18:20], stat[:, 18:20]))
                v.scalar_tensor_tensor(cqn, pj[:, OFF_CQ:OFF_CQ + RANK], stat[:, 18:19], qnw[:, :],
                                       ALU.mult, ALU.mult)
                v.scalar_tensor_tensor(kv, pj[:, OFF_CKV:OFF_CKV + RANK], stat[:, 19:20], kvw[:, :],
                                       ALU.mult, ALU.mult).then_inc(c_ok, 1)
                rotate(kpe, pj[:, OFF_KPE:OFF_KPE + ROPE], ktmp, cos32[:, t, :], sin32[:, t, :], 1, ROPE // 2
                       ).then_inc(kpe_ok, 1)

            def latent(t):
                dve.wait_ge(mm_pe, t + 1)
                rotate(qpe, F[0][:, 0:256], ptmp, cos32[:, t, :], sin32[:, t, :], HEADS, ROPE // 2
                       ).then_inc(qpe_ok, 1)

            def maxima(t, u):
                n = t * HEADS + u
                nk = nkeys(t)
                dve.wait_ge(mm_sc, n + 1)
                if t < SAMPLE:
                    link(v.memset(F[u % 2][0:CHUNK, nk - CHUNK:nk], MASKED))
                link(v.tensor_reduce(stat[:, 20 + u % 2:21 + u % 2], F[u % 2][:, 0:nk], AX_X, ALU.max))
                if u >= 2:
                    dve.wait_ge(exp_ok, n - 1)
                v.tensor_scalar(stat[:, 24 + u % 2:25 + u % 2], stat[:, 20 + u % 2:21 + u % 2], -SCALE, None,
                                ALU.mult).then_inc(nm_ok, 1)

            def normalise(t, u):
                n = t * HEADS + u
                nk = nkeys(t)
                dve.wait_ge(exp_ok, n + 1)
                link(v.reciprocal(stat[:, 28 + u % 2:29 + u % 2], stat[:, 26 + u % 2:27 + u % 2]))
                v.tensor_scalar(prob[u % 2][:, 0:nk], prob[u % 2][:, 0:nk], stat[:, 28 + u % 2:29 + u % 2], None,
                                ALU.mult).then_inc(p_ok, 1)

            def project(t):
                h = hbuf[:, t % 2, :]
                x2 = xn2[:, t % 2, :]
                dve.wait_ge(wblk_used, t * (KD + HP) + KD)
                dve.wait_ge(xres_in, 16 * (t + 1))
                v.tensor_tensor(h[:, 0:512], h[:, 0:512], F[3][:, :], ALU.add)
                link(v.tensor_tensor(h[:, 512:1024], h[:, 512:1024], F[0][:, :], ALU.add))
                link(v.tensor_tensor_reduce(x2, h, h, 1.0, 0.0, ALU.mult, ALU.add, stat[:, 30:31]))
                v.tensor_scalar(stat[:, 30:31], stat[:, 30:31], 1.0 / D_MODEL, EPS, ALU.mult, ALU.add
                                ).then_inc(ms_2, 1)
                dve.wait_ge(root_2, t + 1)
                link(v.reciprocal(stat[:, 31:32], stat[:, 31:32]))
                v.scalar_tensor_tensor(x2, h, stat[:, 31:32], ln2[:, :], ALU.mult, ALU.mult).then_inc(x2_ok, 1)

            def top16(n, values_of, vals, idx):
                for i in range(n):
                    last = v.max(vals[:, i, 0:8], values_of(i))
                link(last)
                for i in range(n):
                    v.max_index(idx[:, i, 0:8], vals[:, i, 0:8], values_of(i))
                for i in range(n):
                    last = v.match_replace(values_of(i), vals[:, i, 0:8], values_of(i), LOWEST)
                link(last)
                for i in range(n):
                    last = v.max(vals[:, i, 8:16], values_of(i))
                link(last)
                for i in range(n):
                    last = v.max_index(idx[:, i, 8:16], vals[:, i, 8:16], values_of(i))
                link(last)

            def route(t):
                dve.wait_ge(ev_ps, 4 * (t + 1))
                top16(HP, lambda i: sc[:, i, :], tv, ti)
                tv4 = tv.rearrange("p (h c) k -> p h c k", c=2)
                tif4 = tif.rearrange("p (h c) k -> p h c k", c=2)
                v.tensor_copy(tif, ti)
                wide = [P, HEADS, TOPK, TOPK]
                link(v.tensor_tensor(cand, tv4[:, :, 0, :].unsqueeze(3).to_broadcast(wide),
                                     tv4[:, :, 1, :].unsqueeze(2).to_broadcast(wide), ALU.add))
                top16(HEADS, lambda i: candf[:, i, :], bv, bj)
                v.tensor_tensor(three(sm[0], HEADS), bv, bv[:, :, 0:1].to_broadcast([P, HEADS, TOPK]),
                                ALU.subtract).then_inc(bd_ok, 1)
                v.tensor_scalar(sm[2].bitcast(U32), bj.rearrange("p h k -> p (h k)"), 4, None,
                                ALU.logical_shift_right)
                link(v.tensor_scalar(sm[3].bitcast(U32), bj.rearrange("p h k -> p (h k)"), 15, None,
                                     ALU.bitwise_and))
                v.tensor_copy(sm[4], sm[2].bitcast(U32))
                link(v.tensor_copy(sm[5], sm[3].bitcast(U32)))
                for c in range(2):
                    hot3 = hot.rearrange("p h k i -> p (h k) i")
                    link(v.tensor_tensor(hot3, row(sm[4 + c], TOPK), mid(count16[:, :], PICKS), ALU.is_equal))
                    link(v.tensor_tensor(hot, hot, tif4[:, :, c, :].unsqueeze(2).to_broadcast(wide), ALU.mult))
                    link(v.tensor_reduce(sm[6 + c], hot3, AX_X, ALU.add))
                v.scalar_tensor_tensor(eidx[:, t % 2, :], sm[6], float(KEYS), sm[7], ALU.mult, ALU.add)
                dve.wait_ge(be_ok, t + 1)
                link(v.tensor_reduce(stat[:, 48:56], three(sm[1], HEADS), AX_X, ALU.add))
                link(v.reciprocal(stat[:, 48:56], stat[:, 48:56]))
                v.tensor_tensor(three(gate[:, t % 2, :], HEADS), three(sm[1], HEADS), row(stat[:, 48:56], TOPK),
                                ALU.mult).then_inc(picks_ok, 1)

            def experts(t, lo, hi):
                if lo == 0:
                    if t >= 1:
                        dve.wait_ge(sq_f, t)
                    v.tensor_copy(xps[:, :], xn2[:, t % 2, :]).then_inc(xps_ok, 1)
                    dve.wait_ge(xps_ok, t + 1)
                with dve.Fori(lo, hi) as r:
                    j = r + t * ROUNDS
                    for s in range(SLOTS):
                        dve.wait_ge(rows_in[s], j * 16 + 16)
                        last = v.tensor_tensor_reduce(rows[:, s, 0:D_MODEL], rows[:, s, 0:D_MODEL], xps[:, :],
                                                      1.0, 0.0, ALU.mult, ALU.add, dots[:, s:s + 1])
                        if s % GROUP == GROUP - 1:
                            last.then_inc(dot_ok, 1)
                if hi == ROUNDS:
                    dve.wait_ge(sq_f, t + 1)
                    v.tensor_scalar(stat[:, 37:38], stat[:, 36:37], 1.0 / D_MODEL, EPS, ALU.mult, ALU.add
                                    ).then_inc(ms_f, 1)
                    dve.wait_ge(root_f, t + 1)
                    link(v.reciprocal(stat[:, 39:40], stat[:, 38:39]))
                    v.scalar_tensor_tensor(hbuf[:, t % 2, :], acc[:, :], stat[:, 39:40], lnf[:, :],
                                           ALU.mult, ALU.mult).then_inc(y_done, 1)

            for t in range(TILES + 1):
                done = 0
                for part in range(PARTS):
                    if t < TILES:
                        if part == 0:
                            retention(t)
                        elif part == 1:
                            latent(t)
                            maxima(t, 0)
                        elif part < 10:
                            u = part - 2
                            if u + 1 < HEADS:
                                maxima(t, u + 1)
                            normalise(t, u)
                        elif part == 10:
                            project(t)
                        elif part == 12:
                            route(t)
                    if t >= 1:
                        experts(t - 1, done, done + SLICES[part])
                        done += SLICES[part]


def kernel(**inputs):
    import concourse.bacc as _bacc
    from concourse.bass_utils import run_bass_kernel_spmd as _run

    x = {k: np.asarray(v) for k, v in inputs.items()}
    con = np.ascontiguousarray
    arrays = dict(tables())

    def spread(w):
        return con(np.broadcast_to(w.reshape(1, -1), (P, w.size)))

    x_all = np.concatenate([x["x_prompt"][0], x["x_sample"].reshape(P, D_MODEL)], axis=0)
    cache = x["cache_mla_ckv"][0]
    arrays.update(
        x_all=x_all,
        x_t=con(x_all.T.reshape(KD, P, TILES * P).transpose(1, 0, 2)),
        ln1=con(x["ln1_w"][0].reshape(KD, P).T),
        w_in=con(x["w_in"][0]),
        gn=spread(x["ret_gn_w"][0]), qn=spread(x["mla_q_norm_w"][0]), kvn=spread(x["mla_kv_norm_w"][0]),
        ln2=spread(x["ln2_w"][0]), lnf=spread(x["lnf_w"]),
        w_uq=con(x["mla_w_uq"][0].reshape(RANK, HEADS * QD)),
        w_ukt=con(x["mla_w_uk"][0].transpose(2, 1, 0)),
        w_uv=con(x["mla_w_uv"][0].reshape(RANK, HEADS * HD)),
        w_o=con(x["w_o"][0]),
        w_q=con(x["peer_w_q"][0].reshape(KD, P, HP, P).transpose(2, 1, 0, 3).reshape(HP, P, D_MODEL)),
        subk=con(x["peer_sub_keys"][0].reshape(HP, KEYS, P).transpose(2, 0, 1)),
        uv=np.concatenate([x["peer_u"][0], x["peer_v"][0]], axis=1),
        cache=con(cache),
        cache_t=con(cache.transpose(0, 2, 1).reshape(DEC_BATCH, 2, P, PAST).transpose(0, 2, 1, 3)),
        cache_rt=con(x["cache_mla_krope"][0].transpose(0, 2, 1)),
        state=con(x["state_retention"][0]),
    )
    outputs = dict(y_prompt=(SEQ, D_MODEL), y_sample=(P, D_MODEL), ckv_p=(SEQ, RANK), kr_p=(SEQ, ROPE),
                   state_p=(HD, HEADS, HD), ckv_s=(P, RANK), kr_s=(P, ROPE),
                   state_s=(DEC_BATCH, HEADS, HD, HD))

    nc = _bacc.Bacc("TRN2", target_bir_lowering=False, num_devices=1)
    ins = {k: nc.dram_tensor(f"in_{k}", v.shape, F32, kind="ExternalInput").ap() for k, v in arrays.items()}
    outs = {k: nc.dram_tensor(f"out_{k}", s, F32, kind="ExternalOutput").ap() for k, s in outputs.items()}
    build(nc, ins, outs)
    got = _run(nc, [{f"in_{k}": v for k, v in arrays.items()}], core_ids=[0]).results[0]
    g = {k: got[f"out_{k}"] for k in outputs}
    return (g["y_prompt"].reshape(1, SEQ, D_MODEL),
            g["y_sample"].reshape(DEC_BATCH, DEC_SEQ, D_MODEL),
            g["ckv_p"].reshape(1, 1, SEQ, RANK),
            g["kr_p"].reshape(1, 1, SEQ, ROPE),
            con(g["state_p"].transpose(1, 0, 2)).reshape(1, 1, HEADS, HD, HD),
            g["ckv_s"].reshape(1, DEC_BATCH, DEC_SEQ, RANK),
            g["kr_s"].reshape(1, DEC_BATCH, DEC_SEQ, ROPE),
            g["state_s"].reshape(1, DEC_BATCH, HEADS, HD, HD))
```

```python
from contextlib import ExitStack

import numpy as np

import concourse.bass as bass
from concourse import mybir

F32 = mybir.dt.float32
U32 = mybir.dt.uint32
ALU = mybir.AluOpType
ACT = mybir.ActivationFunctionType
AX_X = mybir.AxisListType.X

P = 128
D_MODEL = 1024
SEQ = 512
DEC_BATCH = 8
DEC_SEQ = 16
PAST = 256
CHUNK = 64
EPS = 1e-6
HEADS = 8
HD = 64
ROPE = 32
RANK = 256
QD = HD + ROPE
IN_COLS = 4 * HEADS * HD + 2 * RANK + ROPE
PROMPT_TILES = SEQ // P
TILES = PROMPT_TILES + 1
SAMPLE = PROMPT_TILES
KD = D_MODEL // P
KEYS = 128
TOPK = 16
EXPERTS = KEYS * KEYS
HP = 2 * HEADS
PICKS = HEADS * TOPK
SLOTS = 8
ROUNDS = PICKS // SLOTS
GROUP = 2
GROUPS = SLOTS // GROUP
SCALE = float(QD) ** -0.5
OFF_Q, OFF_K, OFF_V, OFF_G = 0, 512, 1024, 1536
OFF_CQ, OFF_CKV, OFF_KPE = 2048, 2304, 2560
MASKED = -1e30
LOWEST = -3.0e38

STEPS = ([("rotate", 0, 1), ("turn_qk", 0, 1), ("ret_scores", 0, 1), ("ret_sums", 0, 2), ("ret_norm", 0, 1),
          ("silu", 0, 1), ("stats", 0, 1), ("latents", 0, 1), ("turn_c", 0, 2), ("q_rope", 0, 1),
          ("q_nope", 0, 1), ("q_lat", 0, 1), ("q_lat", 1, 1)]
         + [("attend", i, 1) for i in range(HEADS + 3)]
         + [("values_up", 0, 2), ("turn_mix", 0, 2)]
         + [("w_o", i, 1) for i in range(4)]
         + [("residual", 0, 1), ("norm2", 0, 1), ("turn_x2", 0, 2)]
         + [("query", i, 1) for i in range(HEADS + 2)]
         + [("pairs", 0, 1)] + [("best", i, 1) for i in range(4)]
         + [("places", 0, 1), ("picks", 0, 1), ("picks", 1, 1), ("gates", 0, 1)])
UNITS = PICKS // GROUP
LAST_UNITS = UNITS - sum(n for _, _, n in STEPS)
assert LAST_UNITS >= 0
def log_decay():
    return np.log1p(-np.exp2(-5.0 - np.arange(HEADS)))


def tables():
    pos = np.concatenate([np.arange(SEQ), PAST + np.tile(np.arange(DEC_SEQ), DEC_BATCH)]).astype(np.float32)

    def angles(half):
        inv = (np.float32(10000.0) ** (-np.arange(half, dtype=np.float32) / half)).astype(np.float32)
        a = (pos[:, None] * inv[None, :]).astype(np.float32).astype(np.float64)
        lay = lambda m: np.ascontiguousarray(m.astype(np.float32).reshape(TILES, P, half).transpose(1, 0, 2))
        return lay(np.cos(a)), lay(np.sin(a))

    lg = log_decay()
    k_scale = HD ** -0.5
    i = np.arange(P)
    gap = np.abs(i[:, None] - i[None, :])
    seen = (i[:, None] // CHUNK) <= (i[None, :] // CHUNK)
    same = (i[:, None] // DEC_SEQ) == (i[None, :] // DEC_SEQ)
    decay = np.exp(lg[None, :, None] * gap[:, None, :]) * k_scale
    d_prompt = decay * seen[:, None, :]
    d_sample = decay * same[:, None, :]
    s = i % DEC_SEQ
    own = (i[:, None] // DEC_SEQ == np.arange(DEC_BATCH)[None, :]).astype(np.float64)
    q_prompt = np.exp(lg[None, :] * (i[:, None] + 1.0))
    q_sample = np.exp(lg[None, :] * (s[:, None] + 1.0))[:, :, None] * own[:, None, :]
    k_prompt = np.exp(lg[None, :] * (P - 1.0 - i[:, None])) * k_scale
    k_sample = np.exp(lg[None, :] * (DEC_SEQ - 1.0 - s[:, None])) * k_scale
    cos64, sin64 = angles(HD // 2)
    cos32, sin32 = angles(ROPE // 2)
    out = dict(cos64=cos64, sin64=sin64, cos32=cos32, sin32=sin32, d_prompt=d_prompt, d_sample=d_sample,
               q_prompt=q_prompt, q_sample=q_sample, k_prompt=k_prompt, k_sample=k_sample, own=own,
               s_decay=np.tile(np.exp(lg * P)[None, :], (HD, 1)), ident=np.eye(P),
               count16=np.tile(np.arange(TOPK)[None, :], (P, 1)))
    return {k: np.ascontiguousarray(v.astype(np.float32)) for k, v in out.items()}


def build(nc, a, out):
    g_sample = [float(np.exp(v * DEC_SEQ)) for v in log_decay()]
    ctx = ExitStack()
    with ctx:
        def sb(name, shape, dt=F32):
            return ctx.enter_context(nc.sbuf_tensor(name, shape, dt))

        def sem(name):
            return ctx.enter_context(nc.semaphore(name))

        proj_d = nc.dram_tensor("proj_d", (TILES, P, IN_COLS), F32, kind="Internal").ap()

        rows = sb("rows", [P, SLOTS, 2 * D_MODEL])
        WB = 3
        wblk = sb("wblk", [P, WB, D_MODEL])
        PJ, MIX, R = 0, 3104, 4128
        work = sb("work", [P, R + 9216])
        w_uq = sb("w_uq", [P, 2, HEADS * QD])
        w_ukt = sb("w_ukt", [HD, HEADS, RANK])
        w_uv = sb("w_uv", [P, 2, HEADS * HD])
        subk = sb("subk", [P, HP, KEYS])
        dmask = sb("dmask", [P, HEADS, P])
        cos64 = sb("cos64", [P, TILES, HD // 2])
        sin64 = sb("sin64", [P, TILES, HD // 2])
        cos32 = sb("cos32", [P, TILES, ROPE // 2])
        sin32 = sb("sin32", [P, TILES, ROPE // 2])
        q_prompt = sb("q_prompt", [P, HEADS])
        q_sample = sb("q_sample", [P, HEADS, DEC_BATCH])
        k_prompt = sb("k_prompt", [P, HEADS])
        k_sample = sb("k_sample", [P, HEADS])
        own = sb("own", [P, DEC_BATCH])
        s_decay = sb("s_decay", [HD, HEADS])
        count16 = sb("count16", [P, TOPK])
        ident = sb("ident", [P, P])
        ln1 = sb("ln1", [P, KD])
        ln2 = sb("ln2", [P, D_MODEL])
        lnf = sb("lnf", [P, D_MODEL])
        gnw = sb("gnw", [P, HEADS * HD])
        qnw = sb("qnw", [P, RANK])
        kvw = sb("kvw", [P, RANK])
        keys_all = sb("keys_all", [P, 2560])
        ckv = keys_all[:, 0:1024].rearrange("p (t c) -> p t c", t=PROMPT_TILES)
        ckvt = keys_all[:, 1024:2048].rearrange("p (k n) -> p k n", k=2)
        krt = keys_all[0:ROPE, 2048:2560]
        st_in = [keys_all[0:HD, 512 * i:512 * i + 512].rearrange("p (b e) -> p b e", b=DEC_BATCH) for i in range(2)]
        st_out = [keys_all[0:HD, 1024 + 512 * i:1536 + 512 * i].rearrange("p (b e) -> p b e", b=DEC_BATCH)
                  for i in range(2)]
        state = sb("state", [HD, HEADS, HD])
        hbuf = sb("hbuf", [P, 2, D_MODEL])
        xn2 = sb("xn2", [P, 2, D_MODEL])
        eidx = sb("eidx", [P, 2, PICKS], U32)
        gate = sb("gate", [P, 2, PICKS])
        cur = sb("cur", [P, 2, SLOTS], U32)
        DR = 4
        diag = sb("diag", [P, DR, P])
        dots = sb("dots", [P, SLOTS])
        gel = sb("gel", [P, SLOTS])
        wgt = sb("wgt", [P, SLOTS])
        ssq1 = sb("ssq1", [P, TILES])
        rstd1 = sb("rstd1", [P, TILES])
        stat = sb("stat", [P, 64])

        def wv(lo, n, parts=P, dt=None):
            return work[0:parts, lo:lo + n]

        def three(ap, k):
            return ap.rearrange("p (k n) -> p k n", k=k)

        flat_rows = rows[:, :, :].rearrange("p s n -> p (s n)")
        xt = three(flat_rows[:, 0:TILES * D_MODEL], KD)
        win = [three(flat_rows[:, 5120 + 4096 * i:9216 + 4096 * i], KD) for i in range(2)]
        stage = three(flat_rows[:, 13312:13312 + 4 * 512], 4)
        xs = three(wv(R, TILES * D_MODEL), TILES)
        sq_junk = wv(R + TILES * D_MODEL, D_MODEL)
        pj = wv(PJ, IN_COLS)
        mix = wv(MIX, D_MODEL)
        qk = wv(R, 1024)
        rtmp = wv(R + 1024, 1024)
        q_t = three(wv(R + 2048, 1024, HD), HEADS)
        k_t = three(wv(R + 3072, 1024, HD), HEADS)
        s_td = [three(wv(R + 4096 + 512 * i, 512), 4) for i in range(2)]
        kdec = wv(R + 5120, 512)
        ret_o = wv(R + 5632, 512)
        osq = wv(R + 6144, 512)
        vmask = [three(wv(R + 6656 + 512 * i, 512), DEC_BATCH) for i in range(2)]
        ost = [three(wv(R + 7680, 512), DEC_BATCH)] * 2
        sgm = wv(R + 8192, 512)
        cqn = wv(R, 256)
        ckvn_s = wv(R + 256, 256)
        cq_t = three(wv(R + 512, 256), 2)
        ckvt_s = three(wv(R + 768, 256), 2)
        krt_s = wv(R + 1024, 128, ROPE)
        qpe = wv(R + 1152, 256)
        ptmp = wv(R + 1408, 256)
        kpe = wv(R + 1664, ROPE)
        ktmp = wv(R + 1696, ROPE)
        qpe_t = three(wv(R + 1728, 1024, ROPE), HEADS)
        qn_t = three(wv(R + 2752, 1024, HD), HEADS)
        prob = [wv(R + 2752 + 512 * i, 512) for i in range(2)]
        qlat = wv(R + 3776, 2048).rearrange("p (k h n) -> p k h n", k=2, h=HEADS)
        qlat_s = wv(R + 3776, 2048).rearrange("p (k b m) -> p k b m", k=2, b=DEC_BATCH)
        prob_t = [wv(R + 5824 + 512 * i, 512) for i in range(2)]
        olat = wv(R + 6848, 2048).rearrange("p (k h n) -> p k h n", k=2, h=HEADS)
        mix_t = three(wv(R + 1728, 1024), KD)
        ca_t = [three(wv(PJ + 1536 * i, 512), 2) for i in range(2)]
        ca = [three(wv(PJ + 1536 * i + 512, 512), 2) for i in range(2)]
        ca_r = [wv(PJ + 1536 * i + 1024, 256, ROPE) for i in range(2)]
        ca_n = [wv(PJ + 1536 * i + 1280, 256, DEC_SEQ) for i in range(2)]
        x2_t = three(wv(R, 1024), KD)
        pq_t = three(wv(R + 1024, 2048), HP)
        sc = three(wv(R + 3072, 2048), HP)
        cand = wv(R + 5120, 2048).rearrange("p (h i j) -> p h i j", h=HEADS, i=TOPK)
        candf = three(wv(R + 5120, 2048), HEADS)
        hot = wv(R + 7168, 2048).rearrange("p (h k i) -> p h k i", h=HEADS, k=TOPK)
        tv = three(wv(MIX, 256), HP)
        ti = three(wv(MIX + 256, 256).bitcast(U32), HP)
        tif = three(wv(MIX + 512, 256), HP)
        bv = three(wv(MIX + 768, 128), HEADS)
        bj = three(wv(MIX + 896, 128).bitcast(U32), HEADS)
        sm = [wv(R + 128 * i, 128) for i in range(8)]

        F = [ctx.enter_context(nc.psum_tensor(f"F{i}", [P, 512], F32)) for i in range(4)]
        acc = ctx.enter_context(nc.psum_tensor("acc", [P, D_MODEL], F32))
        xps = ctx.enter_context(nc.psum_tensor("xps", [P, D_MODEL], F32))

        def f4(i, parts=P):
            return F[i][0:parts, :].rearrange("p (k n) -> p k n", k=4)

        def f8(i, parts=P):
            return F[i][0:parts, :].rearrange("p (k n) -> p k n", k=8)

        xt_in, xs_in, consts_in, small_in = (sem("xt0_in"), sem("xt_in")), sem("xs_in"), sem("consts_in"), sem("small_in")
        win_in = [sem(f"win_in{i}") for i in range(2)]
        stored = [sem(f"stored{i}") for i in range(4)]
        pj_in, xres_in, wblk_in = sem("pj_in"), sem("xres_in"), [sem(f"wblk_in{i}") for i in range(WB)]
        dmask_in = sem("dmask_in")
        st_landed = [sem(f"st_landed{i}") for i in range(2)]
        st_stored = [sem(f"st_stored{i}") for i in range(2)]
        keys_in = [sem(f"keys_in{i}") for i in range(2)]
        values_in = [sem(f"values_in{i}") for i in range(2)]
        outs_done = sem("outs_done")
        new_ckv_out = sem("new_ckv_out")
        y_out = sem("y_out")
        sq_done, ms1, root1, rstd1_ok = sem("sq_done"), sem("ms1"), sem("root1"), sem("rstd1_ok")
        xt_ok, mm_in, ev_in = sem("xt_ok"), sem("mm_in"), sem("ev_in")
        dve_step, act_step = sem("dve_step"), sem("act_step")
        qk_ok, tr_qk, ev_qk = sem("qk_ok"), sem("tr_qk"), sem("ev_qk")
        mm_s, ev_s, mm_oi, mm_os, mm_up = sem("mm_s"), sem("ev_s"), sem("mm_oi"), sem("mm_os"), sem("mm_up")
        mm_ss, ev_ss, mm_su, ev_su, vm_ok = sem("mm_ss"), sem("ev_ss"), sem("mm_su"), sem("ev_su"), sem("vm_ok")
        kd_ok, state_ok = sem("kd_ok"), sem("state_ok")
        ms_gn, root_gn, eg_ok = sem("ms_gn"), sem("root_gn"), sem("eg_ok")
        y_ok = sem("y_ok")
        ms_c, root_c, c_ok, kpe_ok = sem("ms_c"), sem("root_c"), sem("c_ok"), sem("kpe_ok")
        tr_c, ev_c, mm_pe, qpe_ok = sem("tr_c"), sem("ev_c"), sem("mm_pe"), sem("qpe_ok")
        mm_qn, ev_qn, tr_pe, ev_pe, mm_ql, ev_ql = (sem("mm_qn"), sem("ev_qn"), sem("tr_pe"), sem("ev_pe"),
                                                    sem("mm_ql"), sem("ev_ql"))
        mm_sc, nm_ok, exp_ok, p_ok = sem("mm_sc"), sem("nm_ok"), sem("exp_ok"), sem("p_ok")
        tr_p, ev_pt, mm_pv, ev_pv = sem("tr_p"), sem("ev_pt"), sem("mm_pv"), sem("ev_pv")
        mm_mo, ev_mo, tr_mix, ev_mix, mm_wo, h_ok = (sem("mm_mo"), sem("ev_mo"), sem("tr_mix"), sem("ev_mix"),
                                                     sem("mm_wo"), sem("h_ok"))
        wblk_used = sem("wblk_used")
        ms_2, root_2, x2_ok, tr_x2, ev_x2 = sem("ms_2"), sem("root_2"), sem("x2_ok"), sem("tr_x2"), sem("ev_x2")
        ev_pq, mm_ps, ev_ps = sem("ev_pq"), sem("mm_ps"), sem("ev_ps")
        bd_ok, be_ok, picks_ok = sem("bd_ok"), sem("be_ok"), sem("picks_ok")
        idx_here, rows_free = sem("idx_here"), sem("rows_free")
        rows_in = [sem(f"rows_in{i}") for i in range(SLOTS)]
        xps_ok, dot_ok, gel_ok, wgt_ok, diag_ok = (sem("xps_ok"), sem("dot_ok"), sem("gel_ok"), sem("wgt_ok"),
                                                   sem("diag_ok"))
        sq_f, ms_f, root_f, y_done = sem("sq_f"), sem("ms_f"), sem("root_f"), sem("y_done")

        items = [(cb, 0) for cb in range(6)] + [(cb, t) for cb in range(6) for t in range(1, TILES)]
        NIN = len(items)
        banks = [acc[:, 0:512], acc[:, 512:1024], xps[:, 0:512], xps[:, 512:1024]]
        width = [512] * 5 + [ROPE]
        N_SMALL = 7

        stores = [16 * len(range(6 + (i - 6) % 4, NIN, 4)) for i in range(4)]

        def nkeys(t):
            return P * (t + 1) if t < SAMPLE else PAST + DEC_SEQ

        def pieces(t):
            return [(P * j, min(P, nkeys(t) - P * j)) for j in range((nkeys(t) + P - 1) // P)]

        block = ctx.enter_context(nc.Block())

        @block.sync
        def _(sp):
            sp.dma_start(xt[:, :, 0:P], a["x_t"][:, :, 0:P]).then_inc(xt_in[0], 16)
            sp.dma_start(ln1[:, :], a["ln1"]).then_inc(xt_in[0], 16)
            sp.dma_start(xs, a["x_all"].rearrange("(t p) d -> p t d", p=P)).then_inc(xs_in, 16)
            for dst, name in ((cos64, "cos64"), (sin64, "sin64"), (cos32, "cos32"), (sin32, "sin32"),
                              (q_sample, "q_sample"), (dmask, "d_prompt")):
                sp.dma_start(dst[:, :, :], a[name]).then_inc(consts_in, 16)
            for dst, name in ((q_prompt, "q_prompt"), (k_prompt, "k_prompt"), (k_sample, "k_sample"), (own, "own"),
                              (s_decay, "s_decay"), (count16, "count16"), (ident, "ident"), (gnw, "gn"),
                              (qnw, "qn"), (kvw, "kvn"), (ln2, "ln2"), (lnf, "lnf")):
                sp.dma_start(dst[:, :], a[name]).then_inc(consts_in, 16)
            sp.dma_start(xt[:, :, P:], a["x_t"][:, :, P:]).then_inc(xt_in[1], 16)
            sp.dma_start(w_uq[:, :, :], a["w_uq"].rearrange("(k p) n -> p k n", p=P)).then_inc(small_in, 16)
            sp.dma_start(w_ukt[:, :, :], a["w_ukt"]).then_inc(small_in, 16)
            sp.dma_start(w_uv[:, :, :], a["w_uv"].rearrange("(k p) n -> p k n", p=P)).then_inc(small_in, 16)
            sp.dma_start(subk[:, :, :], a["subk"]).then_inc(small_in, 16)

            def store_y(t):
                sp.wait_ge(y_done, t + 1)
                dst = out["y_prompt"][P * t:P * t + P, :] if t < SAMPLE else out["y_sample"]
                sp.dma_start(dst, hbuf[:, t % 2, :]).then_inc(y_out, 16)

            for t in range(TILES):
                if t == SAMPLE:
                    sp.wait_ge(state_ok, SAMPLE)
                    sp.dma_start(out["state_p"], state[:, :, :]).then_inc(outs_done, 16)
                    sp.wait_ge(ev_pv, SAMPLE * HEADS)
                    for h in range(HEADS):
                        if h >= 2:
                            sp.wait_ge(ev_su, h - 1)
                        sp.dma_start(st_in[h % 2], a["state"][:, h].rearrange("b d e -> d b e")
                                     ).then_inc(st_landed[h % 2], 16)
                        if h >= 1:
                            sp.wait_ge(ev_su, h)
                            sp.dma_start(out["state_s"][:, h - 1].rearrange("b d e -> d b e"), st_out[(h - 1) % 2]
                                         ).then_inc(st_stored[(h - 1) % 2], 16)
                    sp.wait_ge(ev_su, HEADS)
                    sp.dma_start(out["state_s"][:, HEADS - 1].rearrange("b d e -> d b e"), st_out[(HEADS - 1) % 2]
                                 ).then_inc(st_stored[(HEADS - 1) % 2], 16)
                sp.wait_ge(c_ok, t + 1)
                if t < SAMPLE:
                    sp.dma_start(out["ckv_p"][P * t:P * t + P, :], ckv[:, t, :]).then_inc(outs_done, 16)
                else:
                    sp.dma_start(out["ckv_s"], ckvn_s).then_inc(new_ckv_out, 16)
                sp.wait_ge(kpe_ok, t + 1)
                dst = out["kr_p"][P * t:P * t + P, :] if t < SAMPLE else out["kr_s"]
                sp.dma_start(dst, kpe).then_inc(outs_done, 16)
                if t >= 2:
                    store_y(t - 2)
                    sp.wait_ge(y_out, 16 * (t - 1))
                sp.dma_start(hbuf[:, t % 2, :], a["x_all"][P * t:P * t + P, :]).then_inc(xres_in, 16)
                if 1 <= t < SAMPLE:
                    sp.dma_start(pj, proj_d[t + 1]).then_inc(pj_in, 16)
                if t == SAMPLE - 1:
                    sp.wait_ge(ev_s, 2 * SAMPLE)
                    sp.dma_start(dmask[:, :, :], a["d_sample"]).then_inc(dmask_in, 16)
                if t == SAMPLE:
                    sp.wait_ge(new_ckv_out, 16)
                    for b in range(DEC_BATCH + 2):
                        if b < DEC_BATCH:
                            if b >= 2:
                                sp.wait_ge(mm_sc, SAMPLE * HEADS + b - 1)
                            s = keys_in[b % 2]
                            sp.dma_start(ca_t[b % 2], a["cache_t"][b]).then_inc(s, 16)
                            sp.dma_start(ca_r[b % 2], a["cache_rt"][b]).then_inc(s, 16)
                        if b >= 2:
                            c = b - 2
                            if c >= 2:
                                sp.wait_ge(mm_pv, SAMPLE * HEADS + c - 1)
                            s = values_in[c % 2]
                            sp.dma_start(ca[c % 2], a["cache"][c].rearrange("(k p) c -> p k c", p=P)
                                         ).then_inc(s, 16)
                            sp.dma_start(ca_n[c % 2], out["ckv_s"][DEC_SEQ * c:DEC_SEQ * c + DEC_SEQ, :]
                                         ).then_inc(s, 16)
                for i in range(KD + HP):
                    n = t * (KD + HP) + i
                    if n >= WB:
                        sp.wait_ge(wblk_used, n - WB + 1)
                    src = a["w_o"][P * i:P * i + P, :] if i < KD else a["w_q"][i - KD]
                    sp.dma_start(wblk[:, n % WB, :], src).then_inc(wblk_in[n % WB], 16)
                if t == 0:
                    for i in range(4):
                        sp.wait_ge(stored[i], stores[i])
                    sp.dma_start(pj, proj_d[1]).then_inc(pj_in, 16)
            store_y(SAMPLE - 1)
            store_y(SAMPLE)
            sp.wait_ge(y_out, 16 * TILES)
            sp.wait_ge(outs_done, 16 * (1 + SAMPLE + TILES))
            for i in range(2):
                sp.wait_ge(st_stored[i], 16 * HEADS // 2)

        @block.gpsimd
        def _(pool):
            for n in range(12):
                cb = n % 6
                if n >= 2:
                    pool.wait_ge(mm_in, n - 1 if n <= 7 else 6 + SAMPLE * (n - 7))
                pool.dma_start(win[n % 2][:, :, 0:width[cb]],
                               a["w_in"][:, 512 * cb:512 * cb + width[cb]].rearrange("(k p) n -> p k n", p=P)
                               ).then_inc(win_in[n % 2], 16)
            pool.wait_ge(mm_in, NIN)
            for i in range(4):
                pool.wait_ge(stored[i], stores[i])
            for t in range(TILES):
                pool.wait_ge(picks_ok, t + 1)
                with pool.Fori(0, ROUNDS // 2) as r2:
                    for half in range(2):
                        j = r2 * 2 + (t * ROUNDS + half)
                        pool.wait_ge(rows_free, j * SLOTS + 1)
                        pool.nop(nofuse=True)
                        nc.gpsimd.tensor_copy(cur[:, half, :], eidx[:, t % 2, bass.ds(r2 * (2 * SLOTS) + half * SLOTS, SLOTS)]
                                              ).then_inc(idx_here, 1)
                        pool.wait_ge(idx_here, j + 1)
                        for s in range(SLOTS):
                            pool.wait_ge(rows_free, j * SLOTS + s + 1)
                            pool.nop(nofuse=True)
                            nc.gpsimd.indirect_dma_start(
                                rows[:, s, :], None, a["uv"], bass.IndirectOffsetOnAxis(cur[:, half, s:s + 1], 0)
                            ).then_inc(rows_in[s], 16)

        @block.tensor
        def _(pe):
            mm, tr = nc.tensor.matmul, nc.tensor.transpose

            def project_in(n):
                cb, t = items[n]
                load = cb if n < 6 else 6 + cb
                if t <= 1:
                    pe.wait_ge(win_in[load % 2], 16 * (load // 2 + 1))
                pe.wait_ge(xt_ok, KD if t == 0 else 2 * KD)
                if n >= 4:
                    pe.wait_ge(ev_in, n - 3)
                for k in range(KD):
                    last = mm(banks[n % 4][:, 0:width[cb]], xt[:, k, P * t:P * t + P],
                              win[load % 2][:, k, 0:width[cb]], start=(k == 0), stop=(k == KD - 1))
                last.then_inc(mm_in, 1)

            for n in range(6):
                project_in(n)
            pe.wait_ge(consts_in, 16 * 18)
            pe.wait_ge(small_in, 16 * 4)

            def turn_qk(t):
                pe.wait_ge(qk_ok, t + 1)
                for g in range(4):
                    dst = f4(g, HD)
                    for i in range(4):
                        last = tr(dst[:, i, :], qk[:, HD * (4 * g + i):HD * (4 * g + i + 1)], ident[:, :])
                    last.then_inc(tr_qk, 1)

            def ret_scores(t):
                pe.wait_ge(ev_qk, 4 * (t + 1))
                for g in range(2):
                    for i in range(4):
                        h = 4 * g + i
                        last = mm(f4(g)[:, i, :], k_t[:, h, :], q_t[:, h, :], start=True, stop=True)
                    last.then_inc(mm_s, 1)

            def ret_sums(t):
                v = pj[:, OFF_V:OFF_V + 512]
                for g in range(2):
                    pe.wait_ge(ev_s, 2 * t + g + 1)
                    for i in range(4):
                        h = 4 * g + i
                        last = mm(f8(2)[:, h, :], s_td[g][:, i, :], v[:, HD * h:HD * h + HD], start=True, stop=True)
                last.then_inc(mm_oi, 1)
                pe.wait_ge(kd_ok, t + 1)
                if t < SAMPLE:
                    if t >= 1:
                        pe.wait_ge(state_ok, t)
                        for h in range(HEADS):
                            last = mm(f8(3)[:, h, :], q_t[:, h, :], state[:, h, :], start=True, stop=True)
                        last.then_inc(mm_os, 1)
                    for h in range(HEADS):
                        last = mm(f8(0, HD)[:, h, :], kdec[:, HD * h:HD * h + HD], v[:, HD * h:HD * h + HD],
                                  start=True, stop=True)
                    last.then_inc(mm_up, 1)
                else:
                    for h in range(HEADS):
                        if h >= 2:
                            pe.wait_ge(ev_ss, h - 1)
                        pe.wait_ge(st_landed[h % 2], 16 * (h // 2 + 1))
                        mm(F[h % 2][:, :], q_t[:, h, :], st_in[h % 2].rearrange("p b e -> p (b e)"),
                           start=True, stop=True).then_inc(mm_ss, 1)
                        if h >= 1:
                            pe.wait_ge(ev_su, h)
                        pe.wait_ge(vm_ok, h + 1)
                        mm(F[3][0:HD, :], kdec[:, HD * h:HD * h + HD], vmask[h % 2].rearrange("p b e -> p (b e)"),
                           start=True, stop=True).then_inc(mm_su, 1)

            w4 = w_uq[:, :, :].rearrange("p k (h d) -> p k h d", h=HEADS)

            def turn_c(t):
                kv_new = ckv[:, t, :] if t < SAMPLE else ckvn_s
                pe.wait_ge(c_ok, t + 1)
                pe.wait_ge(kpe_ok, t + 1)
                for k in range(2):
                    tr(f4(2)[:, k, :], cqn[:, P * k:P * k + P], ident[:, :])
                    tr(f4(2)[:, 2 + k, :], kv_new[:, P * k:P * k + P], ident[:, :])
                tr(F[3][0:ROPE, 0:P], kpe, ident[:, :]).then_inc(tr_c, 1)

            def q_rope(t):
                pe.wait_ge(ev_c, t + 1)
                for k in range(2):
                    last = mm(F[0][:, 0:256], cq_t[:, k, :], w4[:, k, :, HD:QD], start=(k == 0), stop=(k == 1))
                last.then_inc(mm_pe, 1)

            def q_nope(t):
                for g in range(2):
                    for i in range(4):
                        for k in range(2):
                            last = mm(f4(1 + g, HD)[:, i, :], w4[:, k, 4 * g + i, 0:HD], cq_t[:, k, :],
                                      start=(k == 0), stop=(k == 1))
                    last.then_inc(mm_qn, 1)

            def q_lat(t, k):
                if k == 0:
                    pe.wait_ge(qpe_ok, t + 1)
                    for g, bank in ((0, 3), (1, 0)):
                        for i in range(4):
                            h = 4 * g + i
                            last = tr(f4(bank, ROPE)[:, i, :], qpe[:, ROPE * h:ROPE * h + ROPE], ident[:, :])
                        last.then_inc(tr_pe, 1)
                    pe.wait_ge(ev_qn, 2 * (t + 1))
                else:
                    pe.wait_ge(ev_pe, 2 * (t + 1))
                for g in range(2):
                    bank = ((1, 2), (3, 0))[k][g]
                    for i in range(4):
                        h = 4 * g + i
                        last = mm(f4(bank)[:, i, :], w_ukt[:, h, P * k:P * k + P], qn_t[:, h, :],
                                  start=True, stop=True)
                    last.then_inc(mm_ql, 1)

            def scores(t, u):
                n = t * HEADS + u
                if u == 0:
                    pe.wait_ge(ev_ql, 4 * (t + 1))
                if u >= 2:
                    pe.wait_ge(exp_ok, n - 1)
                nk = nkeys(t)
                dst = F[u % 2]
                if t < SAMPLE:
                    for k in range(2):
                        mm(dst[:, 0:nk], qlat[:, k, u, :], ckvt[:, k, 0:nk], start=(k == 0), stop=False)
                    last = mm(dst[:, 0:nk], qpe_t[:, u, :], krt[:, 0:nk], start=False, stop=True)
                else:
                    pe.wait_ge(keys_in[u % 2], 32 * (u // 2 + 1))
                    cut = slice(DEC_SEQ * u, DEC_SEQ * u + DEC_SEQ)
                    for k in range(2):
                        mm(dst[:, 0:PAST], qlat_s[:, k, u, :], ca_t[u % 2][:, k, :], start=(k == 0), stop=False)
                    mm(dst[:, 0:PAST], qpe_t[:, u, :], ca_r[u % 2], start=False, stop=True)
                    for k in range(2):
                        mm(dst[:, PAST:nk], qlat_s[:, k, u, :], ckvt_s[:, k, cut], start=(k == 0), stop=False)
                    last = mm(dst[:, PAST:nk], qpe_t[:, u, :], krt_s[:, cut], start=False, stop=True)
                last.then_inc(mm_sc, 1)

            def turn_probs(t, u):
                n = t * HEADS + u
                pe.wait_ge(p_ok, n + 1)
                if u >= 1:
                    pe.wait_ge(ev_pt, n)
                for j, (lo, w) in enumerate(pieces(t)):
                    last = tr(F[2][0:w, P * j:P * j + P], prob[u % 2][:, lo:lo + w], ident[:, :])
                last.then_inc(tr_p, 1)

            def values(t, u):
                n = t * HEADS + u
                pe.wait_ge(ev_pt, n + 1)
                if t == SAMPLE:
                    pe.wait_ge(values_in[u % 2], 32 * (u // 2 + 1))
                if u >= 1:
                    pe.wait_ge(ev_pv, n)
                for k in range(2):
                    for j, (lo, w) in enumerate(pieces(t)):
                        if t < SAMPLE:
                            lhs = ckv[:, j, P * k:P * k + P]
                        else:
                            lhs = ca[u % 2][:, j, P * k:P * k + P] if j < 2 else ca_n[u % 2][:, P * k:P * k + P]
                        last = mm(F[3][:, P * k:P * k + P], lhs, prob_t[u % 2][0:w, P * j:P * j + P],
                                  start=(j == 0), stop=(j == len(pieces(t)) - 1))
                last.then_inc(mm_pv, 1)

            def values_up(t):
                pe.wait_ge(ev_pv, HEADS * (t + 1))
                for h in range(HEADS):
                    for k in range(2):
                        last = mm(f8(0)[:, h, :], olat[:, k, h, :], w_uv[:, k, HD * h:HD * h + HD],
                                  start=(k == 0), stop=(k == 1))
                last.then_inc(mm_mo, 1)

            def turn_mix(t):
                pe.wait_ge(y_ok, t + 1)
                for g in range(2):
                    if g == 1:
                        pe.wait_ge(ev_mo, t + 1)
                    for i in range(4):
                        k = 4 * g + i
                        last = tr(f4(1 + g)[:, i, :], mix[:, P * k:P * k + P], ident[:, :])
                    last.then_inc(tr_mix, 1)

            def w_o(t, i):
                if i == 0:
                    pe.wait_ge(ev_mix, 2 * (t + 1))
                for k in (2 * i, 2 * i + 1):
                    n = t * (KD + HP) + k
                    pe.wait_ge(wblk_in[n % WB], 16 * (n // WB + 1))
                    for half, bank in ((0, 3), (1, 0)):
                        last = mm(F[bank][:, :], mix_t[:, k, :], wblk[:, n % WB, 512 * half:512 * half + 512],
                                  start=(k == 0), stop=(k == KD - 1), skip_group_check=True)
                    last.then_inc(wblk_used, 1)

            def turn_x2(t):
                pe.wait_ge(x2_ok, t + 1)
                for g in range(2):
                    for i in range(4):
                        k = 4 * g + i
                        last = tr(f4(1 + g)[:, i, :], xn2[:, t % 2, P * k:P * k + P], ident[:, :])
                    last.then_inc(tr_x2, 1)

            def query(t, i):
                if i == 0:
                    pe.wait_ge(ev_x2, 2 * (t + 1))
                g = i // 2
                bank = 3 if g % 2 == 0 else 0
                if g >= 2 and i % 2 == 0:
                    pe.wait_ge(ev_pq, 4 * t + g - 1)
                for hp in (2 * i, 2 * i + 1):
                    n = t * (KD + HP) + KD + hp
                    pe.wait_ge(wblk_in[n % WB], 16 * (n // WB + 1))
                    for k in range(KD):
                        last = mm(f4(bank)[:, hp % 4, :], wblk[:, n % WB, P * k:P * k + P], x2_t[:, k, :],
                                  start=(k == 0), stop=(k == KD - 1))
                    last.then_inc(wblk_used, 1)

            def key_scores(t, g):
                pe.wait_ge(ev_pq, 4 * t + g + 1)
                if g >= 2:
                    pe.wait_ge(ev_ps, 4 * t + g - 1)
                for i in range(4):
                    hp = 4 * g + i
                    last = mm(f4(1 + g % 2)[:, i, :], pq_t[:, hp, :], subk[:, hp, :], start=True, stop=True)
                last.then_inc(mm_ps, 1)

            def first_sum(t):
                if t >= 1:
                    pe.wait_ge(y_done, t)
                else:
                    pe.wait_ge(ev_in, NIN)
                for c in range(2):
                    mm(acc[:, 512 * c:512 * c + 512], ident[:, :], hbuf[:, t % 2, 512 * c:512 * c + 512],
                       start=True, stop=False, skip_group_check=True)

            def add_pick(j, s):
                pe.wait_ge(diag_ok, j * SLOTS + s + 1)
                for c in range(2):
                    last = mm(acc[:, 512 * c:512 * c + 512], diag[:, s % DR, :],
                              rows[:, s, D_MODEL + 512 * c:D_MODEL + 512 * c + 512],
                              start=False, stop=False, skip_group_check=True)
                last.then_inc(rows_free, 1)

            def unit(t, n):
                if t == 0:
                    if 6 + n < NIN:
                        project_in(6 + n)
                    return
                if n == 0:
                    first_sum(t - 1)
                for i in range(GROUP):
                    pick = n * GROUP + i
                    add_pick((t - 1) * ROUNDS + pick // SLOTS, pick % SLOTS)

            pe.sem_inc(rows_free, SLOTS)
            for t in range(TILES):
                n = 0
                for step, i, units in STEPS:
                    if step == "turn_qk":
                        turn_qk(t)
                    elif step == "ret_scores":
                        ret_scores(t)
                    elif step == "ret_sums":
                        ret_sums(t)
                    elif step == "turn_c":
                        turn_c(t)
                    elif step == "q_rope":
                        q_rope(t)
                    elif step == "q_nope":
                        q_nope(t)
                    elif step == "q_lat":
                        q_lat(t, i)
                    elif step == "attend":
                        if i < HEADS:
                            scores(t, i)
                        if i >= 3:
                            values(t, i - 3)
                        if 2 <= i < HEADS + 2:
                            turn_probs(t, i - 2)
                    elif step == "values_up":
                        values_up(t)
                    elif step == "turn_mix":
                        turn_mix(t)
                    elif step == "w_o":
                        w_o(t, i)
                    elif step == "turn_x2":
                        turn_x2(t)
                    elif step == "query":
                        if i < HEADS:
                            query(t, i)
                        if i >= 2 and i % 2 == 0:
                            key_scores(t, i // 2 - 1)
                    for _ in range(units):
                        unit(t, n)
                        n += 1
                for _ in range(LAST_UNITS):
                    unit(t, n)
                    n += 1
            first_sum(SAMPLE)
            with pe.Fori(0, ROUNDS) as r:
                for s in range(SLOTS):
                    add_pick(r + SAMPLE * ROUNDS, s)

        @block.scalar
        def _(act):
            copy = nc.scalar.copy
            act.wait_ge(xs_in, 16)
            for t in range(TILES):
                if t >= 1:
                    act.wait_ge(sq_done, t)
                nc.scalar.activation(sq_junk, xs[:, t, :], ACT.Square, accum_out=ssq1[:, t:t + 1]
                                     ).then_inc(sq_done, 1)
            act.wait_ge(ms1, 1)
            nc.scalar.activation(rstd1[:, :], ssq1[:, :], ACT.Sqrt).then_inc(root1, 1)
            act.wait_ge(rstd1_ok, 1)

            def project_in(n):
                cb, t = items[n]
                act.wait_ge(mm_in, n + 1)
                if n >= 10:
                    act.wait_ge(stored[n % 4], 16 * ((n - 6) // 4))
                dst = pj[:, 512 * cb:512 * cb + width[cb]] if t == 0 else stage[:, n % 4, 0:width[cb]]
                nc.scalar.activation(dst, banks[n % 4][:, 0:width[cb]], ACT.Copy, scale=rstd1[:, t:t + 1]
                                     ).then_inc(ev_in, 1)
                if t >= 1:
                    act.wait_ge(ev_in, n + 1)
                    act.dma_start(proj_d[t, :, 512 * cb:512 * cb + width[cb]], dst).then_inc(stored[n % 4], 16)

            for n in range(6):
                project_in(n)

            def turn_qk(t):
                for g in range(4):
                    act.wait_ge(tr_qk, 4 * t + g + 1)
                    dst = (q_t, q_t, k_t, k_t)[g][:, 4 * (g % 2):4 * (g % 2) + 4, :]
                    copy(dst, f4(g, HD)).then_inc(ev_qk, 1)
                nc.scalar.activation(sgm, pj[:, OFF_G:OFF_G + 512], ACT.Exp, scale=-1.0).then_inc(eg_ok, 1)

            def spread_copy(t, dst, g, src):
                if t < SAMPLE:
                    return copy(dst[:, 4 * g:4 * g + 4, :], src)
                by_seq = dst.rearrange("p b (h s) -> p b h s", h=HEADS)[:, :, 4 * g:4 * g + 4, :]
                return copy(by_seq, src.rearrange("p h (b s) -> p b h s", b=DEC_BATCH))

            def turn_c(t):
                act.wait_ge(tr_c, t + 1)
                copy(cq_t, f4(2)[:, 0:2, :])
                kt, rt = (ckvt[:, :, P * t:P * t + P], krt[:, P * t:P * t + P]) if t < SAMPLE else (ckvt_s, krt_s)
                copy(kt, f4(2)[:, 2:4, :])
                copy(rt, F[3][0:ROPE, 0:P]).then_inc(ev_c, 1)

            def q_nope(t):
                for g in range(2):
                    act.wait_ge(mm_qn, 2 * t + g + 1)
                    copy(qn_t[:, 4 * g:4 * g + 4, :], f4(1 + g, HD)).then_inc(ev_qn, 1)

            def q_lat(t, k):
                if k == 0:
                    for g, bank in ((0, 3), (1, 0)):
                        act.wait_ge(tr_pe, 2 * t + g + 1)
                        spread_copy(t, qpe_t, g, f4(bank, ROPE)).then_inc(ev_pe, 1)
                for g in range(2):
                    bank = ((1, 2), (3, 0))[k][g]
                    act.wait_ge(mm_ql, 4 * t + 2 * k + g + 1)
                    spread_copy(t, qlat[:, k, :, :], g, f4(bank)).then_inc(ev_ql, 1)

            def exps(t, u):
                n = t * HEADS + u
                nk = nkeys(t)
                act.wait_ge(nm_ok, n + 1)
                if u >= 2:
                    act.wait_ge(tr_p, n - 1)
                nc.scalar.activation(prob[u % 2][:, 0:nk], F[u % 2][:, 0:nk], ACT.Exp, scale=SCALE,
                                     bias=stat[:, 24 + u % 2:25 + u % 2],
                                     accum_out=stat[:, 26 + u % 2:27 + u % 2]).then_inc(exp_ok, 1)

            def copy_probs(t, u):
                n = t * HEADS + u
                act.wait_ge(tr_p, n + 1)
                if u >= 2:
                    act.wait_ge(mm_pv, n - 1)
                full = [q for q in pieces(t) if q[1] == P]
                last = copy(prob_t[u % 2][:, 0:P * len(full)], F[2][:, 0:P * len(full)])
                if t == SAMPLE:
                    last = copy(prob_t[u % 2][0:DEC_SEQ, PAST:PAST + P], F[2][0:DEC_SEQ, PAST:PAST + P])
                last.then_inc(ev_pt, 1)

            def copy_values(t, u):
                act.wait_ge(mm_pv, t * HEADS + u + 1)
                src = F[3][:, 0:256].rearrange("p (k n) -> p k n", k=2)
                if t < SAMPLE:
                    copy(olat[:, :, u, :], src).then_inc(ev_pv, 1)
                else:
                    for k in range(2):
                        last = copy(olat[:, k, :, DEC_SEQ * u:DEC_SEQ * u + DEC_SEQ],
                                    src[:, k, :].rearrange("p (h s) -> p h s", h=HEADS))
                    last.then_inc(ev_pv, 1)

            def values_up(t):
                act.wait_ge(mm_mo, t + 1)
                copy(mix[:, 512:1024], F[0][:, :]).then_inc(ev_mo, 1)

            def turn_mix(t):
                for g in range(2):
                    act.wait_ge(tr_mix, 2 * t + g + 1)
                    copy(mix_t[:, 4 * g:4 * g + 4, :], f4(1 + g)).then_inc(ev_mix, 1)

            def turn_x2(t):
                for g in range(2):
                    act.wait_ge(tr_x2, 2 * t + g + 1)
                    copy(x2_t[:, 4 * g:4 * g + 4, :], f4(1 + g)).then_inc(ev_x2, 1)

            def copy_queries(t, g):
                act.wait_ge(wblk_used, t * (KD + HP) + KD + 4 * g + 4)
                copy(pq_t[:, 4 * g:4 * g + 4, :], f4(3 if g % 2 == 0 else 0)).then_inc(ev_pq, 1)

            def copy_key_scores(t, g):
                act.wait_ge(mm_ps, 4 * t + g + 1)
                copy(sc[:, 4 * g:4 * g + 4, :], f4(1 + g % 2)).then_inc(ev_ps, 1)

            def weights(t, j, g, gate_at):
                act.wait_ge(dot_ok, j * GROUPS + g + 1)
                cols = slice(GROUP * g, GROUP * g + GROUP)
                nc.scalar.activation(gel[:, cols], dots[:, cols], ACT.Gelu).then_inc(gel_ok, 1)
                act.wait_ge(gel_ok, j * GROUPS + g + 1)
                act.wait_ge(picks_ok, t + 1)
                for i in range(GROUP):
                    s = GROUP * g + i
                    nc.scalar.activation(wgt[:, s:s + 1], gel[:, s:s + 1], ACT.Copy, scale=gate_at(s)
                                         ).then_inc(wgt_ok, 1)
                for i in range(GROUP):
                    s = GROUP * g + i
                    act.wait_ge(wgt_ok, j * SLOTS + s + 1)
                    act.wait_ge(rows_free, j * SLOTS + s + 1 + SLOTS - DR)
                    nc.scalar.activation(diag[:, s % DR, :], ident[:, :], ACT.Copy, scale=wgt[:, s:s + 1]
                                         ).then_inc(diag_ok, 1)

            def finish(t):
                act.wait_ge(rows_free, SLOTS + PICKS * (t + 1))
                act.wait_ge(dot_ok, GROUPS * ROUNDS * (t + 1))
                nc.scalar.activation(xps[:, :], acc[:, :], ACT.Square, accum_out=stat[:, 36:37]).then_inc(sq_f, 1)
                act.wait_ge(ms_f, t + 1)
                nc.scalar.activation(stat[:, 38:39], stat[:, 37:38], ACT.Sqrt).then_inc(root_f, 1)

            def unit(t, n):
                if t == 0:
                    if 6 + n < NIN:
                        project_in(6 + n)
                    return
                r, g = divmod(n, GROUPS)
                weights(t - 1, (t - 1) * ROUNDS + r, g,
                        lambda s: gate[:, (t - 1) % 2, r * SLOTS + s:r * SLOTS + s + 1])
                if n == UNITS - 1:
                    finish(t - 1)

            for t in range(TILES):
                n = 0
                for step, i, units in STEPS:
                    if step == "turn_qk":
                        turn_qk(t)
                    elif step == "silu":
                        act.wait_ge(ms_gn, t + 1)
                        nc.scalar.activation(stat[:, 8:16], stat[:, 0:8], ACT.Sqrt).then_inc(root_gn, 1)
                    elif step == "latents":
                        act.wait_ge(ms_c, t + 1)
                        nc.scalar.activation(stat[:, 18:20], stat[:, 16:18], ACT.Sqrt).then_inc(root_c, 1)
                    elif step == "turn_c":
                        turn_c(t)
                    elif step == "q_nope":
                        q_nope(t)
                    elif step == "q_lat":
                        q_lat(t, i)
                    elif step == "attend":
                        if 1 <= i <= HEADS:
                            exps(t, i - 1)
                        if i >= 3:
                            copy_values(t, i - 3)
                        if 2 <= i < HEADS + 2:
                            copy_probs(t, i - 2)
                    elif step == "values_up":
                        values_up(t)
                    elif step == "turn_mix":
                        turn_mix(t)
                    elif step == "norm2":
                        act.wait_ge(ms_2, t + 1)
                        nc.scalar.activation(stat[:, 31:32], stat[:, 30:31], ACT.Sqrt).then_inc(root_2, 1)
                    elif step == "turn_x2":
                        turn_x2(t)
                    elif step == "query":
                        if i % 2 == 1 and i < HEADS:
                            copy_queries(t, i // 2)
                        if i >= 2 and i % 2 == 0:
                            copy_key_scores(t, i // 2 - 1)
                    elif step == "picks" and i == 0:
                        act.wait_ge(bd_ok, t + 1)
                        nc.scalar.activation(sm[1], sm[0], ACT.Exp).then_inc(be_ok, 1)
                    for _ in range(units):
                        unit(t, n)
                        n += 1
                for _ in range(LAST_UNITS):
                    unit(t, n)
                    n += 1
            with act.Fori(0, ROUNDS) as r:
                for g in range(GROUPS):
                    weights(SAMPLE, r + SAMPLE * ROUNDS, g,
                            lambda s: gate[:, SAMPLE % 2, bass.ds(r * SLOTS + s, 1)])
            finish(SAMPLE)

        @block.vector
        def _(dve):
            v = nc.vector
            steps = [0]

            def link(ins):
                steps[0] += 1
                ins.then_inc(dve_step, 1)
                dve.wait_ge(dve_step, steps[0])

            def row(ap, n):
                return ap.unsqueeze(2).to_broadcast([ap.shape[0], ap.shape[1], n])

            def mid(ap, n):
                return ap.unsqueeze(1).to_broadcast([ap.shape[0], n, ap.shape[1]])

            def rotate(dst, src, tmp, cos, sin, heads, half):
                s = src.rearrange("p (h c d) -> p h c d", h=heads, c=2)
                d = dst.rearrange("p (h c d) -> p h c d", h=heads, c=2)
                m = tmp.rearrange("p (h c d) -> p h c d", h=heads, c=2)
                c, sn = mid(cos, heads), mid(sin, heads)
                v.tensor_tensor(d[:, :, 0, :], s[:, :, 0, :], c, ALU.mult)
                v.tensor_tensor(m[:, :, 0, :], s[:, :, 1, :], sn, ALU.mult)
                v.tensor_tensor(d[:, :, 1, :], s[:, :, 1, :], c, ALU.mult)
                link(v.tensor_tensor(m[:, :, 1, :], s[:, :, 0, :], sn, ALU.mult))
                v.tensor_tensor(d[:, :, 0, :], d[:, :, 0, :], m[:, :, 0, :], ALU.subtract)
                return v.tensor_tensor(d[:, :, 1, :], d[:, :, 1, :], m[:, :, 1, :], ALU.add)

            for part, (lo, hi) in enumerate(((0, P), (P, TILES * P))):
                dve.wait_ge(xt_in[part], 16 * (2 - part))
                for k in range(KD):
                    v.tensor_scalar(xt[:, k, lo:hi], xt[:, k, lo:hi], ln1[:, k:k + 1], None, ALU.mult
                                    ).then_inc(xt_ok, 1)
            dve.wait_ge(sq_done, TILES)
            v.tensor_scalar(ssq1[:, :], ssq1[:, :], 1.0 / D_MODEL, EPS, ALU.mult, ALU.add).then_inc(ms1, 1)
            dve.wait_ge(root1, 1)
            v.reciprocal(rstd1[:, :], rstd1[:, :]).then_inc(rstd1_ok, 1)
            dve.wait_ge(consts_in, 16 * 18)
            o3 = three(ret_o, HEADS)

            def rotate_qk(t):
                if t == 0:
                    dve.wait_ge(ev_in, 6)
                else:
                    dve.wait_ge(picks_ok, t)
                    dve.wait_ge(pj_in, 16 * t)
                rotate(qk, pj[:, 0:1024], rtmp, cos64[:, t, :], sin64[:, t, :], 2 * HEADS, HD // 2
                       ).then_inc(qk_ok, 1)
                dve.wait_ge(qk_ok, t + 1)
                kd = k_sample if t == SAMPLE else k_prompt
                v.tensor_tensor(three(kdec, HEADS), three(qk[:, 512:1024], HEADS), row(kd[:, :], HD), ALU.mult
                                ).then_inc(kd_ok, 1)

            def ret_scores(t):
                if t == SAMPLE:
                    dve.wait_ge(dmask_in, 16)
                for g in range(2):
                    dve.wait_ge(mm_s, 2 * t + g + 1)
                    v.tensor_tensor(s_td[g], f4(g), dmask[:, 4 * g:4 * g + 4, :], ALU.mult).then_inc(ev_s, 1)

            def sample_states(t):
                vv = three(pj[:, OFF_V:OFF_V + 512], HEADS)
                for h in range(HEADS):
                    if h >= 2:
                        dve.wait_ge(mm_su, h - 1)
                    v.tensor_tensor(vmask[h % 2], mid(vv[:, h, :], DEC_BATCH), row(own[:, :], HD), ALU.mult
                                    ).then_inc(vm_ok, 1)
                    dve.wait_ge(mm_ss, h + 1)
                    v.tensor_tensor(ost[0], f8(h % 2), row(q_sample[:, h, :], HD), ALU.mult).then_inc(ev_ss, 1)
                    dve.wait_ge(ev_ss, h + 1)
                    link(v.tensor_reduce(o3[:, h, :], ost[0].rearrange("p b e -> p e b"), AX_X, ALU.add))
                    dve.wait_ge(mm_su, h + 1)
                    if h >= 2:
                        dve.wait_ge(st_stored[h % 2], 16 * (h // 2))
                    v.scalar_tensor_tensor(st_out[h % 2].rearrange("p b e -> p (b e)"),
                                           st_in[h % 2].rearrange("p b e -> p (b e)"), g_sample[h],
                                           F[3][0:HD, :], ALU.mult, ALU.add).then_inc(ev_su, 1)

            def ret_norm(t):
                dve.wait_ge(mm_oi, t + 1)
                if t == SAMPLE:
                    link(v.tensor_tensor(ret_o, ret_o, F[2][:, :], ALU.add))
                else:
                    if t == 0:
                        link(v.tensor_copy(ret_o, F[2][:, :]))
                    else:
                        dve.wait_ge(mm_os, t)
                        link(v.tensor_tensor(o3, f8(3), row(q_prompt[:, :], HD), ALU.mult))
                        link(v.tensor_tensor(ret_o, ret_o, F[2][:, :], ALU.add))
                    dve.wait_ge(mm_up, t + 1)
                    if t == 0:
                        v.tensor_copy(state[:, :, :], f8(0, HD)).then_inc(state_ok, 1)
                    else:
                        link(v.tensor_tensor(state[:, :, :], state[:, :, :], row(s_decay[:, :], HD), ALU.mult))
                        v.tensor_tensor(state[:, :, :], state[:, :, :], f8(0, HD), ALU.add).then_inc(state_ok, 1)
                mean, var = stat[:, 40:48], stat[:, 0:8]
                link(v.tensor_reduce(mean, o3, AX_X, ALU.add))
                link(v.tensor_scalar(mean, mean, 1.0 / HD, None, ALU.mult))
                link(v.tensor_tensor(o3, o3, row(mean, HD), ALU.subtract))
                link(v.tensor_tensor(osq, ret_o, ret_o, ALU.mult))
                link(v.tensor_reduce(var, three(osq, HEADS), AX_X, ALU.add))
                v.tensor_scalar(var, var, 1.0 / HD, EPS, ALU.mult, ALU.add).then_inc(ms_gn, 1)

            def silu(t):
                dve.wait_ge(eg_ok, t + 1)
                link(v.tensor_scalar(sgm, sgm, 1.0, None, ALU.add))
                link(v.reciprocal(sgm, sgm))
                link(v.tensor_tensor(sgm, sgm, pj[:, OFF_G:OFF_G + 512], ALU.mult))
                link(v.tensor_tensor(sgm, sgm, gnw[:, :], ALU.mult))
                dve.wait_ge(root_gn, t + 1)
                link(v.reciprocal(stat[:, 8:16], stat[:, 8:16]))
                link(v.tensor_tensor(o3, o3, row(stat[:, 8:16], HD), ALU.mult))
                v.tensor_tensor(mix[:, 0:512], ret_o, sgm, ALU.mult).then_inc(y_ok, 1)

            def stats(t):
                dve.wait_ge(y_ok, t + 1)
                kv = ckvn_s if t == SAMPLE else ckv[:, t, :]
                v.tensor_tensor_reduce(cqn, pj[:, OFF_CQ:OFF_CQ + RANK], pj[:, OFF_CQ:OFF_CQ + RANK], 1.0, 0.0,
                                       ALU.mult, ALU.add, stat[:, 16:17])
                link(v.tensor_tensor_reduce(kv, pj[:, OFF_CKV:OFF_CKV + RANK], pj[:, OFF_CKV:OFF_CKV + RANK],
                                            1.0, 0.0, ALU.mult, ALU.add, stat[:, 17:18]))
                v.tensor_scalar(stat[:, 16:18], stat[:, 16:18], 1.0 / RANK, EPS, ALU.mult, ALU.add
                                ).then_inc(ms_c, 1)

            def latents(t):
                kv = ckvn_s if t == SAMPLE else ckv[:, t, :]
                dve.wait_ge(root_c, t + 1)
                link(v.reciprocal(stat[:, 18:20], stat[:, 18:20]))
                v.scalar_tensor_tensor(cqn, pj[:, OFF_CQ:OFF_CQ + RANK], stat[:, 18:19], qnw[:, :],
                                       ALU.mult, ALU.mult)
                v.scalar_tensor_tensor(kv, pj[:, OFF_CKV:OFF_CKV + RANK], stat[:, 19:20], kvw[:, :],
                                       ALU.mult, ALU.mult).then_inc(c_ok, 1)
                rotate(kpe, pj[:, OFF_KPE:OFF_KPE + ROPE], ktmp, cos32[:, t, :], sin32[:, t, :], 1, ROPE // 2
                       ).then_inc(kpe_ok, 1)

            def maxima(t, u):
                n = t * HEADS + u
                nk = nkeys(t)
                dve.wait_ge(mm_sc, n + 1)
                if t < SAMPLE:
                    link(v.memset(F[u % 2][0:CHUNK, nk - CHUNK:nk], MASKED))
                link(v.tensor_reduce(stat[:, 20 + u % 2:21 + u % 2], F[u % 2][:, 0:nk], AX_X, ALU.max))
                if u >= 2:
                    dve.wait_ge(exp_ok, n - 1)
                v.tensor_scalar(stat[:, 24 + u % 2:25 + u % 2], stat[:, 20 + u % 2:21 + u % 2], -SCALE, None,
                                ALU.mult).then_inc(nm_ok, 1)

            def normalise(t, u):
                n = t * HEADS + u
                nk = nkeys(t)
                dve.wait_ge(exp_ok, n + 1)
                link(v.reciprocal(stat[:, 28 + u % 2:29 + u % 2], stat[:, 26 + u % 2:27 + u % 2]))
                v.tensor_scalar(prob[u % 2][:, 0:nk], prob[u % 2][:, 0:nk], stat[:, 28 + u % 2:29 + u % 2], None,
                                ALU.mult).then_inc(p_ok, 1)

            def residual(t):
                h = hbuf[:, t % 2, :]
                dve.wait_ge(wblk_used, t * (KD + HP) + KD)
                dve.wait_ge(xres_in, 16 * (t + 1))
                v.tensor_tensor(h[:, 0:512], h[:, 0:512], F[3][:, :], ALU.add)
                link(v.tensor_tensor(h[:, 512:1024], h[:, 512:1024], F[0][:, :], ALU.add))
                link(v.tensor_tensor_reduce(xn2[:, t % 2, :], h, h, 1.0, 0.0, ALU.mult, ALU.add, stat[:, 30:31]))
                v.tensor_scalar(stat[:, 30:31], stat[:, 30:31], 1.0 / D_MODEL, EPS, ALU.mult, ALU.add
                                ).then_inc(ms_2, 1)

            def norm2(t):
                dve.wait_ge(root_2, t + 1)
                link(v.reciprocal(stat[:, 31:32], stat[:, 31:32]))
                v.scalar_tensor_tensor(xn2[:, t % 2, :], hbuf[:, t % 2, :], stat[:, 31:32], ln2[:, :],
                                       ALU.mult, ALU.mult).then_inc(x2_ok, 1)

            def top16(span, values_of, vals, idx):
                for i in span:
                    last = v.max(vals[:, i, 0:8], values_of(i))
                link(last)
                for i in span:
                    v.max_index(idx[:, i, 0:8], vals[:, i, 0:8], values_of(i))
                for i in span:
                    last = v.match_replace(values_of(i), vals[:, i, 0:8], values_of(i), LOWEST)
                link(last)
                for i in span:
                    last = v.max(vals[:, i, 8:16], values_of(i))
                link(last)
                for i in span:
                    last = v.max_index(idx[:, i, 8:16], vals[:, i, 8:16], values_of(i))
                link(last)

            tv4 = tv.rearrange("p (h c) k -> p h c k", c=2)
            tif4 = tif.rearrange("p (h c) k -> p h c k", c=2)
            hot3 = hot.rearrange("p h k i -> p (h k) i")
            wide = [P, HEADS, TOPK, TOPK]

            def pairs():
                v.tensor_copy(tif, ti)
                link(v.tensor_tensor(cand, tv4[:, :, 0, :].unsqueeze(3).to_broadcast(wide),
                                     tv4[:, :, 1, :].unsqueeze(2).to_broadcast(wide), ALU.add))

            def places(t):
                v.tensor_tensor(three(sm[0], HEADS), bv, bv[:, :, 0:1].to_broadcast([P, HEADS, TOPK]),
                                ALU.subtract).then_inc(bd_ok, 1)
                v.tensor_scalar(sm[2].bitcast(U32), bj.rearrange("p h k -> p (h k)"), 4, None,
                                ALU.logical_shift_right)
                link(v.tensor_scalar(sm[3].bitcast(U32), bj.rearrange("p h k -> p (h k)"), TOPK - 1, None,
                                     ALU.bitwise_and))
                v.tensor_copy(sm[4], sm[2].bitcast(U32))
                link(v.tensor_copy(sm[5], sm[3].bitcast(U32)))

            def look_up(c):
                link(v.tensor_tensor(hot3, row(sm[4 + c], TOPK), mid(count16[:, :], PICKS), ALU.is_equal))
                link(v.tensor_tensor(hot, hot, tif4[:, :, c, :].unsqueeze(2).to_broadcast(wide), ALU.mult))
                link(v.tensor_reduce(sm[6 + c], hot3, AX_X, ALU.add))

            def gates(t):
                v.scalar_tensor_tensor(eidx[:, t % 2, :], sm[6], float(KEYS), sm[7], ALU.mult, ALU.add)
                dve.wait_ge(be_ok, t + 1)
                link(v.tensor_reduce(stat[:, 48:56], three(sm[1], HEADS), AX_X, ALU.add))
                link(v.reciprocal(stat[:, 48:56], stat[:, 48:56]))
                v.tensor_tensor(three(gate[:, t % 2, :], HEADS), three(sm[1], HEADS), row(stat[:, 48:56], TOPK),
                                ALU.mult).then_inc(picks_ok, 1)

            def first_dot(t):
                if t >= 1:
                    dve.wait_ge(sq_f, t)
                else:
                    dve.wait_ge(ev_in, NIN)
                v.tensor_copy(xps[:, :], xn2[:, t % 2, :]).then_inc(xps_ok, 1)
                dve.wait_ge(xps_ok, t + 1)

            def dot(j, s):
                dve.wait_ge(rows_in[s], j * 16 + 16)
                last = v.tensor_tensor_reduce(rows[:, s, 0:D_MODEL], rows[:, s, 0:D_MODEL], xps[:, :],
                                              1.0, 0.0, ALU.mult, ALU.add, dots[:, s:s + 1])
                if s % GROUP == GROUP - 1:
                    last.then_inc(dot_ok, 1)

            def finish(t):
                dve.wait_ge(sq_f, t + 1)
                v.tensor_scalar(stat[:, 37:38], stat[:, 36:37], 1.0 / D_MODEL, EPS, ALU.mult, ALU.add
                                ).then_inc(ms_f, 1)
                dve.wait_ge(root_f, t + 1)
                link(v.reciprocal(stat[:, 39:40], stat[:, 38:39]))
                v.scalar_tensor_tensor(hbuf[:, t % 2, :], acc[:, :], stat[:, 39:40], lnf[:, :],
                                       ALU.mult, ALU.mult).then_inc(y_done, 1)

            def unit(t, n):
                if t == 0:
                    return
                if n == 0:
                    first_dot(t - 1)
                for i in range(GROUP):
                    pick = n * GROUP + i
                    dot((t - 1) * ROUNDS + pick // SLOTS, pick % SLOTS)
                if n == UNITS - 1:
                    finish(t - 1)

            for t in range(TILES):
                n = 0
                for step, i, units in STEPS:
                    if step == "rotate":
                        rotate_qk(t)
                    elif step == "ret_scores":
                        ret_scores(t)
                    elif step == "ret_sums" and t == SAMPLE:
                        sample_states(t)
                    elif step == "ret_norm":
                        ret_norm(t)
                    elif step == "silu":
                        silu(t)
                    elif step == "stats":
                        stats(t)
                    elif step == "latents":
                        latents(t)
                    elif step == "q_rope":
                        dve.wait_ge(mm_pe, t + 1)
                        rotate(qpe, F[0][:, 0:256], ptmp, cos32[:, t, :], sin32[:, t, :], HEADS, ROPE // 2
                               ).then_inc(qpe_ok, 1)
                    elif step == "attend":
                        if 2 <= i < HEADS + 2:
                            normalise(t, i - 2)
                        if 1 <= i <= HEADS:
                            maxima(t, i - 1)
                    elif step == "residual":
                        residual(t)
                    elif step == "norm2":
                        norm2(t)
                    elif step == "query" and i >= 3 and i % 2 == 1:
                        dve.wait_ge(ev_ps, 4 * t + i // 2)
                        top16(range(4 * (i // 2 - 1), 4 * (i // 2)), lambda i: sc[:, i, :], tv, ti)
                    elif step == "pairs":
                        pairs()
                    elif step == "best":
                        top16(range(2 * i, 2 * i + 2), lambda i: candf[:, i, :], bv, bj)
                    elif step == "places":
                        places(t)
                    elif step == "picks":
                        look_up(i)
                    elif step == "gates":
                        gates(t)
                    for _ in range(units):
                        unit(t, n)
                        n += 1
                for _ in range(LAST_UNITS):
                    unit(t, n)
                    n += 1
            first_dot(SAMPLE)
            with dve.Fori(0, ROUNDS) as r:
                for s in range(SLOTS):
                    dot(r + SAMPLE * ROUNDS, s)
            finish(SAMPLE)


def kernel(**inputs):
    import concourse.bacc as _bacc
    from concourse.bass_utils import run_bass_kernel_spmd as _run

    x = {k: np.asarray(v) for k, v in inputs.items()}
    con = np.ascontiguousarray
    arrays = dict(tables())

    def spread(w):
        return con(np.broadcast_to(w.reshape(1, -1), (P, w.size)))

    x_all = np.concatenate([x["x_prompt"][0], x["x_sample"].reshape(P, D_MODEL)], axis=0)
    cache = x["cache_mla_ckv"][0]
    arrays.update(
        x_all=x_all,
        x_t=con(x_all.T.reshape(KD, P, TILES * P).transpose(1, 0, 2)),
        ln1=con(x["ln1_w"][0].reshape(KD, P).T),
        w_in=con(x["w_in"][0]),
        gn=spread(x["ret_gn_w"][0]), qn=spread(x["mla_q_norm_w"][0]), kvn=spread(x["mla_kv_norm_w"][0]),
        ln2=spread(x["ln2_w"][0]), lnf=spread(x["lnf_w"]),
        w_uq=con(x["mla_w_uq"][0].reshape(RANK, HEADS * QD)),
        w_ukt=con(x["mla_w_uk"][0].transpose(2, 1, 0)),
        w_uv=con(x["mla_w_uv"][0].reshape(RANK, HEADS * HD)),
        w_o=con(x["w_o"][0]),
        w_q=con(x["peer_w_q"][0].reshape(KD, P, HP, P).transpose(2, 1, 0, 3).reshape(HP, P, D_MODEL)),
        subk=con(x["peer_sub_keys"][0].reshape(HP, KEYS, P).transpose(2, 0, 1)),
        uv=np.concatenate([x["peer_u"][0], x["peer_v"][0]], axis=1),
        cache=con(cache),
        cache_t=con(cache.transpose(0, 2, 1).reshape(DEC_BATCH, 2, P, PAST).transpose(0, 2, 1, 3)),
        cache_rt=con(x["cache_mla_krope"][0].transpose(0, 2, 1)),
        state=con(x["state_retention"][0]),
    )
    outputs = dict(y_prompt=(SEQ, D_MODEL), y_sample=(P, D_MODEL), ckv_p=(SEQ, RANK), kr_p=(SEQ, ROPE),
                   state_p=(HD, HEADS, HD), ckv_s=(P, RANK), kr_s=(P, ROPE),
                   state_s=(DEC_BATCH, HEADS, HD, HD))

    nc = _bacc.Bacc("TRN2", target_bir_lowering=False, num_devices=1)
    ins = {k: nc.dram_tensor(f"in_{k}", v.shape, F32, kind="ExternalInput").ap() for k, v in arrays.items()}
    outs = {k: nc.dram_tensor(f"out_{k}", s, F32, kind="ExternalOutput").ap() for k, s in outputs.items()}
    build(nc, ins, outs)
    got = _run(nc, [{f"in_{k}": v for k, v in arrays.items()}], core_ids=[0]).results[0]
    g = {k: got[f"out_{k}"] for k in outputs}
    return (g["y_prompt"].reshape(1, SEQ, D_MODEL),
            g["y_sample"].reshape(DEC_BATCH, DEC_SEQ, D_MODEL),
            g["ckv_p"].reshape(1, 1, SEQ, RANK),
            g["kr_p"].reshape(1, 1, SEQ, ROPE),
            con(g["state_p"].transpose(1, 0, 2)).reshape(1, 1, HEADS, HD, HD),
            g["ckv_s"].reshape(1, DEC_BATCH, DEC_SEQ, RANK),
            g["kr_s"].reshape(1, DEC_BATCH, DEC_SEQ, ROPE),
            g["state_s"].reshape(1, DEC_BATCH, HEADS, HD, HD))
```

```python
from contextlib import ExitStack

import numpy as np

import concourse.bass as bass
from concourse import mybir

F32 = mybir.dt.float32
U32 = mybir.dt.uint32
ALU = mybir.AluOpType
ACT = mybir.ActivationFunctionType
AX_X = mybir.AxisListType.X

P = 128
D_MODEL = 1024
SEQ = 512
DEC_BATCH = 8
DEC_SEQ = 16
PAST = 256
CHUNK = 64
EPS = 1e-6
HEADS = 8
HD = 64
ROPE = 32
RANK = 256
QD = HD + ROPE
IN_COLS = 4 * HEADS * HD + 2 * RANK + ROPE
PROMPT_TILES = SEQ // P
TILES = PROMPT_TILES + 1
SAMPLE = PROMPT_TILES
KD = D_MODEL // P
KEYS = 128
TOPK = 16
EXPERTS = KEYS * KEYS
HP = 2 * HEADS
PICKS = HEADS * TOPK
SLOTS = 8
ROUNDS = PICKS // SLOTS
GROUP = 2
GROUPS = SLOTS // GROUP
SCALE = float(QD) ** -0.5
OFF_Q, OFF_K, OFF_V, OFF_G = 0, 512, 1024, 1536
OFF_CQ, OFF_CKV, OFF_KPE = 2048, 2304, 2560
MASKED = -1e30
LOWEST = -3.0e38

PARTS = 2
PART_PICKS = PICKS // PARTS


def steps_of(t):
    attend = (1.2, 1.7, 2.1, 2.5, 2.0)[t]
    states = [("state", i, 0.8) for i in range(HEADS)] if t == SAMPLE else []
    return ([("rotate", 0, 2.2), ("turn_qk", 0, 1.8), ("ret_scores", 0, 1.1), ("ret_sums", 0, 1.4)] + states
            + [("ret_norm", 0, 1.4), ("silu", 0, 1.2), ("stats", 0, 0.5), ("latents", 0, 0.6), ("turn_c", 0, 0.6),
               ("q_rope", 0, 0.5), ("q_nope", 0, 1.5), ("q_lat", 0, 1.5), ("q_lat", 1, 0.8)]
            + [("attend", i, attend) for i in range(HEADS + 3)]
            + [("values_up", 0, 0.9), ("turn_mix", 0, 0.9)]
            + [("w_o", i, 1.5) for i in range(4)]
            + [("residual", 0, 1.5), ("norm2", 0, 1.0), ("turn_x2", 0, 0.9)]
            + [("query", i, 1.5) for i in range(HEADS + 1)]
            + [("keys", 2, 1.7), ("keys", 3, 1.7), ("pairs", 1, 0.5), ("best", 2, 1.4), ("best", 3, 1.4),
               ("places", 1, 0.4), ("picks", 1, 2.6), ("gates", 1, 0.8)])


UNITS = PICKS // GROUP
RESERVE = 7
EARLY = (("pairs", 1), ("best", 3), ("places", 1), ("gates", 1))
DVE_LEAD = 1


def slot_units(t):
    if t == 0:
        return [int((step, i) in EARLY) for step, i, _ in steps_of(t)]
    shares = [share for _, _, share in steps_of(t)]
    total = UNITS - RESERVE - len(EARLY) if t == 1 else UNITS
    upto = [round(total * sum(shares[:i]) / sum(shares)) for i in range(len(shares) + 1)]
    return [after - before for before, after in zip(upto, upto[1:])]


def unit_span(t, step):
    before = (0, len(EARLY))[t] if t < 2 else UNITS * (t - 1) - RESERVE
    before += sum(slot_units(t)[:step])
    return range(before, before + slot_units(t)[step])


def log_decay():
    return np.log1p(-np.exp2(-5.0 - np.arange(HEADS)))


def tables():
    pos = np.concatenate([np.arange(SEQ), PAST + np.tile(np.arange(DEC_SEQ), DEC_BATCH)]).astype(np.float32)

    def angles(half):
        inv = (np.float32(10000.0) ** (-np.arange(half, dtype=np.float32) / half)).astype(np.float32)
        a = (pos[:, None] * inv[None, :]).astype(np.float32).astype(np.float64)
        lay = lambda m: np.ascontiguousarray(m.astype(np.float32).reshape(TILES, P, half).transpose(1, 0, 2))
        return lay(np.cos(a)), lay(np.sin(a))

    lg = log_decay()
    k_scale = HD ** -0.5
    i = np.arange(P)
    gap = np.abs(i[:, None] - i[None, :])
    seen = (i[:, None] // CHUNK) <= (i[None, :] // CHUNK)
    same = (i[:, None] // DEC_SEQ) == (i[None, :] // DEC_SEQ)
    decay = np.exp(lg[None, :, None] * gap[:, None, :]) * k_scale
    d_prompt = decay * seen[:, None, :]
    d_sample = decay * same[:, None, :]
    s = i % DEC_SEQ
    own = (i[:, None] // DEC_SEQ == np.arange(DEC_BATCH)[None, :]).astype(np.float64)
    q_prompt = np.exp(lg[None, :] * (i[:, None] + 1.0))
    q_sample = np.exp(lg[None, :] * (s[:, None] + 1.0))[:, :, None] * own[:, None, :]
    k_prompt = np.exp(lg[None, :] * (P - 1.0 - i[:, None])) * k_scale
    k_sample = np.exp(lg[None, :] * (DEC_SEQ - 1.0 - s[:, None])) * k_scale
    cos64, sin64 = angles(HD // 2)
    cos32, sin32 = angles(ROPE // 2)
    out = dict(cos64=cos64, sin64=sin64, cos32=cos32, sin32=sin32, d_prompt=d_prompt, d_sample=d_sample,
               q_prompt=q_prompt, q_sample=q_sample, k_prompt=k_prompt, k_sample=k_sample, own=own,
               s_decay=np.tile(np.exp(lg * P)[None, :], (HD, 1)), ident=np.eye(P),
               count16=np.tile(np.arange(TOPK)[None, :], (P, 1)))
    return {k: np.ascontiguousarray(v.astype(np.float32)) for k, v in out.items()}


def build(nc, a, out):
    g_sample = [float(np.exp(v * DEC_SEQ)) for v in log_decay()]
    ctx = ExitStack()
    with ctx:
        def sb(name, shape, dt=F32):
            return ctx.enter_context(nc.sbuf_tensor(name, shape, dt))

        def sem(name):
            return ctx.enter_context(nc.semaphore(name))

        proj_d = nc.dram_tensor("proj_d", (TILES, P, IN_COLS), F32, kind="Internal").ap()

        rows = sb("rows", [P, SLOTS, 2 * D_MODEL])
        win_last = sb("win_last", [P, KD, ROPE])
        WB = 3
        wblk = sb("wblk", [P, WB, D_MODEL])
        PJ, MIX, R = 0, 3104, 4128
        work = sb("work", [P, R + 9216])
        w_uq = sb("w_uq", [P, 2, HEADS * QD])
        w_ukt = sb("w_ukt", [HD, HEADS, RANK])
        w_uv = sb("w_uv", [P, 2, HEADS * HD])
        subk = sb("subk", [P, HP, KEYS])
        dmask = sb("dmask", [P, HEADS, P])
        cos64 = sb("cos64", [P, TILES, HD // 2])
        sin64 = sb("sin64", [P, TILES, HD // 2])
        cos32 = sb("cos32", [P, TILES, ROPE // 2])
        sin32 = sb("sin32", [P, TILES, ROPE // 2])
        q_prompt = sb("q_prompt", [P, HEADS])
        q_sample = sb("q_sample", [P, HEADS, DEC_BATCH])
        k_prompt = sb("k_prompt", [P, HEADS])
        k_sample = sb("k_sample", [P, HEADS])
        own = sb("own", [P, DEC_BATCH])
        s_decay = sb("s_decay", [HD, HEADS])
        count16 = sb("count16", [P, TOPK])
        ident = sb("ident", [P, P])
        ln1 = sb("ln1", [P, KD])
        ln2 = sb("ln2", [P, D_MODEL])
        lnf = sb("lnf", [P, D_MODEL])
        gnw = sb("gnw", [P, HEADS * HD])
        qnw = sb("qnw", [P, RANK])
        kvw = sb("kvw", [P, RANK])
        keys_all = sb("keys_all", [P, 2560])
        ckv = keys_all[:, 0:1024].rearrange("p (t c) -> p t c", t=PROMPT_TILES)
        ckvt = keys_all[:, 1024:2048].rearrange("p (k n) -> p k n", k=2)
        krt = keys_all[0:ROPE, 2048:2560]
        st_in = [keys_all[0:HD, 512 * i:512 * i + 512].rearrange("p (b e) -> p b e", b=DEC_BATCH) for i in range(2)]
        st_out = [keys_all[0:HD, 1024 + 512 * i:1536 + 512 * i].rearrange("p (b e) -> p b e", b=DEC_BATCH)
                  for i in range(2)]
        state = sb("state", [HD, HEADS, HD])
        hbuf = sb("hbuf", [P, 2, D_MODEL])
        xn2 = sb("xn2", [P, 2, D_MODEL])
        eidx = sb("eidx", [P, 2, PICKS], U32)
        gate = sb("gate", [P, 2, PICKS])
        cur = sb("cur", [P, 2, SLOTS], U32)
        DR = 4
        diag = sb("diag", [P, DR, P])
        dots = sb("dots", [P, SLOTS])
        gel = sb("gel", [P, SLOTS])
        wgt = sb("wgt", [P, SLOTS])
        ssq1 = sb("ssq1", [P, TILES])
        rstd1 = sb("rstd1", [P, TILES])
        stat = sb("stat", [P, 64])

        def wv(lo, n, parts=P, dt=None):
            return work[0:parts, lo:lo + n]

        def three(ap, k):
            return ap.rearrange("p (k n) -> p k n", k=k)

        flat_rows = rows[:, :, :].rearrange("p s n -> p (s n)")
        xt = three(flat_rows[:, 0:TILES * D_MODEL], KD)
        win = [three(flat_rows[:, 5120 + 4096 * i:9216 + 4096 * i], KD) for i in range(2)]
        win.append(win_last[:, :, :])
        stage = three(flat_rows[:, 13312:13312 + 4 * 512], 4)
        xs = [wv(R, D_MODEL)] + [buf[:, i, :] for buf in (hbuf, xn2) for i in range(2)]
        sq_junk = flat_rows[:, 15360:15360 + D_MODEL]
        pj = wv(PJ, IN_COLS)
        mix = wv(MIX, D_MODEL)
        qk = wv(R, 1024)
        rtmp = wv(R + 1024, 1024)
        q_t = three(wv(R + 2048, 1024, HD), HEADS)
        k_t = three(wv(R + 3072, 1024, HD), HEADS)
        s_td = [three(wv(R + 4096 + 512 * i, 512), 4) for i in range(2)]
        kdec = wv(R + 5120, 512)
        ret_o = wv(R + 5632, 512)
        osq = wv(R + 6144, 512)
        vmask = [three(wv(R + 6656 + 512 * i, 512), DEC_BATCH) for i in range(2)]
        ost = [three(wv(R + 7680, 512), DEC_BATCH)] * 2
        sgm = wv(R + 8192, 512)
        cqn = wv(R, 256)
        ckvn_s = wv(R + 256, 256)
        cq_t = three(wv(R + 512, 256), 2)
        ckvt_s = three(wv(R + 768, 256), 2)
        krt_s = wv(R + 1024, 128, ROPE)
        qpe = wv(R + 1152, 256)
        ptmp = wv(R + 1408, 256)
        kpe = wv(R + 1664, ROPE)
        ktmp = wv(R + 1696, ROPE)
        qpe_t = three(wv(R + 1728, 1024, ROPE), HEADS)
        qn_t = three(wv(R + 2752, 1024, HD), HEADS)
        prob = [wv(R + 2752 + 512 * i, 512) for i in range(2)]
        qlat = wv(R + 3776, 2048).rearrange("p (k h n) -> p k h n", k=2, h=HEADS)
        qlat_s = wv(R + 3776, 2048).rearrange("p (k b m) -> p k b m", k=2, b=DEC_BATCH)
        prob_t = [wv(R + 5824 + 512 * i, 512) for i in range(2)]
        olat = wv(R + 6848, 2048).rearrange("p (k h n) -> p k h n", k=2, h=HEADS)
        mix_t = three(wv(R + 1728, 1024), KD)
        ca_t = [three(wv(PJ + 1536 * i, 512), 2) for i in range(2)]
        ca = [three(wv(PJ + 1536 * i + 512, 512), 2) for i in range(2)]
        ca_r = [wv(PJ + 1536 * i + 1024, 256, ROPE) for i in range(2)]
        ca_n = [wv(PJ + 1536 * i + 1280, 256, DEC_SEQ) for i in range(2)]
        x2_t = three(wv(R, 1024), KD)
        pq_t = three(wv(R + 1024, 2048), HP)
        sc = three(wv(R + 3072, 2048), HP)
        PART = HEADS // PARTS
        cand = wv(R + 5120, 1024).rearrange("p (h i j) -> p h i j", h=PART, i=TOPK)
        candf = three(wv(R + 5120, 1024), PART)
        hot = wv(R + 7168, 1024).rearrange("p (h k i) -> p h k i", h=PART, k=TOPK)
        tv = three(wv(MIX, 256), HP)
        ti = three(wv(MIX + 256, 256).bitcast(U32), HP)
        tif = three(wv(MIX + 512, 256), HP)
        bv = three(wv(MIX + 768, 128), HEADS)
        bj = three(wv(MIX + 896, 128).bitcast(U32), HEADS)
        sm = [wv(R + 6144 + PART_PICKS * i, PART_PICKS) for i in range(8)]

        F = [ctx.enter_context(nc.psum_tensor(f"F{i}", [P, 512], F32)) for i in range(4)]
        acc = ctx.enter_context(nc.psum_tensor("acc", [P, D_MODEL], F32))
        xps = ctx.enter_context(nc.psum_tensor("xps", [P, D_MODEL], F32))

        def f4(i, parts=P):
            return F[i][0:parts, :].rearrange("p (k n) -> p k n", k=4)

        def f8(i, parts=P):
            return F[i][0:parts, :].rearrange("p (k n) -> p k n", k=8)

        xt_in, xs_in = (sem("xt0_in"), sem("xt_in")), (sem("xs0_in"), sem("xs_in"))
        consts_in, small_in = (sem("consts0_in"), sem("consts_in")), sem("small_in")
        win_in = [sem(f"win_in{i}") for i in range(3)]
        stored = [sem(f"stored{i}") for i in range(4)]
        pj_in, xres_in, wblk_in = sem("pj_in"), sem("xres_in"), [sem(f"wblk_in{i}") for i in range(WB)]
        dmask_in, gains_in = sem("dmask_in"), sem("gains_in")
        st_landed = [sem(f"st_landed{i}") for i in range(2)]
        st_stored = [sem(f"st_stored{i}") for i in range(2)]
        keys_in = [sem(f"keys_in{i}") for i in range(2)]
        values_in = [sem(f"values_in{i}") for i in range(2)]
        outs_done = sem("outs_done")
        new_ckv_out = sem("new_ckv_out")
        y_out = sem("y_out")
        sq_done, ms1, root1, rstd1_ok = sem("sq_done"), sem("ms1"), sem("root1"), sem("rstd1_ok")
        xt_ok, mm_in, ev_in = sem("xt_ok"), sem("mm_in"), sem("ev_in")
        dve_step, act_step = sem("dve_step"), sem("act_step")
        qk_ok, tr_qk, ev_qk = sem("qk_ok"), sem("tr_qk"), sem("ev_qk")
        mm_s, ev_s, mm_oi, mm_os, mm_up = sem("mm_s"), sem("ev_s"), sem("mm_oi"), sem("mm_os"), sem("mm_up")
        mm_ss, ev_ss, mm_su, ev_su, vm_ok = sem("mm_ss"), sem("ev_ss"), sem("mm_su"), sem("ev_su"), sem("vm_ok")
        kd_ok, state_ok = sem("kd_ok"), sem("state_ok")
        ms_gn, root_gn, eg_ok = sem("ms_gn"), sem("root_gn"), sem("eg_ok")
        y_ok = sem("y_ok")
        ms_c, root_c, c_ok, kpe_ok = sem("ms_c"), sem("root_c"), sem("c_ok"), sem("kpe_ok")
        tr_c, ev_c, mm_pe, qpe_ok = sem("tr_c"), sem("ev_c"), sem("mm_pe"), sem("qpe_ok")
        mm_qn, ev_qn, tr_pe, ev_pe, mm_ql, ev_ql = (sem("mm_qn"), sem("ev_qn"), sem("tr_pe"), sem("ev_pe"),
                                                    sem("mm_ql"), sem("ev_ql"))
        mm_sc, nm_ok, exp_ok, p_ok = sem("mm_sc"), sem("nm_ok"), sem("exp_ok"), sem("p_ok")
        tr_p, ev_pt, mm_pv, ev_pv = sem("tr_p"), sem("ev_pt"), sem("mm_pv"), sem("ev_pv")
        mm_mo, ev_mo, tr_mix, ev_mix, mm_wo, h_ok = (sem("mm_mo"), sem("ev_mo"), sem("tr_mix"), sem("ev_mix"),
                                                     sem("mm_wo"), sem("h_ok"))
        wblk_used = sem("wblk_used")
        ms_2, root_2, x2_ok, tr_x2, ev_x2 = sem("ms_2"), sem("root_2"), sem("x2_ok"), sem("tr_x2"), sem("ev_x2")
        ev_pq, mm_ps, ev_ps = sem("ev_pq"), sem("mm_ps"), sem("ev_ps")
        bd_ok, be_ok, picks_ok = sem("bd_ok"), sem("be_ok"), sem("picks_ok")
        idx_here, rows_free = sem("idx_here"), sem("rows_free")
        rows_in = [sem(f"rows_in{i}") for i in range(SLOTS)]
        xps_ok, dot_ok, gel_ok, wgt_ok, diag_ok = (sem("xps_ok"), sem("dot_ok"), sem("gel_ok"), sem("wgt_ok"),
                                                   sem("diag_ok"))
        sq_f, ms_f, root_f, y_done = sem("sq_f"), sem("ms_f"), sem("root_f"), sem("y_done")

        second = [3, 4, 0, 1, 2, 5]
        items = [(cb, 0) for cb in range(6)] + [(cb, t) for cb in second for t in range(1, TILES)]
        loads = [(0, 0), (1, 1), (2, 0), (3, 1), (4, 0), (5, 2), (0, 1), (1, 0), (2, 1)]
        NIN = len(items)
        last_beside = [name for name, i, _ in steps_of(0)].index("query") + HEADS - 1
        halves = 2 * (NIN - 6)

        def beside_first(step):
            at = [halves * min(k, last_beside + 1) // (last_beside + 1) for k in (step, step + 1)]
            return [(6 + m // 2, m % 2) for m in range(at[0], at[1])]

        banks = [acc[:, 0:512], acc[:, 512:1024], xps[:, 0:512], xps[:, 512:1024]]
        width = [512] * 5 + [ROPE]

        stores = [16 * len(range(6 + (i - 6) % 4, NIN, 4)) for i in range(4)]

        def nkeys(t):
            return P * (t + 1) if t < SAMPLE else PAST + DEC_SEQ

        def pieces(t):
            return [(P * j, min(P, nkeys(t) - P * j)) for j in range((nkeys(t) + P - 1) // P)]

        block = ctx.enter_context(nc.Block())

        @block.sync
        def _(sp):
            sp.dma_start(xt[:, :, 0:P], a["x_t"][:, :, 0:P]).then_inc(xt_in[0], 16)
            sp.dma_start(ln1[:, :], a["ln1"]).then_inc(xt_in[0], 16)
            sp.dma_start(xs[0], a["x_all"][0:P, :]).then_inc(xs_in[0], 16)
            sp.wait_ge(win_in[0], 16 * 2)
            for dst, name in ((cos64, "cos64"), (sin64, "sin64"), (dmask, "d_prompt")):
                sp.dma_start(dst[:, :, :], a[name]).then_inc(consts_in[0], 16)
            for dst, name in ((k_prompt, "k_prompt"), (ident, "ident")):
                sp.dma_start(dst[:, :], a[name]).then_inc(consts_in[0], 16)
            sp.wait_ge(win_in[0], 16 * 3)
            sp.dma_start(xt[:, :, P:], a["x_t"][:, :, P:]).then_inc(xt_in[1], 16)
            for t in range(1, TILES):
                sp.dma_start(xs[t], a["x_all"][P * t:P * t + P, :]).then_inc(xs_in[1], 16)
            sp.wait_ge(mm_in, 6)
            for dst, name in ((gnw, "gn"), (q_prompt, "q_prompt"), (qnw, "qn"), (kvw, "kvn"), (s_decay, "s_decay"),
                              (k_sample, "k_sample"), (own, "own"), (count16, "count16")):
                sp.dma_start(dst[:, :], a[name]).then_inc(consts_in[1], 16)
            for dst, name in ((cos32, "cos32"), (sin32, "sin32"), (q_sample, "q_sample")):
                sp.dma_start(dst[:, :, :], a[name]).then_inc(consts_in[1], 16)
            sp.dma_start(w_uq[:, :, :], a["w_uq"].rearrange("(k p) n -> p k n", p=P)).then_inc(small_in, 16)
            sp.dma_start(w_ukt[:, :, :], a["w_ukt"]).then_inc(small_in, 16)
            sp.dma_start(w_uv[:, :, :], a["w_uv"].rearrange("(k p) n -> p k n", p=P)).then_inc(small_in, 16)
            for dst, name in ((ln2, "ln2"), (lnf, "lnf")):
                sp.dma_start(dst[:, :], a[name]).then_inc(gains_in, 16)
            sp.dma_start(subk[:, :, :], a["subk"]).then_inc(gains_in, 16)

            def store_y(t):
                sp.wait_ge(y_done, t + 1)
                dst = out["y_prompt"][P * t:P * t + P, :] if t < SAMPLE else out["y_sample"]
                sp.dma_start(dst, hbuf[:, t % 2, :]).then_inc(y_out, 16)

            for t in range(TILES):
                if t == SAMPLE:
                    sp.wait_ge(state_ok, SAMPLE)
                    sp.dma_start(out["state_p"], state[:, :, :]).then_inc(outs_done, 16)
                    sp.wait_ge(ev_pv, SAMPLE * HEADS)
                    for h in range(HEADS):
                        if h >= 2:
                            sp.wait_ge(ev_su, h - 1)
                        sp.dma_start(st_in[h % 2], a["state"][:, h].rearrange("b d e -> d b e")
                                     ).then_inc(st_landed[h % 2], 16)
                        if h >= 1:
                            sp.wait_ge(ev_su, h)
                            sp.dma_start(out["state_s"][:, h - 1].rearrange("b d e -> d b e"), st_out[(h - 1) % 2]
                                         ).then_inc(st_stored[(h - 1) % 2], 16)
                    sp.wait_ge(ev_su, HEADS)
                    sp.dma_start(out["state_s"][:, HEADS - 1].rearrange("b d e -> d b e"), st_out[(HEADS - 1) % 2]
                                 ).then_inc(st_stored[(HEADS - 1) % 2], 16)
                sp.wait_ge(c_ok, t + 1)
                if t < SAMPLE:
                    sp.dma_start(out["ckv_p"][P * t:P * t + P, :], ckv[:, t, :]).then_inc(outs_done, 16)
                else:
                    sp.dma_start(out["ckv_s"], ckvn_s).then_inc(new_ckv_out, 16)
                sp.wait_ge(kpe_ok, t + 1)
                dst = out["kr_p"][P * t:P * t + P, :] if t < SAMPLE else out["kr_s"]
                sp.dma_start(dst, kpe).then_inc(outs_done, 16)
                if t >= 2:
                    store_y(t - 2)
                    sp.wait_ge(y_out, 16 * (t - 1))
                if t < 2:
                    sp.wait_ge(sq_done, TILES)
                sp.dma_start(hbuf[:, t % 2, :], a["x_all"][P * t:P * t + P, :]).then_inc(xres_in, 16)
                if 1 <= t < SAMPLE:
                    sp.dma_start(pj, proj_d[t + 1]).then_inc(pj_in, 16)
                if t == SAMPLE - 1:
                    sp.wait_ge(ev_s, 2 * SAMPLE)
                    sp.dma_start(dmask[:, :, :], a["d_sample"]).then_inc(dmask_in, 16)
                if t == SAMPLE:
                    sp.wait_ge(new_ckv_out, 16)
                    for b in range(DEC_BATCH + 2):
                        if b < DEC_BATCH:
                            if b >= 2:
                                sp.wait_ge(mm_sc, SAMPLE * HEADS + b - 1)
                            s = keys_in[b % 2]
                            sp.dma_start(ca_t[b % 2], a["cache_t"][b]).then_inc(s, 16)
                            sp.dma_start(ca_r[b % 2], a["cache_rt"][b]).then_inc(s, 16)
                        if b >= 2:
                            c = b - 2
                            if c >= 2:
                                sp.wait_ge(mm_pv, SAMPLE * HEADS + c - 1)
                            s = values_in[c % 2]
                            sp.dma_start(ca[c % 2], a["cache"][c].rearrange("(k p) c -> p k c", p=P)
                                         ).then_inc(s, 16)
                            sp.dma_start(ca_n[c % 2], out["ckv_s"][DEC_SEQ * c:DEC_SEQ * c + DEC_SEQ, :]
                                         ).then_inc(s, 16)
                for i in range(KD + HP):
                    n = t * (KD + HP) + i
                    if n >= WB:
                        sp.wait_ge(wblk_used, n - WB + 1)
                    src = a["w_o"][P * i:P * i + P, :] if i < KD else a["w_q"][i - KD]
                    sp.dma_start(wblk[:, n % WB, :], src).then_inc(wblk_in[n % WB], 16)
                if t == 0:
                    for i in range(4):
                        sp.wait_ge(stored[i], stores[i])
                    sp.dma_start(pj, proj_d[1]).then_inc(pj_in, 16)
            store_y(SAMPLE - 1)
            store_y(SAMPLE)
            sp.wait_ge(y_out, 16 * TILES)
            sp.wait_ge(outs_done, 16 * (1 + SAMPLE + TILES))
            for i in range(2):
                sp.wait_ge(st_stored[i], 16 * HEADS // 2)

        @block.gpsimd
        def _(pool):
            for n, (cb, buf) in enumerate(loads):
                if n >= 2 and buf < 2:
                    pool.wait_ge(mm_in, n - 1 if n < 6 else 6 + SAMPLE * (n - 5))
                pool.dma_start(win[buf][:, :, 0:width[cb]],
                               a["w_in"][:, 512 * cb:512 * cb + width[cb]].rearrange("(k p) n -> p k n", p=P)
                               ).then_inc(win_in[buf], 16)
            pool.wait_ge(mm_in, NIN)
            for i in range(4):
                pool.wait_ge(stored[i], stores[i])
            for t in range(TILES):
                for part in range(PARTS):
                    pool.wait_ge(picks_ok, PARTS * t + part + 1)
                    with pool.Fori(part * ROUNDS // 2 // PARTS, (part + 1) * ROUNDS // 2 // PARTS) as r2:
                        for half in range(2):
                            j = r2 * 2 + (t * ROUNDS + half)
                            pool.wait_ge(rows_free, j * SLOTS + 1)
                            pool.nop(nofuse=True)
                            first = r2 * (2 * SLOTS) + half * SLOTS
                            nc.gpsimd.tensor_copy(cur[:, half, :], eidx[:, t % 2, bass.ds(first, SLOTS)]
                                                  ).then_inc(idx_here, 1)
                            pool.wait_ge(idx_here, j + 1)
                            for s in range(SLOTS):
                                pool.wait_ge(rows_free, j * SLOTS + s + 1)
                                pool.nop(nofuse=True)
                                nc.gpsimd.indirect_dma_start(
                                    rows[:, s, :], None, a["uv"], bass.IndirectOffsetOnAxis(cur[:, half, s:s + 1], 0)
                                ).then_inc(rows_in[s], 16)

        @block.tensor
        def _(pe):
            mm, tr = nc.tensor.matmul, nc.tensor.transpose

            def project_in(n, half):
                cb, t = items[n]
                load = cb if n < 6 or cb >= 3 else 6 + cb
                buf = loads[load][1]
                if t <= 1 and half == 0:
                    pe.wait_ge(win_in[buf], 16 * sum(b == buf for _, b in loads[:load + 1]))
                if half == 0:
                    pe.wait_ge(xt_ok, KD if t == 0 else 2 * KD)
                if n >= 4 and half == 0:
                    pe.wait_ge(ev_in, n - 3)
                for k in range(KD // 2 * half, KD // 2 * half + KD // 2):
                    last = mm(banks[n % 4][:, 0:width[cb]], xt[:, k, P * t:P * t + P],
                              win[buf][:, k, 0:width[cb]], start=(k == 0), stop=(k == KD - 1))
                if half == 1:
                    last.then_inc(mm_in, 1)

            for n in range(6):
                for half in range(2):
                    project_in(n, half)
            pe.wait_ge(consts_in[0], 16 * 5)

            def turn_qk(t):
                pe.wait_ge(qk_ok, t + 1)
                for g in range(4):
                    dst = f4(g, HD)
                    for i in range(4):
                        last = tr(dst[:, i, :], qk[:, HD * (4 * g + i):HD * (4 * g + i + 1)], ident[:, :])
                    last.then_inc(tr_qk, 1)

            def ret_scores(t):
                pe.wait_ge(ev_qk, 4 * (t + 1))
                for g in range(2):
                    for i in range(4):
                        h = 4 * g + i
                        last = mm(f4(g)[:, i, :], k_t[:, h, :], q_t[:, h, :], start=True, stop=True)
                    last.then_inc(mm_s, 1)

            def ret_sums(t):
                v = pj[:, OFF_V:OFF_V + 512]
                for g in range(2):
                    pe.wait_ge(ev_s, 2 * t + g + 1)
                    for i in range(4):
                        h = 4 * g + i
                        last = mm(f8(2)[:, h, :], s_td[g][:, i, :], v[:, HD * h:HD * h + HD], start=True, stop=True)
                last.then_inc(mm_oi, 1)
                pe.wait_ge(kd_ok, t + 1)
                if t < SAMPLE:
                    if t >= 1:
                        pe.wait_ge(state_ok, t)
                        for h in range(HEADS):
                            last = mm(f8(3)[:, h, :], q_t[:, h, :], state[:, h, :], start=True, stop=True)
                        last.then_inc(mm_os, 1)
                    for h in range(HEADS):
                        last = mm(f8(0, HD)[:, h, :], kdec[:, HD * h:HD * h + HD], v[:, HD * h:HD * h + HD],
                                  start=True, stop=True)
                    last.then_inc(mm_up, 1)

            def sample_state(h):
                if h >= 2:
                    pe.wait_ge(ev_ss, h - 1)
                pe.wait_ge(st_landed[h % 2], 16 * (h // 2 + 1))
                mm(F[h % 2][:, :], q_t[:, h, :], st_in[h % 2].rearrange("p b e -> p (b e)"),
                   start=True, stop=True).then_inc(mm_ss, 1)
                if h >= 1:
                    pe.wait_ge(ev_su, h)
                pe.wait_ge(vm_ok, h + 1)
                mm(F[3][0:HD, :], kdec[:, HD * h:HD * h + HD], vmask[h % 2].rearrange("p b e -> p (b e)"),
                   start=True, stop=True).then_inc(mm_su, 1)

            w4 = w_uq[:, :, :].rearrange("p k (h d) -> p k h d", h=HEADS)

            def turn_c(t):
                kv_new = ckv[:, t, :] if t < SAMPLE else ckvn_s
                if t == 0:
                    pe.wait_ge(small_in, 16 * 3)
                pe.wait_ge(c_ok, t + 1)
                pe.wait_ge(kpe_ok, t + 1)
                for k in range(2):
                    tr(f4(2)[:, k, :], cqn[:, P * k:P * k + P], ident[:, :])
                    tr(f4(2)[:, 2 + k, :], kv_new[:, P * k:P * k + P], ident[:, :])
                tr(F[3][0:ROPE, 0:P], kpe, ident[:, :]).then_inc(tr_c, 1)

            def q_rope(t):
                pe.wait_ge(ev_c, t + 1)
                for k in range(2):
                    last = mm(F[0][:, 0:256], cq_t[:, k, :], w4[:, k, :, HD:QD], start=(k == 0), stop=(k == 1))
                last.then_inc(mm_pe, 1)

            def q_nope(t):
                for g in range(2):
                    for i in range(4):
                        for k in range(2):
                            last = mm(f4(1 + g, HD)[:, i, :], w4[:, k, 4 * g + i, 0:HD], cq_t[:, k, :],
                                      start=(k == 0), stop=(k == 1))
                    last.then_inc(mm_qn, 1)

            def q_lat(t, k):
                if k == 0:
                    pe.wait_ge(qpe_ok, t + 1)
                    for g, bank in ((0, 3), (1, 0)):
                        for i in range(4):
                            h = 4 * g + i
                            last = tr(f4(bank, ROPE)[:, i, :], qpe[:, ROPE * h:ROPE * h + ROPE], ident[:, :])
                        last.then_inc(tr_pe, 1)
                    pe.wait_ge(ev_qn, 2 * (t + 1))
                else:
                    pe.wait_ge(ev_pe, 2 * (t + 1))
                for g in range(2):
                    bank = ((1, 2), (3, 0))[k][g]
                    for i in range(4):
                        h = 4 * g + i
                        last = mm(f4(bank)[:, i, :], w_ukt[:, h, P * k:P * k + P], qn_t[:, h, :],
                                  start=True, stop=True)
                    last.then_inc(mm_ql, 1)

            def scores(t, u):
                n = t * HEADS + u
                if u == 0:
                    pe.wait_ge(ev_ql, 4 * (t + 1))
                if u >= 2:
                    pe.wait_ge(exp_ok, n - 1)
                nk = nkeys(t)
                dst = F[u % 2]
                if t < SAMPLE:
                    for k in range(2):
                        mm(dst[:, 0:nk], qlat[:, k, u, :], ckvt[:, k, 0:nk], start=(k == 0), stop=False)
                    last = mm(dst[:, 0:nk], qpe_t[:, u, :], krt[:, 0:nk], start=False, stop=True)
                else:
                    pe.wait_ge(keys_in[u % 2], 32 * (u // 2 + 1))
                    cut = slice(DEC_SEQ * u, DEC_SEQ * u + DEC_SEQ)
                    for k in range(2):
                        mm(dst[:, 0:PAST], qlat_s[:, k, u, :], ca_t[u % 2][:, k, :], start=(k == 0), stop=False)
                    mm(dst[:, 0:PAST], qpe_t[:, u, :], ca_r[u % 2], start=False, stop=True)
                    for k in range(2):
                        mm(dst[:, PAST:nk], qlat_s[:, k, u, :], ckvt_s[:, k, cut], start=(k == 0), stop=False)
                    last = mm(dst[:, PAST:nk], qpe_t[:, u, :], krt_s[:, cut], start=False, stop=True)
                last.then_inc(mm_sc, 1)

            def turn_probs(t, u):
                n = t * HEADS + u
                pe.wait_ge(p_ok, n + 1)
                if u >= 1:
                    pe.wait_ge(ev_pt, n)
                for j, (lo, w) in enumerate(pieces(t)):
                    last = tr(F[2][0:w, P * j:P * j + P], prob[u % 2][:, lo:lo + w], ident[:, :])
                last.then_inc(tr_p, 1)

            def values(t, u):
                n = t * HEADS + u
                pe.wait_ge(ev_pt, n + 1)
                if t == SAMPLE:
                    pe.wait_ge(values_in[u % 2], 32 * (u // 2 + 1))
                if u >= 1:
                    pe.wait_ge(ev_pv, n)
                for k in range(2):
                    for j, (lo, w) in enumerate(pieces(t)):
                        if t < SAMPLE:
                            lhs = ckv[:, j, P * k:P * k + P]
                        else:
                            lhs = ca[u % 2][:, j, P * k:P * k + P] if j < 2 else ca_n[u % 2][:, P * k:P * k + P]
                        last = mm(F[3][:, P * k:P * k + P], lhs, prob_t[u % 2][0:w, P * j:P * j + P],
                                  start=(j == 0), stop=(j == len(pieces(t)) - 1))
                last.then_inc(mm_pv, 1)

            def values_up(t):
                pe.wait_ge(ev_pv, HEADS * (t + 1))
                for h in range(HEADS):
                    for k in range(2):
                        last = mm(f8(0)[:, h, :], olat[:, k, h, :], w_uv[:, k, HD * h:HD * h + HD],
                                  start=(k == 0), stop=(k == 1))
                last.then_inc(mm_mo, 1)

            def turn_mix(t):
                pe.wait_ge(y_ok, t + 1)
                for g in range(2):
                    if g == 1:
                        pe.wait_ge(ev_mo, t + 1)
                    for i in range(4):
                        k = 4 * g + i
                        last = tr(f4(1 + g)[:, i, :], mix[:, P * k:P * k + P], ident[:, :])
                    last.then_inc(tr_mix, 1)

            def w_o(t, i):
                if i == 0:
                    pe.wait_ge(ev_mix, 2 * (t + 1))
                for k in (2 * i, 2 * i + 1):
                    n = t * (KD + HP) + k
                    pe.wait_ge(wblk_in[n % WB], 16 * (n // WB + 1))
                    for half, bank in ((0, 3), (1, 0)):
                        last = mm(F[bank][:, :], mix_t[:, k, :], wblk[:, n % WB, 512 * half:512 * half + 512],
                                  start=(k == 0), stop=(k == KD - 1), skip_group_check=True)
                    last.then_inc(wblk_used, 1)

            def turn_x2(t):
                pe.wait_ge(x2_ok, t + 1)
                for g in range(2):
                    for i in range(4):
                        k = 4 * g + i
                        last = tr(f4(1 + g)[:, i, :], xn2[:, t % 2, P * k:P * k + P], ident[:, :])
                    last.then_inc(tr_x2, 1)

            def query(t, i):
                if i == 0:
                    pe.wait_ge(ev_x2, 2 * (t + 1))
                g = i // 2
                bank = 3 if g % 2 == 0 else 0
                if g >= 2 and i % 2 == 0:
                    pe.wait_ge(ev_pq, 4 * t + g - 1)
                for hp in (2 * i, 2 * i + 1):
                    n = t * (KD + HP) + KD + hp
                    pe.wait_ge(wblk_in[n % WB], 16 * (n // WB + 1))
                    for k in range(KD):
                        last = mm(f4(bank)[:, hp % 4, :], wblk[:, n % WB, P * k:P * k + P], x2_t[:, k, :],
                                  start=(k == 0), stop=(k == KD - 1))
                    last.then_inc(wblk_used, 1)

            def key_scores(t, g):
                if t == 0 and g == 0:
                    pe.wait_ge(gains_in, 16 * 3)
                pe.wait_ge(ev_pq, 4 * t + g + 1)
                if g >= 2:
                    pe.wait_ge(ev_ps, 4 * t + g - 1)
                for i in range(4):
                    hp = 4 * g + i
                    last = mm(f4(1 + g % 2)[:, i, :], pq_t[:, hp, :], subk[:, hp, :], start=True, stop=True)
                last.then_inc(mm_ps, 1)

            def first_sum(t):
                if t >= 1:
                    pe.wait_ge(y_done, t)
                else:
                    pe.wait_ge(ev_in, NIN)
                for c in range(2):
                    mm(acc[:, 512 * c:512 * c + 512], ident[:, :], hbuf[:, t % 2, 512 * c:512 * c + 512],
                       start=True, stop=False, skip_group_check=True)

            def add_pick(j, s):
                pe.wait_ge(diag_ok, j * SLOTS + s + 1)
                for c in range(2):
                    last = mm(acc[:, 512 * c:512 * c + 512], diag[:, s % DR, :],
                              rows[:, s, D_MODEL + 512 * c:D_MODEL + 512 * c + 512],
                              start=False, stop=False, skip_group_check=True)
                last.then_inc(rows_free, 1)

            def unit(number):
                e, n = divmod(number, UNITS)
                if n == 0:
                    first_sum(e)
                for i in range(GROUP):
                    pick = number * GROUP + i
                    add_pick(pick // SLOTS, pick % SLOTS)

            def run_units(t, step):
                if t == 0:
                    for n, half in beside_first(step):
                        project_in(n, half)
                for number in unit_span(t, step):
                    unit(number)

            pe.sem_inc(rows_free, SLOTS)
            for t in range(TILES):
                for number, (step, i, _) in enumerate(steps_of(t)):
                    if step == "turn_qk":
                        turn_qk(t)
                    elif step == "ret_scores":
                        ret_scores(t)
                    elif step == "ret_sums":
                        ret_sums(t)
                    elif step == "state":
                        sample_state(i)
                    elif step == "turn_c":
                        turn_c(t)
                    elif step == "q_rope":
                        q_rope(t)
                    elif step == "q_nope":
                        q_nope(t)
                    elif step == "q_lat":
                        q_lat(t, i)
                    elif step == "attend":
                        if i < HEADS:
                            scores(t, i)
                        if i >= 3:
                            values(t, i - 3)
                        if 2 <= i < HEADS + 2:
                            turn_probs(t, i - 2)
                    elif step == "values_up":
                        values_up(t)
                    elif step == "turn_mix":
                        turn_mix(t)
                    elif step == "w_o":
                        w_o(t, i)
                    elif step == "turn_x2":
                        turn_x2(t)
                    elif step == "query":
                        if i < HEADS:
                            query(t, i)
                        if i >= 2 and i % 2 == 0:
                            key_scores(t, i // 2 - 1)
                    run_units(t, number)
            for number in range(UNITS * SAMPLE - RESERVE, UNITS * SAMPLE):
                unit(number)
            first_sum(SAMPLE)
            with pe.Fori(0, ROUNDS) as r:
                for s in range(SLOTS):
                    add_pick(r + SAMPLE * ROUNDS, s)

        @block.scalar
        def _(act):
            copy = nc.scalar.copy

            def token_roots(first, last):
                act.wait_ge(xs_in[first], 16 * (last - first))
                for t in range(first, last):
                    if t >= 1:
                        act.wait_ge(sq_done, t)
                    nc.scalar.activation(sq_junk, xs[t], ACT.Square, accum_out=ssq1[:, t:t + 1]
                                         ).then_inc(sq_done, 1)
                act.wait_ge(ms1, 1 + (first > 0))
                nc.scalar.activation(rstd1[:, first:last], ssq1[:, first:last], ACT.Sqrt).then_inc(root1, 1)

            token_roots(0, 1)
            act.wait_ge(rstd1_ok, 1)

            def project_in(n):
                cb, t = items[n]
                act.wait_ge(mm_in, n + 1)
                if n >= 10:
                    act.wait_ge(stored[n % 4], 16 * ((n - 6) // 4))
                dst = pj[:, 512 * cb:512 * cb + width[cb]] if t == 0 else stage[:, n % 4, 0:width[cb]]
                nc.scalar.activation(dst, banks[n % 4][:, 0:width[cb]], ACT.Copy, scale=rstd1[:, t:t + 1]
                                     ).then_inc(ev_in, 1)
                if t >= 1:
                    act.wait_ge(ev_in, n + 1)
                    act.dma_start(proj_d[t, :, 512 * cb:512 * cb + width[cb]], dst).then_inc(stored[n % 4], 16)

            for n in range(6):
                project_in(n)
            token_roots(1, TILES)
            act.wait_ge(rstd1_ok, 2)

            def turn_qk(t):
                for g in range(4):
                    act.wait_ge(tr_qk, 4 * t + g + 1)
                    dst = (q_t, q_t, k_t, k_t)[g][:, 4 * (g % 2):4 * (g % 2) + 4, :]
                    copy(dst, f4(g, HD)).then_inc(ev_qk, 1)
                nc.scalar.activation(sgm, pj[:, OFF_G:OFF_G + 512], ACT.Exp, scale=-1.0).then_inc(eg_ok, 1)

            def spread_copy(t, dst, g, src):
                if t < SAMPLE:
                    return copy(dst[:, 4 * g:4 * g + 4, :], src)
                by_seq = dst.rearrange("p b (h s) -> p b h s", h=HEADS)[:, :, 4 * g:4 * g + 4, :]
                return copy(by_seq, src.rearrange("p h (b s) -> p b h s", b=DEC_BATCH))

            def turn_c(t):
                act.wait_ge(tr_c, t + 1)
                copy(cq_t, f4(2)[:, 0:2, :])
                kt, rt = (ckvt[:, :, P * t:P * t + P], krt[:, P * t:P * t + P]) if t < SAMPLE else (ckvt_s, krt_s)
                copy(kt, f4(2)[:, 2:4, :])
                copy(rt, F[3][0:ROPE, 0:P]).then_inc(ev_c, 1)

            def q_nope(t):
                for g in range(2):
                    act.wait_ge(mm_qn, 2 * t + g + 1)
                    copy(qn_t[:, 4 * g:4 * g + 4, :], f4(1 + g, HD)).then_inc(ev_qn, 1)

            def q_lat(t, k):
                if k == 0:
                    for g, bank in ((0, 3), (1, 0)):
                        act.wait_ge(tr_pe, 2 * t + g + 1)
                        spread_copy(t, qpe_t, g, f4(bank, ROPE)).then_inc(ev_pe, 1)
                for g in range(2):
                    bank = ((1, 2), (3, 0))[k][g]
                    act.wait_ge(mm_ql, 4 * t + 2 * k + g + 1)
                    spread_copy(t, qlat[:, k, :, :], g, f4(bank)).then_inc(ev_ql, 1)

            def exps(t, u):
                n = t * HEADS + u
                nk = nkeys(t)
                act.wait_ge(nm_ok, n + 1)
                if u >= 2:
                    act.wait_ge(tr_p, n - 1)
                nc.scalar.activation(prob[u % 2][:, 0:nk], F[u % 2][:, 0:nk], ACT.Exp, scale=SCALE,
                                     bias=stat[:, 24 + u % 2:25 + u % 2],
                                     accum_out=stat[:, 26 + u % 2:27 + u % 2]).then_inc(exp_ok, 1)

            def copy_probs(t, u):
                n = t * HEADS + u
                act.wait_ge(tr_p, n + 1)
                if u >= 2:
                    act.wait_ge(mm_pv, n - 1)
                full = [q for q in pieces(t) if q[1] == P]
                last = copy(prob_t[u % 2][:, 0:P * len(full)], F[2][:, 0:P * len(full)])
                if t == SAMPLE:
                    last = copy(prob_t[u % 2][0:DEC_SEQ, PAST:PAST + P], F[2][0:DEC_SEQ, PAST:PAST + P])
                last.then_inc(ev_pt, 1)

            def copy_values(t, u):
                act.wait_ge(mm_pv, t * HEADS + u + 1)
                src = F[3][:, 0:256].rearrange("p (k n) -> p k n", k=2)
                if t < SAMPLE:
                    copy(olat[:, :, u, :], src).then_inc(ev_pv, 1)
                else:
                    for k in range(2):
                        last = copy(olat[:, k, :, DEC_SEQ * u:DEC_SEQ * u + DEC_SEQ],
                                    src[:, k, :].rearrange("p (h s) -> p h s", h=HEADS))
                    last.then_inc(ev_pv, 1)

            def values_up(t):
                act.wait_ge(mm_mo, t + 1)
                copy(mix[:, 512:1024], F[0][:, :]).then_inc(ev_mo, 1)

            def turn_mix(t):
                for g in range(2):
                    act.wait_ge(tr_mix, 2 * t + g + 1)
                    copy(mix_t[:, 4 * g:4 * g + 4, :], f4(1 + g)).then_inc(ev_mix, 1)

            def turn_x2(t):
                for g in range(2):
                    act.wait_ge(tr_x2, 2 * t + g + 1)
                    copy(x2_t[:, 4 * g:4 * g + 4, :], f4(1 + g)).then_inc(ev_x2, 1)

            def copy_queries(t, g):
                act.wait_ge(wblk_used, t * (KD + HP) + KD + 4 * g + 4)
                copy(pq_t[:, 4 * g:4 * g + 4, :], f4(3 if g % 2 == 0 else 0)).then_inc(ev_pq, 1)

            def copy_key_scores(t, g):
                act.wait_ge(mm_ps, 4 * t + g + 1)
                copy(sc[:, 4 * g:4 * g + 4, :], f4(1 + g % 2)).then_inc(ev_ps, 1)

            def exp_gates(t, part):
                act.wait_ge(bd_ok, PARTS * t + part + 1)
                nc.scalar.activation(sm[1], sm[0], ACT.Exp).then_inc(be_ok, 1)

            def weights(t, part, j, g, gate_at):
                act.wait_ge(dot_ok, j * GROUPS + g + 1)
                cols = slice(GROUP * g, GROUP * g + GROUP)
                nc.scalar.activation(gel[:, cols], dots[:, cols], ACT.Gelu).then_inc(gel_ok, 1)
                act.wait_ge(gel_ok, j * GROUPS + g + 1)
                act.wait_ge(picks_ok, PARTS * t + part + 1)
                for i in range(GROUP):
                    s = GROUP * g + i
                    nc.scalar.activation(wgt[:, s:s + 1], gel[:, s:s + 1], ACT.Copy, scale=gate_at(s)
                                         ).then_inc(wgt_ok, 1)
                for i in range(GROUP):
                    s = GROUP * g + i
                    act.wait_ge(wgt_ok, j * SLOTS + s + 1)
                    act.wait_ge(rows_free, j * SLOTS + s + 1 + SLOTS - DR)
                    nc.scalar.activation(diag[:, s % DR, :], ident[:, :], ACT.Copy, scale=wgt[:, s:s + 1]
                                         ).then_inc(diag_ok, 1)

            def finish(t):
                act.wait_ge(rows_free, SLOTS + PICKS * (t + 1))
                act.wait_ge(dot_ok, GROUPS * ROUNDS * (t + 1))
                nc.scalar.activation(xps[:, :], acc[:, :], ACT.Square, accum_out=stat[:, 36:37]).then_inc(sq_f, 1)
                act.wait_ge(ms_f, t + 1)
                nc.scalar.activation(stat[:, 38:39], stat[:, 37:38], ACT.Sqrt).then_inc(root_f, 1)

            def unit(number):
                e, n = divmod(number, UNITS)
                r, g = divmod(n, GROUPS)
                weights(e, r * PARTS // ROUNDS, e * ROUNDS + r, g,
                        lambda s: gate[:, e % 2, r * SLOTS + s:r * SLOTS + s + 1])
                if n == UNITS - 1:
                    finish(e)

            def run_units(t, step):
                if t == 0:
                    for n, half in beside_first(step):
                        if half == 1:
                            project_in(n)
                for number in unit_span(t, step):
                    unit(number)

            for t in range(TILES):
                for number, (step, i, _) in enumerate(steps_of(t)):
                    units_first = step == "attend" and i % 2 == 1
                    if units_first:
                        run_units(t, number)
                    if step == "turn_qk":
                        turn_qk(t)
                    elif step == "silu":
                        act.wait_ge(ms_gn, t + 1)
                        nc.scalar.activation(stat[:, 8:16], stat[:, 0:8], ACT.Sqrt).then_inc(root_gn, 1)
                    elif step == "latents":
                        act.wait_ge(ms_c, t + 1)
                        nc.scalar.activation(stat[:, 18:20], stat[:, 16:18], ACT.Sqrt).then_inc(root_c, 1)
                    elif step == "turn_c":
                        turn_c(t)
                    elif step == "q_nope":
                        q_nope(t)
                    elif step == "q_lat":
                        q_lat(t, i)
                    elif step == "attend":
                        if 1 <= i <= HEADS:
                            exps(t, i - 1)
                        if i >= 3:
                            copy_values(t, i - 3)
                        if 2 <= i < HEADS + 2:
                            copy_probs(t, i - 2)
                    elif step == "values_up":
                        values_up(t)
                    elif step == "turn_mix":
                        turn_mix(t)
                    elif step == "norm2":
                        act.wait_ge(ms_2, t + 1)
                        nc.scalar.activation(stat[:, 31:32], stat[:, 30:31], ACT.Sqrt).then_inc(root_2, 1)
                    elif step == "turn_x2":
                        turn_x2(t)
                    elif step == "query":
                        if i % 2 == 1 and i < HEADS:
                            copy_queries(t, i // 2)
                        if i >= 2 and i % 2 == 0:
                            copy_key_scores(t, i // 2 - 1)
                        if i == 8:
                            exp_gates(t, 0)
                    elif step == "picks":
                        exp_gates(t, i)
                    if not units_first:
                        run_units(t, number)
            for number in range(UNITS * SAMPLE - RESERVE, UNITS * SAMPLE):
                unit(number)
            with act.Fori(0, ROUNDS) as r:
                for g in range(GROUPS):
                    weights(SAMPLE, PARTS - 1, r + SAMPLE * ROUNDS, g,
                            lambda s: gate[:, SAMPLE % 2, bass.ds(r * SLOTS + s, 1)])
            finish(SAMPLE)

        @block.vector
        def _(dve):
            v = nc.vector
            steps = [0]

            def link(ins):
                steps[0] += 1
                ins.then_inc(dve_step, 1)
                dve.wait_ge(dve_step, steps[0])

            def row(ap, n):
                return ap.unsqueeze(2).to_broadcast([ap.shape[0], ap.shape[1], n])

            def mid(ap, n):
                return ap.unsqueeze(1).to_broadcast([ap.shape[0], n, ap.shape[1]])

            def rotate(dst, src, tmp, cos, sin, heads, half):
                s = src.rearrange("p (h c d) -> p h c d", h=heads, c=2)
                d = dst.rearrange("p (h c d) -> p h c d", h=heads, c=2)
                m = tmp.rearrange("p (h c d) -> p h c d", h=heads, c=2)
                c, sn = mid(cos, heads), mid(sin, heads)
                v.tensor_tensor(d[:, :, 0, :], s[:, :, 0, :], c, ALU.mult)
                v.tensor_tensor(m[:, :, 0, :], s[:, :, 1, :], sn, ALU.mult)
                v.tensor_tensor(d[:, :, 1, :], s[:, :, 1, :], c, ALU.mult)
                link(v.tensor_tensor(m[:, :, 1, :], s[:, :, 0, :], sn, ALU.mult))
                v.tensor_tensor(d[:, :, 0, :], d[:, :, 0, :], m[:, :, 0, :], ALU.subtract)
                return v.tensor_tensor(d[:, :, 1, :], d[:, :, 1, :], m[:, :, 1, :], ALU.add)

            def scale_xt(first, last):
                dve.wait_ge(xt_in[first], 16 if first else 32)
                for k in range(KD):
                    v.tensor_scalar(xt[:, k, P * first:P * last], xt[:, k, P * first:P * last], ln1[:, k:k + 1], None,
                                    ALU.mult).then_inc(xt_ok, 1)

            def token_roots(first, last):
                dve.wait_ge(sq_done, last)
                v.tensor_scalar(ssq1[:, first:last], ssq1[:, first:last], 1.0 / D_MODEL, EPS, ALU.mult, ALU.add
                                ).then_inc(ms1, 1)
                dve.wait_ge(root1, 1 + first)
                v.reciprocal(rstd1[:, first:last], rstd1[:, first:last]).then_inc(rstd1_ok, 1)

            scale_xt(0, 1)
            token_roots(0, 1)
            scale_xt(1, TILES)
            dve.wait_ge(consts_in[0], 16 * 5)
            o3 = three(ret_o, HEADS)

            def rotate_qk(t):
                if t == 0:
                    dve.wait_ge(ev_in, 6)
                else:
                    dve.wait_ge(picks_ok, PARTS * t)
                    dve.wait_ge(pj_in, 16 * t)
                rotate(qk, pj[:, 0:1024], rtmp, cos64[:, t, :], sin64[:, t, :], 2 * HEADS, HD // 2
                       ).then_inc(qk_ok, 1)
                dve.wait_ge(qk_ok, t + 1)
                kd = k_sample if t == SAMPLE else k_prompt
                v.tensor_tensor(three(kdec, HEADS), three(qk[:, 512:1024], HEADS), row(kd[:, :], HD), ALU.mult
                                ).then_inc(kd_ok, 1)

            def ret_scores(t):
                if t == SAMPLE:
                    dve.wait_ge(dmask_in, 16)
                for g in range(2):
                    dve.wait_ge(mm_s, 2 * t + g + 1)
                    v.tensor_tensor(s_td[g], f4(g), dmask[:, 4 * g:4 * g + 4, :], ALU.mult).then_inc(ev_s, 1)

            def sample_state(h):
                vv = three(pj[:, OFF_V:OFF_V + 512], HEADS)
                if h >= 2:
                    dve.wait_ge(mm_su, h - 1)
                v.tensor_tensor(vmask[h % 2], mid(vv[:, h, :], DEC_BATCH), row(own[:, :], HD), ALU.mult
                                ).then_inc(vm_ok, 1)
                dve.wait_ge(mm_ss, h + 1)
                v.tensor_tensor(ost[0], f8(h % 2), row(q_sample[:, h, :], HD), ALU.mult).then_inc(ev_ss, 1)
                dve.wait_ge(ev_ss, h + 1)
                link(v.tensor_reduce(o3[:, h, :], ost[0].rearrange("p b e -> p e b"), AX_X, ALU.add))
                dve.wait_ge(mm_su, h + 1)
                if h >= 2:
                    dve.wait_ge(st_stored[h % 2], 16 * (h // 2))
                v.scalar_tensor_tensor(st_out[h % 2].rearrange("p b e -> p (b e)"),
                                       st_in[h % 2].rearrange("p b e -> p (b e)"), g_sample[h],
                                       F[3][0:HD, :], ALU.mult, ALU.add).then_inc(ev_su, 1)

            def ret_norm(t):
                dve.wait_ge(mm_oi, t + 1)
                if t == SAMPLE:
                    link(v.tensor_tensor(ret_o, ret_o, F[2][:, :], ALU.add))
                else:
                    if t == 0:
                        link(v.tensor_copy(ret_o, F[2][:, :]))
                    else:
                        dve.wait_ge(mm_os, t)
                        link(v.tensor_tensor(o3, f8(3), row(q_prompt[:, :], HD), ALU.mult))
                        link(v.tensor_tensor(ret_o, ret_o, F[2][:, :], ALU.add))
                    dve.wait_ge(mm_up, t + 1)
                    if t == 0:
                        v.tensor_copy(state[:, :, :], f8(0, HD)).then_inc(state_ok, 1)
                    else:
                        link(v.tensor_tensor(state[:, :, :], state[:, :, :], row(s_decay[:, :], HD), ALU.mult))
                        v.tensor_tensor(state[:, :, :], state[:, :, :], f8(0, HD), ALU.add).then_inc(state_ok, 1)
                mean, var = stat[:, 40:48], stat[:, 0:8]
                link(v.tensor_reduce(mean, o3, AX_X, ALU.add))
                link(v.tensor_scalar(mean, mean, 1.0 / HD, None, ALU.mult))
                link(v.tensor_tensor(o3, o3, row(mean, HD), ALU.subtract))
                link(v.tensor_tensor(osq, ret_o, ret_o, ALU.mult))
                link(v.tensor_reduce(var, three(osq, HEADS), AX_X, ALU.add))
                v.tensor_scalar(var, var, 1.0 / HD, EPS, ALU.mult, ALU.add).then_inc(ms_gn, 1)

            def silu(t):
                if t == 0:
                    dve.wait_ge(consts_in[1], 16 * 11)
                dve.wait_ge(eg_ok, t + 1)
                link(v.tensor_scalar(sgm, sgm, 1.0, None, ALU.add))
                link(v.reciprocal(sgm, sgm))
                link(v.tensor_tensor(sgm, sgm, pj[:, OFF_G:OFF_G + 512], ALU.mult))
                link(v.tensor_tensor(sgm, sgm, gnw[:, :], ALU.mult))
                dve.wait_ge(root_gn, t + 1)
                link(v.reciprocal(stat[:, 8:16], stat[:, 8:16]))
                link(v.tensor_tensor(o3, o3, row(stat[:, 8:16], HD), ALU.mult))
                v.tensor_tensor(mix[:, 0:512], ret_o, sgm, ALU.mult).then_inc(y_ok, 1)

            def stats(t):
                dve.wait_ge(y_ok, t + 1)
                kv = ckvn_s if t == SAMPLE else ckv[:, t, :]
                v.tensor_tensor_reduce(cqn, pj[:, OFF_CQ:OFF_CQ + RANK], pj[:, OFF_CQ:OFF_CQ + RANK], 1.0, 0.0,
                                       ALU.mult, ALU.add, stat[:, 16:17])
                link(v.tensor_tensor_reduce(kv, pj[:, OFF_CKV:OFF_CKV + RANK], pj[:, OFF_CKV:OFF_CKV + RANK],
                                            1.0, 0.0, ALU.mult, ALU.add, stat[:, 17:18]))
                v.tensor_scalar(stat[:, 16:18], stat[:, 16:18], 1.0 / RANK, EPS, ALU.mult, ALU.add
                                ).then_inc(ms_c, 1)

            def latents(t):
                kv = ckvn_s if t == SAMPLE else ckv[:, t, :]
                dve.wait_ge(root_c, t + 1)
                link(v.reciprocal(stat[:, 18:20], stat[:, 18:20]))
                v.scalar_tensor_tensor(cqn, pj[:, OFF_CQ:OFF_CQ + RANK], stat[:, 18:19], qnw[:, :],
                                       ALU.mult, ALU.mult)
                v.scalar_tensor_tensor(kv, pj[:, OFF_CKV:OFF_CKV + RANK], stat[:, 19:20], kvw[:, :],
                                       ALU.mult, ALU.mult).then_inc(c_ok, 1)
                rotate(kpe, pj[:, OFF_KPE:OFF_KPE + ROPE], ktmp, cos32[:, t, :], sin32[:, t, :], 1, ROPE // 2
                       ).then_inc(kpe_ok, 1)

            def maxima(t, u):
                n = t * HEADS + u
                nk = nkeys(t)
                dve.wait_ge(mm_sc, n + 1)
                if t < SAMPLE:
                    link(v.memset(F[u % 2][0:CHUNK, nk - CHUNK:nk], MASKED))
                link(v.tensor_reduce(stat[:, 20 + u % 2:21 + u % 2], F[u % 2][:, 0:nk], AX_X, ALU.max))
                if u >= 2:
                    dve.wait_ge(exp_ok, n - 1)
                v.tensor_scalar(stat[:, 24 + u % 2:25 + u % 2], stat[:, 20 + u % 2:21 + u % 2], -SCALE, None,
                                ALU.mult).then_inc(nm_ok, 1)

            def normalise(t, u):
                n = t * HEADS + u
                nk = nkeys(t)
                dve.wait_ge(exp_ok, n + 1)
                link(v.reciprocal(stat[:, 28 + u % 2:29 + u % 2], stat[:, 26 + u % 2:27 + u % 2]))
                v.tensor_scalar(prob[u % 2][:, 0:nk], prob[u % 2][:, 0:nk], stat[:, 28 + u % 2:29 + u % 2], None,
                                ALU.mult).then_inc(p_ok, 1)

            def residual(t):
                h = hbuf[:, t % 2, :]
                dve.wait_ge(wblk_used, t * (KD + HP) + KD)
                dve.wait_ge(xres_in, 16 * (t + 1))
                v.tensor_tensor(h[:, 0:512], h[:, 0:512], F[3][:, :], ALU.add)
                link(v.tensor_tensor(h[:, 512:1024], h[:, 512:1024], F[0][:, :], ALU.add))
                link(v.tensor_tensor_reduce(xn2[:, t % 2, :], h, h, 1.0, 0.0, ALU.mult, ALU.add, stat[:, 30:31]))
                v.tensor_scalar(stat[:, 30:31], stat[:, 30:31], 1.0 / D_MODEL, EPS, ALU.mult, ALU.add
                                ).then_inc(ms_2, 1)

            def norm2(t):
                if t == 0:
                    dve.wait_ge(gains_in, 16 * 3)
                dve.wait_ge(root_2, t + 1)
                link(v.reciprocal(stat[:, 31:32], stat[:, 31:32]))
                v.scalar_tensor_tensor(xn2[:, t % 2, :], hbuf[:, t % 2, :], stat[:, 31:32], ln2[:, :],
                                       ALU.mult, ALU.mult).then_inc(x2_ok, 1)

            def top16(span, values_of, vals, idx):
                for i in span:
                    last = v.max(vals[:, i, 0:8], values_of(i))
                link(last)
                for i in span:
                    v.max_index(idx[:, i, 0:8], vals[:, i, 0:8], values_of(i))
                for i in span:
                    last = v.match_replace(values_of(i), vals[:, i, 0:8], values_of(i), LOWEST)
                link(last)
                for i in span:
                    last = v.max(vals[:, i, 8:16], values_of(i))
                link(last)
                for i in span:
                    last = v.max_index(idx[:, i, 8:16], vals[:, i, 8:16], values_of(i))
                link(last)

            tv4 = tv.rearrange("p (h c) k -> p h c k", c=2)
            ti4 = ti.rearrange("p (h c) k -> p h c k", c=2)
            tif4 = tif.rearrange("p (h c) k -> p h c k", c=2)
            hot3 = hot.rearrange("p h k i -> p (h k) i")
            wide = [P, PART, TOPK, TOPK]

            def pairs(part):
                heads = slice(PART * part, PART * part + PART)
                v.tensor_copy(tif4[:, heads], ti4[:, heads])
                link(v.tensor_tensor(cand, tv4[:, heads, 0, :].unsqueeze(3).to_broadcast(wide),
                                     tv4[:, heads, 1, :].unsqueeze(2).to_broadcast(wide), ALU.add))

            def places(t, part):
                heads = slice(PART * part, PART * part + PART)
                v.tensor_tensor(three(sm[0], PART), bv[:, heads], bv[:, heads, 0:1].to_broadcast([P, PART, TOPK]),
                                ALU.subtract).then_inc(bd_ok, 1)
                place = bj[:, heads].rearrange("p h k -> p (h k)")
                v.tensor_scalar(sm[2].bitcast(U32), place, 4, None, ALU.logical_shift_right)
                link(v.tensor_scalar(sm[3].bitcast(U32), place, TOPK - 1, None, ALU.bitwise_and))
                v.tensor_copy(sm[4], sm[2].bitcast(U32))
                link(v.tensor_copy(sm[5], sm[3].bitcast(U32)))

            def look_up(part, c):
                heads = slice(PART * part, PART * part + PART)
                link(v.tensor_tensor(hot3, row(sm[4 + c], TOPK), mid(count16[:, :], PART_PICKS), ALU.is_equal))
                link(v.tensor_tensor(hot, hot, tif4[:, heads, c, :].unsqueeze(2).to_broadcast(wide), ALU.mult))
                link(v.tensor_reduce(sm[6 + c], hot3, AX_X, ALU.add))

            def gates(t, part):
                cols = slice(PART_PICKS * part, PART_PICKS * part + PART_PICKS)
                v.scalar_tensor_tensor(eidx[:, t % 2, cols], sm[6], float(KEYS), sm[7], ALU.mult, ALU.add)
                dve.wait_ge(be_ok, PARTS * t + part + 1)
                link(v.tensor_reduce(stat[:, 48:48 + PART], three(sm[1], PART), AX_X, ALU.add))
                link(v.reciprocal(stat[:, 48:48 + PART], stat[:, 48:48 + PART]))
                v.tensor_tensor(three(gate[:, t % 2, cols], PART), three(sm[1], PART), row(stat[:, 48:48 + PART], TOPK),
                                ALU.mult).then_inc(picks_ok, 1)

            def key_top16(t, g):
                dve.wait_ge(ev_ps, 4 * t + g + 1)
                top16(range(4 * g, 4 * g + 4), lambda i: sc[:, i, :], tv, ti)

            def best(i):
                top16(range(2 * i, 2 * i + 2), lambda i: candf[:, i % PART, :], bv, bj)

            def first_dot(t):
                if t >= 1:
                    dve.wait_ge(sq_f, t)
                else:
                    dve.wait_ge(ev_in, NIN)
                v.tensor_copy(xps[:, :], xn2[:, t % 2, :]).then_inc(xps_ok, 1)
                dve.wait_ge(xps_ok, t + 1)

            def dot(j, s):
                dve.wait_ge(rows_in[s], j * 16 + 16)
                last = v.tensor_tensor_reduce(rows[:, s, 0:D_MODEL], rows[:, s, 0:D_MODEL], xps[:, :],
                                              1.0, 0.0, ALU.mult, ALU.add, dots[:, s:s + 1])
                if s % GROUP == GROUP - 1:
                    last.then_inc(dot_ok, 1)

            def finish(t):
                dve.wait_ge(sq_f, t + 1)
                v.tensor_scalar(stat[:, 37:38], stat[:, 36:37], 1.0 / D_MODEL, EPS, ALU.mult, ALU.add
                                ).then_inc(ms_f, 1)
                dve.wait_ge(root_f, t + 1)
                link(v.reciprocal(stat[:, 39:40], stat[:, 38:39]))
                v.scalar_tensor_tensor(hbuf[:, t % 2, :], acc[:, :], stat[:, 39:40], lnf[:, :],
                                       ALU.mult, ALU.mult).then_inc(y_done, 1)

            def unit(number):
                e, n = divmod(number, UNITS)
                if n == 0:
                    if e >= 1:
                        finish(e - 1)
                    first_dot(e)
                for i in range(GROUP):
                    pick = number * GROUP + i
                    dot(pick // SLOTS, pick % SLOTS)

            def run_units(t, step):
                if len(unit_span(t, step)):
                    span = unit_span(t, step)
                    lead = DVE_LEAD if span.start > 0 else 0
                    for number in range(span.start + lead, span.stop + DVE_LEAD):
                        unit(number)

            for t in range(TILES):
                for number, (step, i, _) in enumerate(steps_of(t)):
                    if step == "rotate":
                        rotate_qk(t)
                        if t == 0:
                            token_roots(1, TILES)
                    elif step == "ret_scores":
                        ret_scores(t)
                    elif step == "state":
                        sample_state(i)
                    elif step == "ret_norm":
                        ret_norm(t)
                    elif step == "silu":
                        silu(t)
                    elif step == "stats":
                        stats(t)
                    elif step == "latents":
                        latents(t)
                    elif step == "q_rope":
                        dve.wait_ge(mm_pe, t + 1)
                        rotate(qpe, F[0][:, 0:256], ptmp, cos32[:, t, :], sin32[:, t, :], HEADS, ROPE // 2
                               ).then_inc(qpe_ok, 1)
                    elif step == "attend":
                        if 2 <= i < HEADS + 2:
                            normalise(t, i - 2)
                        if 1 <= i <= HEADS:
                            maxima(t, i - 1)
                    elif step == "residual":
                        residual(t)
                    elif step == "norm2":
                        norm2(t)
                    elif step == "query":
                        if i == 3 or i == 5:
                            key_top16(t, (i - 3) // 2)
                        elif i == 6:
                            pairs(0)
                            best(0)
                        elif i == 7:
                            best(1)
                            places(t, 0)
                        elif i == 8:
                            for c in range(2):
                                look_up(0, c)
                            gates(t, 0)
                    elif step == "keys":
                        key_top16(t, i)
                    elif step == "pairs":
                        pairs(i)
                    elif step == "best":
                        best(i)
                    elif step == "places":
                        places(t, i)
                    elif step == "picks":
                        for c in range(2):
                            look_up(i, c)
                    elif step == "gates":
                        gates(t, i)
                    run_units(t, number)
            for number in range(UNITS * SAMPLE - RESERVE + DVE_LEAD, UNITS * SAMPLE):
                unit(number)
            finish(SAMPLE - 1)
            first_dot(SAMPLE)
            with dve.Fori(0, ROUNDS) as r:
                for s in range(SLOTS):
                    dot(r + SAMPLE * ROUNDS, s)
            finish(SAMPLE)


def kernel(**inputs):
    import concourse.bacc as _bacc
    from concourse.bass_utils import run_bass_kernel_spmd as _run

    x = {k: np.asarray(v) for k, v in inputs.items()}
    con = np.ascontiguousarray
    arrays = dict(tables())

    def spread(w):
        return con(np.broadcast_to(w.reshape(1, -1), (P, w.size)))

    x_all = np.concatenate([x["x_prompt"][0], x["x_sample"].reshape(P, D_MODEL)], axis=0)
    cache = x["cache_mla_ckv"][0]
    arrays.update(
        x_all=x_all,
        x_t=con(x_all.T.reshape(KD, P, TILES * P).transpose(1, 0, 2)),
        ln1=con(x["ln1_w"][0].reshape(KD, P).T),
        w_in=con(x["w_in"][0]),
        gn=spread(x["ret_gn_w"][0]), qn=spread(x["mla_q_norm_w"][0]), kvn=spread(x["mla_kv_norm_w"][0]),
        ln2=spread(x["ln2_w"][0]), lnf=spread(x["lnf_w"]),
        w_uq=con(x["mla_w_uq"][0].reshape(RANK, HEADS * QD)),
        w_ukt=con(x["mla_w_uk"][0].transpose(2, 1, 0)),
        w_uv=con(x["mla_w_uv"][0].reshape(RANK, HEADS * HD)),
        w_o=con(x["w_o"][0]),
        w_q=con(x["peer_w_q"][0].reshape(KD, P, HP, P).transpose(2, 1, 0, 3).reshape(HP, P, D_MODEL)),
        subk=con(x["peer_sub_keys"][0].reshape(HP, KEYS, P).transpose(2, 0, 1)),
        uv=np.concatenate([x["peer_u"][0], x["peer_v"][0]], axis=1),
        cache=con(cache),
        cache_t=con(cache.transpose(0, 2, 1).reshape(DEC_BATCH, 2, P, PAST).transpose(0, 2, 1, 3)),
        cache_rt=con(x["cache_mla_krope"][0].transpose(0, 2, 1)),
        state=con(x["state_retention"][0]),
    )
    outputs = dict(y_prompt=(SEQ, D_MODEL), y_sample=(P, D_MODEL), ckv_p=(SEQ, RANK), kr_p=(SEQ, ROPE),
                   state_p=(HD, HEADS, HD), ckv_s=(P, RANK), kr_s=(P, ROPE),
                   state_s=(DEC_BATCH, HEADS, HD, HD))

    nc = _bacc.Bacc("TRN2", target_bir_lowering=False, num_devices=1)
    ins = {k: nc.dram_tensor(f"in_{k}", v.shape, F32, kind="ExternalInput").ap() for k, v in arrays.items()}
    outs = {k: nc.dram_tensor(f"out_{k}", s, F32, kind="ExternalOutput").ap() for k, s in outputs.items()}
    build(nc, ins, outs)
    got = _run(nc, [{f"in_{k}": v for k, v in arrays.items()}], core_ids=[0]).results[0]
    g = {k: got[f"out_{k}"] for k in outputs}
    return (g["y_prompt"].reshape(1, SEQ, D_MODEL),
            g["y_sample"].reshape(DEC_BATCH, DEC_SEQ, D_MODEL),
            g["ckv_p"].reshape(1, 1, SEQ, RANK),
            g["kr_p"].reshape(1, 1, SEQ, ROPE),
            con(g["state_p"].transpose(1, 0, 2)).reshape(1, 1, HEADS, HD, HD),
            g["ckv_s"].reshape(1, DEC_BATCH, DEC_SEQ, RANK),
            g["kr_s"].reshape(1, DEC_BATCH, DEC_SEQ, ROPE),
            g["state_s"].reshape(1, DEC_BATCH, HEADS, HD, HD))
```
